# Optimizing a Trainium2 kernel written in Bass

```python
import jax, jax.numpy as jnp
from jax import lax
import numpy as np
import math
import jax
import jax.numpy as jnp

D_MODEL = 1024
BATCH = 1
SEQ = 256
DEPTH = 1

D_MIX = D_MODEL
D_CONF = D_MIX // 4
D_ATT = D_MIX // 4
D_SC = D_MIX // 4
D_POOL = D_MIX - D_CONF - D_ATT - D_SC
HEAD_DIM = 64
N_ATT_HEADS = D_ATT // HEAD_DIM
CONF_KERNEL = 31
SC_KERNEL = 3
POOL_WINDOWS = (2, 4, 8, 16)
N_POOL_GROUPS = len(POOL_WINDOWS)
POOL_GROUP_DIM = D_POOL // N_POOL_GROUPS
D_FF = 4 * D_MODEL
D_PLE = 256
Q_BLOCK = 128
EPS = 1e-6
SPLITS = (2 * D_CONF, D_ATT, D_ATT, D_ATT, N_ATT_HEADS, D_SC, D_SC, D_SC, D_POOL)
D_IN = sum(SPLITS)
SPLIT_IDX = tuple(int(s) for s in np.cumsum(SPLITS)[:-1])


def rms_norm(x, g):
    x32 = x.astype(jnp.float32)
    y = x32 * lax.rsqrt(jnp.mean(x32 * x32, axis=-1, keepdims=True) + EPS)
    return (y * g.astype(jnp.float32)).astype(x.dtype)

def layer_norm(x, g, b):
    x32 = x.astype(jnp.float32)
    mu = jnp.mean(x32, axis=-1, keepdims=True)
    xc = x32 - mu
    y = xc * lax.rsqrt(jnp.mean(xc * xc, axis=-1, keepdims=True) + EPS)
    return (y * g.astype(jnp.float32) + b.astype(jnp.float32)).astype(x.dtype)

def causal_depthwise_conv(u, w):
    k = w.shape[0]
    return lax.conv_general_dilated(
        u, w[:, None, :].astype(u.dtype), window_strides=(1,), padding=((k - 1, 0),),
        dimension_numbers=("NWC", "WIO", "NWC"), feature_group_count=u.shape[-1])

def conformer_conv(ab, w_dw, ln_g, ln_b, w_pw):
    a, b = jnp.split(ab, 2, axis=-1)
    u = a * jax.nn.sigmoid(b)
    u = causal_depthwise_conv(u, w_dw)
    u = jax.nn.silu(layer_norm(u, ln_g, ln_b))
    return u @ w_pw

def forgetting_attention(q, k, v, f_logit):
    b, s, _ = q.shape
    q = q.reshape(b, s, N_ATT_HEADS, HEAD_DIM).transpose(0, 2, 1, 3)
    k = k.reshape(b, s, N_ATT_HEADS, HEAD_DIM).transpose(0, 2, 1, 3)
    v = v.reshape(b, s, N_ATT_HEADS, HEAD_DIM).transpose(0, 2, 1, 3)
    log_f = jax.nn.log_sigmoid(f_logit.astype(jnp.float32))
    c = jnp.cumsum(log_f, axis=1).transpose(0, 2, 1)
    nb = s // Q_BLOCK
    qb = q.reshape(b, N_ATT_HEADS, nb, Q_BLOCK, HEAD_DIM).transpose(2, 0, 1, 3, 4)
    cb = c.reshape(b, N_ATT_HEADS, nb, Q_BLOCK).transpose(2, 0, 1, 3)
    pos = jnp.arange(s, dtype=jnp.int32)
    posb = pos.reshape(nb, Q_BLOCK)
    k32 = k.astype(jnp.float32)
    scale = HEAD_DIM ** -0.5

    def block(args):
        qi, ci, pi = args
        logits = jnp.einsum("bhqd,bhkd->bhqk", qi.astype(jnp.float32), k32) * scale
        logits = logits + ci[..., None] - c[:, :, None, :]
        mask = pi[:, None] >= pos[None, :]
        logits = jnp.where(mask, logits, -jnp.inf)
        probs = jax.nn.softmax(logits, axis=-1)
        return jnp.einsum("bhqk,bhkd->bhqd", probs.astype(v.dtype), v)

    o = lax.map(block, (qb, cb, posb))
    return o.transpose(1, 0, 3, 2, 4).reshape(b, s, D_ATT)

def short_conv_mixer(h, bg, cg, w_sc):
    return bg * causal_depthwise_conv(cg * h, w_sc)

def multiscale_pool(v, w_pool, scale):
    b, s, _ = v.shape
    v32 = v.astype(jnp.float32)
    count = jnp.arange(1, s + 1, dtype=jnp.float32)[None, :, None]
    groups = jnp.split(v32, N_POOL_GROUPS, axis=-1)
    outs = []
    for g, w in zip(groups, POOL_WINDOWS):
        csum = jnp.cumsum(g, axis=1)
        lag = jnp.pad(csum, ((0, 0), (w, 0), (0, 0)))[:, :s]
        mean = (csum - lag) / jnp.minimum(count, w)
        outs.append(mean - g)
    d = jnp.stack(outs, axis=2).astype(v.dtype)
    d = jnp.einsum("bsgc,gcd->bsgd", d, w_pool).reshape(b, s, D_POOL)
    return d * scale

def first_inputs(seed: int = 0) -> dict:
    key = jax.random.key(seed)
    ks = jax.random.split(key, 24)
    f32 = jnp.float32
    L = DEPTH

    def nrm(k, shape, fan_in):
        return jax.random.normal(k, shape, f32) * (fan_in ** -0.5)

    def gain(k, shape):
        return 1.0 + 0.05 * jax.random.normal(k, shape, f32)

    return {
        "x": jax.random.normal(ks[0], (BATCH, SEQ, D_MODEL), f32),
        "p": jax.random.normal(ks[1], (DEPTH, BATCH, SEQ, D_PLE), f32),
        "g_mix_pre": gain(ks[2], (L, D_MODEL)),
        "w_in": nrm(ks[3], (L, D_MODEL, D_IN), D_MODEL),
        "b_forget": 0.1 * jax.random.normal(ks[4], (L, N_ATT_HEADS), f32),
        "w_conf_dw": nrm(ks[5], (L, CONF_KERNEL, D_CONF), CONF_KERNEL),
        "conf_ln_g": gain(ks[6], (L, D_CONF)),
        "conf_ln_b": 0.02 * jax.random.normal(ks[7], (L, D_CONF), f32),
        "w_conf_pw": nrm(ks[8], (L, D_CONF, D_CONF), D_CONF),
        "w_sc": nrm(ks[9], (L, SC_KERNEL, D_SC), SC_KERNEL),
        "w_pool": nrm(ks[10], (L, N_POOL_GROUPS, POOL_GROUP_DIM, POOL_GROUP_DIM), POOL_GROUP_DIM),
        "pool_scale": gain(ks[11], (L, D_POOL)),
        "w_out": nrm(ks[12], (L, D_MIX, D_MODEL), D_MIX),
        "g_mix_post": gain(ks[13], (L, D_MODEL)),
        "g_mlp_pre": gain(ks[14], (L, D_MODEL)),
        "w_up": nrm(ks[15], (L, D_MODEL, D_FF), D_MODEL),
        "w_down": nrm(ks[16], (L, D_FF, D_MODEL), D_FF),
        "g_mlp_post": gain(ks[17], (L, D_MODEL)),
        "g_ple_pre": gain(ks[18], (L, D_MODEL)),
        "w_ple_gate": nrm(ks[19], (L, D_MODEL, D_MODEL), D_MODEL),
        "w_ple_proj": nrm(ks[20], (L, D_PLE, D_MODEL), D_PLE),
        "g_ple_post": gain(ks[21], (L, D_MODEL)),
    }

def first_block(x, p, g_mix_pre, w_in, b_forget, w_conf_dw, conf_ln_g, conf_ln_b, w_conf_pw,
              w_sc, w_pool, pool_scale, w_out, g_mix_post, g_mlp_pre, w_up, w_down,
              g_mlp_post, g_ple_pre, w_ple_gate, w_ple_proj, g_ple_post):
    h = x
    for i in range(DEPTH):
        xn = rms_norm(h, g_mix_pre[i])
        z = xn @ w_in[i]
        conf_ab, q, k, v, f_logit, sc_h, sc_b, sc_c, pool_v = jnp.split(z, SPLIT_IDX, axis=-1)
        y_conf = conformer_conv(conf_ab, w_conf_dw[i], conf_ln_g[i], conf_ln_b[i], w_conf_pw[i])
        y_att = forgetting_attention(q, k, v, f_logit + b_forget[i])
        y_sc = short_conv_mixer(sc_h, sc_b, sc_c, w_sc[i])
        y_pool = multiscale_pool(pool_v, w_pool[i], pool_scale[i])
        mix = jnp.concatenate([y_conf, y_att, y_sc, y_pool], axis=-1) @ w_out[i]
        h = h + rms_norm(mix, g_mix_post[i])
        hn = rms_norm(h, g_mlp_pre[i])
        ff = jnp.square(jax.nn.relu(hn @ w_up[i])) @ w_down[i]
        h = h + rms_norm(ff, g_mlp_post[i])
        gate = jax.nn.sigmoid(rms_norm(h, g_ple_pre[i]) @ w_ple_gate[i])
        e = (p[i] @ w_ple_proj[i]) * gate
        h = h + rms_norm(e, g_ple_post[i])
    return h


DEPTH_2 = 2

N_EVEN = (DEPTH_2 + 1) // 2
N_ODD = DEPTH_2 // 2
ROPE_THETA = 10000.0

MLA_HEADS = 8
MLA_Q_LORA = 384
MLA_KV_LORA = 256
MLA_NOPE = 64
MLA_ROPE = 32
MLA_V = 64
DIFF_HEADS = 4
DIFF_HD = 64
DIFF_V = 2 * DIFF_HD
A_IN = MLA_Q_LORA + MLA_KV_LORA + MLA_ROPE + 2 * DIFF_HEADS * 2 * DIFF_HD + DIFF_HEADS * DIFF_V
A_MIX = MLA_HEADS * MLA_V + DIFF_HEADS * DIFF_V

SSM_HEADS = 8
SSM_HEADDIM = 64
SSM_INNER = SSM_HEADS * SSM_HEADDIM
SSM_GROUPS = 2
SSM_STATE = 128
SSM_CONV = 4
SSM_CHUNK = 128
SSM_CONV_DIM = SSM_INNER + 2 * SSM_GROUPS * SSM_STATE
HG_HEADS = 4
HG_EXPAND = 128
HG_VDIM = 128
HG_KDIM_TOTAL = HG_HEADS * HG_EXPAND
HG_WIDTH = HG_HEADS * HG_VDIM
HG_CHUNK = 64
S_IN = SSM_INNER + SSM_CONV_DIM + SSM_HEADS + 2 * HG_KDIM_TOTAL + 2 * HG_WIDTH
S_MIX = SSM_INNER + HG_WIDTH

D_FF_2 = -(-8 * D_MODEL // (3 * 256)) * 256


F32 = jnp.float32

def rms_norm_2(x, w):
    xf = x.astype(F32)
    y = xf * lax.rsqrt(jnp.mean(xf * xf, axis=-1, keepdims=True) + EPS)
    return (y * w.astype(F32)).astype(x.dtype)

def split_cols(y, sizes):
    offsets = [int(v) for v in np.cumsum(sizes)[:-1]]
    return jnp.split(y, offsets, axis=-1)

def rope_tables(seq_len, dim):
    inv_freq = 1.0 / (ROPE_THETA ** (jnp.arange(0, dim, 2, dtype=F32) / dim))
    ang = jnp.arange(seq_len, dtype=F32)[:, None] * inv_freq[None, :]
    ang = jnp.concatenate([ang, ang], axis=-1)
    return jnp.cos(ang), jnp.sin(ang)

def apply_rope(x, cos, sin):
    half = x.shape[-1] // 2
    x1, x2 = x[..., :half], x[..., half:]
    rot = jnp.concatenate([-x2, x1], axis=-1)
    return (x.astype(F32) * cos + rot.astype(F32) * sin).astype(x.dtype)

def causal_attention(q, k, v, scale):
    bsz, nh, s_len, dk = q.shape
    dv = v.shape[-1]
    nb = s_len // Q_BLOCK
    qb = q.reshape(bsz, nh, nb, Q_BLOCK, dk).transpose(2, 0, 1, 3, 4)
    kpos = jnp.arange(s_len)

    def one_block(args):
        qi, bi = args
        s = jnp.einsum('bhqd,bhkd->bhqk', qi, k, preferred_element_type=F32) * scale
        qpos = bi * Q_BLOCK + jnp.arange(Q_BLOCK)
        s = jnp.where(kpos[None, :] <= qpos[:, None], s, -jnp.inf)
        p = jax.nn.softmax(s, axis=-1)
        return jnp.einsum('bhqk,bhkd->bhqd', p.astype(v.dtype), v)

    out = lax.map(one_block, (qb, jnp.arange(nb)))
    return out.transpose(1, 2, 0, 3, 4).reshape(bsz, nh, s_len, dv)

def attention_mixer(h, w_in, q_norm, w_uq, kv_norm, w_ukv, lq1, lk1, lq2, lk2, subln, w_out, lambda_init):
    bsz, s_len, _ = h.shape
    proj = h @ w_in
    c_q, c_kv, k_rope, dq, dk, dv = split_cols(
        proj, [MLA_Q_LORA, MLA_KV_LORA, MLA_ROPE, DIFF_HEADS * 2 * DIFF_HD, DIFF_HEADS * 2 * DIFF_HD, DIFF_HEADS * DIFF_V])
    q = (rms_norm_2(c_q, q_norm) @ w_uq).reshape(bsz, s_len, MLA_HEADS, MLA_NOPE + MLA_ROPE).transpose(0, 2, 1, 3)
    q_nope, q_pe = q[..., :MLA_NOPE], q[..., MLA_NOPE:]
    kv = (rms_norm_2(c_kv, kv_norm) @ w_ukv).reshape(bsz, s_len, MLA_HEADS, MLA_NOPE + MLA_V).transpose(0, 2, 1, 3)
    k_nope, v_mla = kv[..., :MLA_NOPE], kv[..., MLA_NOPE:]
    cos_r, sin_r = rope_tables(s_len, MLA_ROPE)
    q_pe = apply_rope(q_pe, cos_r, sin_r)
    k_pe = apply_rope(k_rope[:, None], cos_r, sin_r)
    q_mla = jnp.concatenate([q_nope, q_pe], axis=-1)
    k_mla = jnp.concatenate([k_nope, jnp.broadcast_to(k_pe, (bsz, MLA_HEADS, s_len, MLA_ROPE))], axis=-1)
    o_mla = causal_attention(q_mla, k_mla, v_mla, (MLA_NOPE + MLA_ROPE) ** -0.5)
    o_mla = o_mla.transpose(0, 2, 1, 3).reshape(bsz, s_len, MLA_HEADS * MLA_V)
    cos_d, sin_d = rope_tables(s_len, DIFF_HD)
    dq = apply_rope(dq.reshape(bsz, s_len, DIFF_HEADS, 2, DIFF_HD).transpose(0, 3, 2, 1, 4), cos_d, sin_d)
    dk = apply_rope(dk.reshape(bsz, s_len, DIFF_HEADS, 2, DIFF_HD).transpose(0, 3, 2, 1, 4), cos_d, sin_d)
    dv = dv.reshape(bsz, s_len, DIFF_HEADS, DIFF_V).transpose(0, 2, 1, 3)
    v2 = jnp.broadcast_to(dv[:, None], (bsz, 2, DIFF_HEADS, s_len, DIFF_V)).reshape(bsz, 2 * DIFF_HEADS, s_len, DIFF_V)
    o2 = causal_attention(dq.reshape(bsz, 2 * DIFF_HEADS, s_len, DIFF_HD),
                          dk.reshape(bsz, 2 * DIFF_HEADS, s_len, DIFF_HD), v2, DIFF_HD ** -0.5)
    o2 = o2.reshape(bsz, 2, DIFF_HEADS, s_len, DIFF_V)
    lam = (jnp.exp(jnp.sum(lq1.astype(F32) * lk1.astype(F32))) - jnp.exp(jnp.sum(lq2.astype(F32) * lk2.astype(F32)))
           + lambda_init).astype(o2.dtype)
    o_diff = o2[:, 0] - lam * o2[:, 1]
    o_diff = rms_norm_2(o_diff, subln) * (1.0 - lambda_init)
    o_diff = o_diff.transpose(0, 2, 1, 3).reshape(bsz, s_len, DIFF_HEADS * DIFF_V)
    return jnp.concatenate([o_mla, o_diff], axis=-1) @ w_out

def causal_depthwise_conv_2(x, w, b):
    ch = x.shape[-1]
    y = lax.conv_general_dilated(x, w[:, None, :].astype(x.dtype), window_strides=(1,),
                                 padding=[(SSM_CONV - 1, 0)], dimension_numbers=('NWC', 'WIO', 'NWC'),
                                 feature_group_count=ch)
    return y + b

def ssd_chunked(xs, dt, a_head, b_in, c_in):
    bsz, s_len, _ = xs.shape
    nc, L = s_len // SSM_CHUNK, SSM_CHUNK
    G, R, P, N = SSM_GROUPS, SSM_HEADS // SSM_GROUPS, SSM_HEADDIM, SSM_STATE
    dtc = dt.reshape(bsz, nc, L, G, R)
    xh = xs.astype(F32).reshape(bsz, nc, L, G, R, P) * dtc[..., None]
    a = (dtc * a_head.reshape(G, R)).transpose(0, 1, 3, 4, 2)
    a_cs = jnp.cumsum(a, axis=-1)
    causal = jnp.tril(jnp.ones((L, L), dtype=bool))
    seg = jnp.exp(jnp.where(causal, a_cs[..., :, None] - a_cs[..., None, :], -jnp.inf))
    bc = b_in.astype(F32).reshape(bsz, nc, L, G, N)
    cc = c_in.astype(F32).reshape(bsz, nc, L, G, N)
    cb = jnp.einsum('bclgn,bcsgn->bcgls', cc, bc)
    y_diag = jnp.einsum('bcgls,bcgrls,bcsgrp->bclgrp', cb, seg, xh)
    decay_states = jnp.exp(a_cs[..., -1:] - a_cs)
    states = jnp.einsum('bclgn,bcgrl,bclgrp->bcgrpn', bc, decay_states, xh)
    chunk_decay = jnp.exp(a_cs[..., -1])

    def step(h_prev, inp):
        st, dec = inp
        return dec[..., None, None] * h_prev + st, h_prev

    h0 = jnp.zeros((bsz, G, R, P, N), F32)
    _, prev = lax.scan(step, h0, (states.transpose(1, 0, 2, 3, 4, 5), chunk_decay.transpose(1, 0, 2, 3)))
    prev = prev.transpose(1, 0, 2, 3, 4, 5)
    y_off = jnp.einsum('bclgn,bcgrpn,bcgrl->bclgrp', cc, prev, jnp.exp(a_cs))
    return (y_diag + y_off).reshape(bsz, s_len, SSM_HEADS, P)

def hgrn2_chunked(q, k, v, log_f):
    bsz, s_len, nh, kd = q.shape
    vd = v.shape[-1]
    nc, L = s_len // HG_CHUNK, HG_CHUNK

    def chunks(t):
        return t.astype(F32).reshape(bsz, nc, L, nh, t.shape[-1]).transpose(1, 0, 3, 2, 4)

    causal = jnp.tril(jnp.ones((L, L), dtype=bool))[None, None, :, :, None]

    def step(state, inp):
        qc, kc, vc, gc = inp
        g_cum = jnp.cumsum(gc, axis=2)
        g_last = g_cum[:, :, -1:, :]
        o_inter = jnp.einsum('bhlk,bhkv->bhlv', qc * jnp.exp(g_cum), state)
        decay = jnp.exp(jnp.where(causal, g_cum[:, :, :, None, :] - g_cum[:, :, None, :, :], -jnp.inf))
        scores = jnp.einsum('bhlk,bhlsk,bhsk->bhls', qc, decay, kc)
        o = o_inter + jnp.einsum('bhls,bhsv->bhlv', scores, vc)
        state = (jnp.exp(g_last[:, :, 0, :])[..., None] * state
                 + jnp.einsum('bhsk,bhsv->bhkv', kc * jnp.exp(g_last - g_cum), vc))
        return state, o

    s0 = jnp.zeros((bsz, nh, kd, vd), F32)
    _, o = lax.scan(step, s0, (chunks(q), chunks(k), chunks(v), chunks(log_f)))
    return o.transpose(1, 0, 3, 2, 4).reshape(bsz, s_len, nh, vd)

def recurrent_mixer(h, w_in, conv_w, conv_b, dt_bias, a_log, d_skip, ssm_norm, g_norm, lb, w_out):
    bsz, s_len, _ = h.shape
    proj = h @ w_in
    z, xbc, dt, hq, hf, hi, hg = split_cols(
        proj, [SSM_INNER, SSM_CONV_DIM, SSM_HEADS, HG_KDIM_TOTAL, HG_KDIM_TOTAL, HG_WIDTH, HG_WIDTH])
    xbc = jax.nn.silu(causal_depthwise_conv_2(xbc, conv_w, conv_b))
    xs, b_in, c_in = split_cols(xbc, [SSM_INNER, SSM_GROUPS * SSM_STATE, SSM_GROUPS * SSM_STATE])
    dt = jax.nn.softplus(dt.astype(F32) + dt_bias.astype(F32))
    a_head = -jnp.exp(a_log.astype(F32))
    y = ssd_chunked(xs, dt, a_head, b_in, c_in)
    y = y + d_skip.astype(F32)[:, None] * xs.astype(F32).reshape(bsz, s_len, SSM_HEADS, SSM_HEADDIM)
    y = y.astype(h.dtype).reshape(bsz, s_len, SSM_INNER) * jax.nn.silu(z)
    gsz = SSM_INNER // SSM_GROUPS
    y = rms_norm_2(y.reshape(bsz, s_len, SSM_GROUPS, gsz), ssm_norm.reshape(SSM_GROUPS, gsz)).reshape(bsz, s_len, SSM_INNER)
    lb = lb.astype(F32)
    xf = hf.astype(F32)
    log_f = jnp.logaddexp(jnp.log(lb), jnp.log1p(-lb) + jax.nn.log_sigmoid(xf))
    k_in = (1.0 - lb) * jax.nn.sigmoid(-xf)
    q = jax.nn.silu(hq).reshape(bsz, s_len, HG_HEADS, HG_EXPAND)
    o = hgrn2_chunked(q, k_in.reshape(bsz, s_len, HG_HEADS, HG_EXPAND), hi.reshape(bsz, s_len, HG_HEADS, HG_VDIM),
                      log_f.reshape(bsz, s_len, HG_HEADS, HG_EXPAND)).astype(h.dtype)
    o = rms_norm_2(o, g_norm) * jax.nn.silu(hg).reshape(bsz, s_len, HG_HEADS, HG_VDIM)
    o = o.reshape(bsz, s_len, HG_WIDTH)
    return jnp.concatenate([y, o], axis=-1) @ w_out

def swiglu(h, w_gate, w_up, w_down):
    return (jax.nn.silu(h @ w_gate) * (h @ w_up)) @ w_down

def second_inputs(seed: int = 0) -> dict:
    key = jax.random.key(seed)
    ks = jax.random.split(key, 32)

    def nrm(k, shape, fan_in):
        return jax.random.normal(k, shape, F32) * (fan_in ** -0.5)

    def gain(k, shape):
        return 1.0 + 0.05 * jax.random.normal(k, shape, F32)

    dt0 = jnp.exp(jax.random.uniform(ks[20], (N_ODD, SSM_HEADS), F32, math.log(1e-3), math.log(1e-1)))
    return {
        'x': jax.random.normal(ks[0], (BATCH, SEQ, D_MODEL), F32),
        'norm_mix': gain(ks[1], (DEPTH_2, D_MODEL)),
        'norm_ffn': gain(ks[2], (DEPTH_2, D_MODEL)),
        'norm_final': gain(ks[3], (D_MODEL,)),
        'a_w_in': nrm(ks[4], (N_EVEN, D_MODEL, A_IN), D_MODEL),
        'a_q_norm': gain(ks[5], (N_EVEN, MLA_Q_LORA)),
        'a_w_uq': nrm(ks[6], (N_EVEN, MLA_Q_LORA, MLA_HEADS * (MLA_NOPE + MLA_ROPE)), MLA_Q_LORA),
        'a_kv_norm': gain(ks[7], (N_EVEN, MLA_KV_LORA)),
        'a_w_ukv': nrm(ks[8], (N_EVEN, MLA_KV_LORA, MLA_HEADS * (MLA_NOPE + MLA_V)), MLA_KV_LORA),
        'a_lq1': 0.1 * jax.random.normal(ks[9], (N_EVEN, DIFF_HD), F32),
        'a_lk1': 0.1 * jax.random.normal(ks[10], (N_EVEN, DIFF_HD), F32),
        'a_lq2': 0.1 * jax.random.normal(ks[11], (N_EVEN, DIFF_HD), F32),
        'a_lk2': 0.1 * jax.random.normal(ks[12], (N_EVEN, DIFF_HD), F32),
        'a_subln': gain(ks[13], (N_EVEN, DIFF_V)),
        'a_w_out': nrm(ks[14], (N_EVEN, A_MIX, D_MODEL), A_MIX),
        's_w_in': nrm(ks[15], (N_ODD, D_MODEL, S_IN), D_MODEL),
        's_conv_w': nrm(ks[16], (N_ODD, SSM_CONV, SSM_CONV_DIM), SSM_CONV),
        's_conv_b': 0.02 * jax.random.normal(ks[17], (N_ODD, SSM_CONV_DIM), F32),
        's_dt_bias': dt0 + jnp.log(-jnp.expm1(-dt0)),
        's_a_log': jnp.log(jax.random.uniform(ks[18], (N_ODD, SSM_HEADS), F32, 1.0, 16.0)),
        's_d': gain(ks[19], (N_ODD, SSM_HEADS)),
        's_norm': gain(ks[21], (N_ODD, SSM_INNER)),
        'h_g_norm': gain(ks[22], (N_ODD, HG_VDIM)),
        'h_lower_bound': 0.1 * jax.random.normal(ks[23], (DEPTH_2, HG_KDIM_TOTAL), F32),
        's_w_out': nrm(ks[24], (N_ODD, S_MIX, D_MODEL), S_MIX),
        'ffn_gate': nrm(ks[25], (DEPTH_2, D_MODEL, D_FF_2), D_MODEL),
        'ffn_up': nrm(ks[26], (DEPTH_2, D_MODEL, D_FF_2), D_MODEL),
        'ffn_down': nrm(ks[27], (DEPTH_2, D_FF_2, D_MODEL), D_FF_2),
    }

def second_block(x, norm_mix, norm_ffn, norm_final, a_w_in, a_q_norm, a_w_uq, a_kv_norm, a_w_ukv,
              a_lq1, a_lk1, a_lq2, a_lk2, a_subln, a_w_out, s_w_in, s_conv_w, s_conv_b, s_dt_bias,
              s_a_log, s_d, s_norm, h_g_norm, h_lower_bound, s_w_out, ffn_gate, ffn_up, ffn_down):
    p_lb = jax.nn.softmax(h_lower_bound.astype(F32), axis=0)
    lb_all = jnp.cumsum(p_lb, axis=0) - p_lb[0:1]
    for l in range(DEPTH_2):
        hn = rms_norm_2(x, norm_mix[l])
        i = l // 2
        if l % 2 == 0:
            lambda_init = 0.8 - 0.6 * math.exp(-0.3 * l)
            m = attention_mixer(hn, a_w_in[i], a_q_norm[i], a_w_uq[i], a_kv_norm[i], a_w_ukv[i],
                                a_lq1[i], a_lk1[i], a_lq2[i], a_lk2[i], a_subln[i], a_w_out[i], lambda_init)
        else:
            m = recurrent_mixer(hn, s_w_in[i], s_conv_w[i], s_conv_b[i], s_dt_bias[i], s_a_log[i], s_d[i],
                                s_norm[i], h_g_norm[i], lb_all[l], s_w_out[i])
        x = x + m
        x = x + swiglu(rms_norm_2(x, norm_ffn[l]), ffn_gate[l], ffn_up[l], ffn_down[l])
    return rms_norm_2(x, norm_final)


def setup_inputs(seed=0):
    out = dict(first_inputs(seed))
    for name, value in second_inputs(seed + 1).items():
        if name != "x":
            out[name + "_2"] = value
    return out


def reference(
    x, p, g_mix_pre, w_in, b_forget, w_conf_dw, conf_ln_g, conf_ln_b, w_conf_pw, w_sc, w_pool,
    pool_scale, w_out, g_mix_post, g_mlp_pre, w_up, w_down, g_mlp_post, g_ple_pre, w_ple_gate,
    w_ple_proj, g_ple_post, norm_mix_2, norm_ffn_2, norm_final_2, a_w_in_2, a_q_norm_2,
    a_w_uq_2, a_kv_norm_2, a_w_ukv_2, a_lq1_2, a_lk1_2, a_lq2_2, a_lk2_2, a_subln_2, a_w_out_2,
    s_w_in_2, s_conv_w_2, s_conv_b_2, s_dt_bias_2, s_a_log_2, s_d_2, s_norm_2, h_g_norm_2,
    h_lower_bound_2, s_w_out_2, ffn_gate_2, ffn_up_2, ffn_down_2,
):
    x = first_block(
        x, p, g_mix_pre, w_in, b_forget, w_conf_dw, conf_ln_g, conf_ln_b, w_conf_pw, w_sc,
        w_pool, pool_scale, w_out, g_mix_post, g_mlp_pre, w_up, w_down, g_mlp_post, g_ple_pre,
        w_ple_gate, w_ple_proj, g_ple_post,
    )
    return second_block(
        x, norm_mix_2, norm_ffn_2, norm_final_2, a_w_in_2, a_q_norm_2, a_w_uq_2, a_kv_norm_2,
        a_w_ukv_2, a_lq1_2, a_lk1_2, a_lq2_2, a_lk2_2, a_subln_2, a_w_out_2, s_w_in_2,
        s_conv_w_2, s_conv_b_2, s_dt_bias_2, s_a_log_2, s_d_2, s_norm_2, h_g_norm_2,
        h_lower_bound_2, s_w_out_2, ffn_gate_2, ffn_up_2, ffn_down_2,
    )


_drawn_inputs = setup_inputs


def setup_inputs(seed=0):
    import zlib

    import numpy as np

    out = dict(_drawn_inputs(seed))
    spreads = {}
    factors = {'b_forget': 8.0,
     'conf_ln_g': 2.872,
     'conf_ln_b': 7.677,
     'pool_scale': 2.773,
     'g_ple_pre': 5.235,
     'a_q_norm_2': 8.0,
     'a_kv_norm_2': 8.0,
     'a_lq1_2': 5.757,
     'a_lk1_2': 200.0,
     'a_subln_2': 9.11,
     's_conv_b_2': 6.762,
     's_d_2': 200.0,
     's_norm_2': 39.65,
     'h_g_norm_2': 72.714,
     'h_lower_bound_2': 8.0,
     'norm_ffn_2': 5.936,
     'a_lq2_2': 5.433,
     'a_lk2_2': 4.901,
     's_dt_bias_2': 8.0,
     's_a_log_2': 8.0}
    for name, (base, spread) in spreads.items():
        noise = np.random.default_rng([zlib.crc32(name.encode()), seed]).standard_normal(out[name].shape)
        drawn = base * np.exp(spread * noise) if base else spread * noise
        out[name] = jnp.asarray(drawn.astype(out[name].dtype))
    for name, factor in factors.items():
        out[name] = (out[name] * factor).astype(out[name].dtype)
    return out
```

```python
from collections import namedtuple
from contextlib import ExitStack

import numpy as np

import concourse.bass as bass
from concourse import mybir

ALU = mybir.AluOpType
ACT = mybir.ActivationFunctionType
F32 = mybir.dt.float32
F32R = mybir.dt.float32r
BF16 = mybir.dt.bfloat16
AX = mybir.AxisListType.X

EPS = 1e-6
LAMBDA0 = 0.8 - 0.6 * float(np.exp(-0.3 * 0))
NEG = -1e30
NRAW = 3
NW = 4
SCN = 13568
LEVELS = [64, 32, 16, 8, 4, 2, 1]
TAPS = 31

C_ID, C_MA, C_MT, C_ONE, C_SEL, C_ROPE = 0, 128, 256, 384, 512, 1536
C_N = C_ROPE + 2 * 96

P_COLS = [("g_mix_pre", 8), ("g_mlp_pre", 8), ("g_ple_pre", 8), ("nm0", 8), ("nm1", 8), ("nf0", 8), ("nf1", 8),
          ("dw", 2 * TAPS), ("ln_g", 2), ("ln_b", 2), ("sc", 6), ("pool_scale", 2), ("cw", 32), ("cb", 8),
          ("qn", 3), ("kvn", 2), ("subln", 1), ("s_norm", 4), ("g_norm", 1), ("lb0", 4), ("lb1", 4),
          ("bf", 1), ("dtb", 1), ("alog", 1), ("fsel", 4), ("eps", 1)]
P_AT = {}
_at = 0
for _n, _c in P_COLS:
    P_AT[_n] = _at
    _at += _c
P_N = _at


Done = namedtuple("Done", "sem count")


class Queue:

    def __init__(self, sem):
        self.sem, self.n, self.items, self.seen = sem, 0, [], {}

    def emit(self, fn, waits, inc=True):
        need = []
        for sem, count in flat(waits):
            if self.seen.get(id(sem), 0) < count:
                self.seen[id(sem)] = count
                need.append((sem, count))
        if inc:
            self.n += 1
        self.items.append((need, fn, inc))
        return Done(self.sem, self.n)

    def last(self):
        return Done(self.sem, self.n) if self.n else None

    def replay(self, eng):
        for need, fn, inc in self.items:
            for sem, count in need:
                eng.wait_ge(sem, count)
            ins = fn(eng)
            if inc:
                ins.then_inc(self.sem, 1)


def flat(w):
    if w is None:
        return []
    if isinstance(w, Done):
        return [w]
    return [t for x in w for t in flat(x)]


def program(nc, D, out):
    with ExitStack() as ctx:
        def sb(name, shape, dt=F32):
            return ctx.enter_context(nc.sbuf_tensor(name, shape, dt))

        def sem(name):
            return ctx.enter_context(nc.semaphore(name))

        ps = [ctx.enter_context(nc.psum_tensor(f"ps{i}", [128, 512], F32)) for i in range(8)]
        cst = sb("cst", [128, C_N])
        prm = sb("prm", [128, P_N])
        rows = sb("rows", [128, 2, 1024])
        srow = sb("srow", [128, 264])
        h = sb("h", [128, 2, 1024])
        xf = sb("xf", [128, 8, 256])
        xh = sb("xh", [128, 8, 256], F32R)
        xl = sb("xl", [128, 8, 256], F32R)
        hs = sb("hs", [128, 1024])
        junk = sb("junk", [128, 1024])
        raw = [sb(f"raw{i}", [128, 2048]) for i in range(NRAW)]
        wh = [sb(f"wh{i}", [128, 2048], F32R) for i in range(NW)]
        wl = [sb(f"wl{i}", [128, 2048], F32R) for i in range(NW)]
        fh = sb("fh", [128, 2, 512], F32R)
        fl = sb("fl", [128, 2, 512], F32R)
        idb = sb("idb", [128, 128], BF16)
        mab = sb("mab", [128, 128], BF16)
        mtb = sb("mtb", [128, 128], BF16)
        st = sb("st", [128, 64])
        SC = sb("SC", [128, SCN])

        PE, AC, VE, GP = (Queue(sem(n)) for n in ("s_pe", "s_act", "s_dve", "s_pool"))
        SP = Queue(sem("s_sp"))
        s_raw = [sem(f"s_raw{i}") for i in range(NRAW)]
        s_misc = {}

        def pe(fn, *w, inc=True):
            return PE.emit(fn, w, inc)

        def act(o, i, f, *w, **kw):
            return AC.emit(lambda e: e.activation(o, i, f, **kw), w)

        def vec(fn, *w):
            return VE.emit(fn, w)

        def pool(fn, *w):
            return GP.emit(fn, w)

        def dma(name, dst, src, *w, q=None):
            if name not in s_misc:
                s_misc[name] = [sem("d_" + name), 0]
            box = s_misc[name]
            box[1] += 16
            (q or SP).emit(lambda e: e.dma_start(dst, src).then_inc(box[0], 16), w, inc=False)
            return Done(box[0], box[1])

        def tt(o, a, b, op, *w):
            return vec(lambda e: e.tensor_tensor(o, a, b, op), *w)

        def ts(o, a, s1, s2, o1, o2, *w):
            if o2 is None:
                return vec(lambda e: e.tensor_scalar(o, a, s1, None, o1), *w)
            return vec(lambda e: e.tensor_scalar(o, a, s1, s2, o1, o2), *w)

        def stt(o, a, s, b, o1, o2, *w):
            return vec(lambda e: e.scalar_tensor_tensor(o, a, s, b, o1, o2), *w)

        def vcopy(o, a, *w):
            return vec(lambda e: e.tensor_copy(o, a), *w)

        def bar():
            return [q.last() for q in (PE, AC, VE, GP) if q.last()]

        free = [(i, None) for i in range(8)]

        def take():
            return free.pop(0)

        def give(i, tok):
            free.append((i, tok))

        def P(name, i=0, n=1):
            return prm[:, P_AT[name] + i:P_AT[name] + i + n]

        def C(a, n=128):
            return cst[:, a:a + n]

        slots = []

        def slot(src, kt, n):
            slots.append((src, kt, n))
            return len(slots) - 1

        def cols(w, a, n):
            return slot(w.rearrange("(k p) n -> p k n", p=128)[:, :, a:a + n], w.shape[0] // 128, n)

        def krows(w, a, n):
            return slot(w[a * 128:(a + n) * 128, :].rearrange("(k p) n -> p k n", p=128), n, w.shape[1])

        def kcols(w, k, nk, a, n):
            return slot(w[k * 128:(k + nk) * 128, a:a + n].rearrange("(k p) n -> p k n", p=128), nk, n)

        w_in = D["w_in"]
        SEG = {"a": 0, "b": 256, "q": 512, "k": 768, "v": 1024, "h": 1284, "sb": 1540, "c": 1796, "p": 2052}
        S = {}
        for n in ("a", "b", "q", "k", "v", "h", "c", "sb", "p"):
            S[n] = cols(w_in, SEG[n], 256)
        S["out"] = [krows(D["w_out"], 2 * i, 2) for i in range(4)]
        S["ff"] = [(cols(D["w_up"], 256 * j, 256), krows(D["w_down"], 2 * j, 2)) for j in range(16)]
        S["proj"] = krows(D["w_ple_proj"], 0, 2)
        S["gate"] = [krows(D["w_ple_gate"], 2 * i, 2) for i in range(4)]
        aw = D["a_w_in_2"]
        for n, c in (("dq", 672), ("dk", 1184), ("dv", 1696)):
            S[n] = [kcols(aw, 4 * i, 4, c, 512) for i in range(2)]
        S["cq"] = [cols(aw, 0, 256), cols(aw, 256, 128)]
        S["ckv"] = cols(aw, 384, 256)
        S["kr"] = cols(aw, 640, 32)
        S["uq"] = [cols(D["a_w_uq_2"], 384 * i, 384) for i in range(2)]
        S["ukv"] = krows(D["a_w_ukv_2"], 0, 2)
        S["aout"] = [krows(D["a_w_out_2"], 2 * i, 2) for i in range(4)]

        def ffn_slots(l):
            return [(cols(D[f"ffn_gate_{l}"], 256 * j, 256), cols(D[f"ffn_up_{l}"], 256 * j, 256),
                     krows(D[f"ffn_down_{l}"], 2 * j, 2)) for j in range(11)]

        S["f0"] = ffn_slots(0)
        sw = D["s_w_in_2"]
        S["z"] = [kcols(sw, 4 * i, 4, 0, 512) for i in range(2)]
        S["xbc"] = [cols(sw, 512 + 256 * i, 256) for i in range(4)]
        S["hq"] = [cols(sw, 1544 + 256 * i, 256) for i in range(2)]
        S["hf"] = [cols(sw, 2056 + 256 * i, 256) for i in range(2)]
        S["hi"] = [kcols(sw, 4 * i, 4, 2568, 512) for i in range(2)]
        S["hg"] = [kcols(sw, 4 * i, 4, 3080, 512) for i in range(2)]
        S["sout"] = [krows(D["s_w_out_2"], 2 * i, 2) for i in range(4)]
        S["f1"] = ffn_slots(1)

        loaded, split_tok, used = [], [], {}

        def load(i):
            src, kt, n = slots[i]
            r = i % NRAW
            dst = raw[r][:, 0:kt * n].rearrange("p (k n) -> p k n", k=kt)
            free_at = split_tok[i - NRAW] if i >= NRAW else None
            SP.emit(lambda e: e.dma_start(dst, src).then_inc(s_raw[r], 16), [free_at], inc=False)
            loaded.append(Done(s_raw[r], 16 * (i // NRAW + 1)))

        def split(i):
            src, kt, n = slots[i]
            r, b, m = i % NRAW, i % NW, kt * n
            gone = used[i - NW] if i >= NW else None
            hi = act(wh[b][:, 0:m], raw[r][:, 0:m], ACT.Copy, loaded[i], gone)
            lo = tt(wl[b][:, 0:m], raw[r][:, 0:m], wh[b][:, 0:m].bitcast(F32), ALU.subtract, loaded[i], gone, hi)
            split_tok.append(lo)
            if i + NRAW < len(slots):
                load(i + NRAW)

        def use(i):
            while len(split_tok) <= min(i + NW - 1, len(slots) - 1) and (
                    len(split_tok) < NW or len(split_tok) - NW in used):
                split(len(split_tok))
            _, kt, n = slots[i]
            b = i % NW
            v = [t[b][:, 0:kt * n].rearrange("p (k n) -> p k n", k=kt) for t in (wh, wl)]
            return v[0], v[1], split_tok[i]

        def mm3(o, a, al, b, bl, start, stop, *w, inc=False):
            pe(lambda e: e.matmul(o, a, b, start=start, stop=False, skip_group_check=True), *w, inc=False)
            pe(lambda e: e.matmul(o, al, b, start=False, stop=False, skip_group_check=True), inc=False)
            return pe(lambda e: e.matmul(o, a, bl, start=False, stop=stop, skip_group_check=True), inc=inc)

        def mm(o, a, b, start, stop, *w, inc=False):
            return pe(lambda e: e.matmul(o, a, b, start=start, stop=stop, skip_group_check=True), *w, inc=inc)

        def feat_mm(i, o, act_tok, *w):
            wH, wL, tok = use(i)
            kt = slots[i][1]
            nt = slots[i][2] // 128
            for t in range(nt):
                c = slice(128 * t, 128 * t + 128)
                for k in range(kt):
                    done = mm3(o[:, 256 * t:256 * t + 256], wH[:, k, c], wL[:, k, c], xh[:, k, :], xl[:, k, :],
                               k == 0, k == kt - 1, tok, act_tok, *w, inc=(t == nt - 1 and k == kt - 1))
            used[i] = done
            return done

        def tok_mm(i, outs, act_tok, *w, k0=0, first=True, final=True, a=None, wcols=None):
            wH, wL, tok = use(i)
            kt = slots[i][1]
            ah, al = a or (xh, xl)
            n = sum(len(o) for o in outs)
            for tb in range(2):
                s = slice(128 * tb, 128 * tb + 128)
                for o, c in outs[tb]:
                    n -= 1
                    for k in range(kt):
                        done = mm3(o, ah[:, k0 + k, s], al[:, k0 + k, s], wH[:, k, c], wL[:, k, c],
                                   first and k == 0, final and k == kt - 1, tok, act_tok, *w,
                                   inc=(n == 0 and k == kt - 1))
            used[i] = done
            return done

        epsc = P("eps")

        def rstd(dst, ss, n, *w):
            a = act(dst, ss, ACT.Ln, *w, scale=1.0 / n, bias=epsc)
            return act(dst, dst, ACT.Exp, a, scale=-0.5)

        def hilo(t0, t1, tok, *w):
            a = act(xh[:, t0:t1, :], xf[:, t0:t1, :], ACT.Copy, tok, *w)
            b = tt(xl[:, t0:t1, :], xf[:, t0:t1, :], xh[:, t0:t1, :].bitcast(F32), ALU.subtract, a, tok, *w)
            return [a, b]

        def to_xf(src, nt, t0, tb, gain, tok, *w):
            s = slice(128 * tb, 128 * tb + 128)
            done = []
            for c in range(0, nt, 4):
                m = min(4, nt - c)
                b, fr = take()
                for k in range(m):
                    t = pe(lambda e, k=k, c=c, b=b: e.transpose(ps[b][:, 128 * k:128 * k + 128],
                                                                src[:, 128 * (c + k):128 * (c + k) + 128],
                                                                C(C_ID)), tok, fr, t_c, inc=(k == m - 1))
                g = gain[:, c:c + m] if gain.shape[1] > 1 else gain.to_broadcast([128, m])
                g = g.unsqueeze(2).to_broadcast([128, m, 128])
                v = tt(xf[:, t0 + c:t0 + c + m, s], ps[b][:, 0:128 * m].rearrange("p (k n) -> p k n", k=m), g,
                       ALU.mult, t, *w)
                give(b, v)
                done.append(v)
            return done

        def norm_t(gain, tok):
            b0 = bar()
            done = []
            for tb in range(2):
                q = act(junk[:, :], h[:, tb, :], ACT.Square, tok, b0, accum_out=st[:, tb:tb + 1])
                r = rstd(st[:, 2 + tb:3 + tb], st[:, tb:tb + 1], 1024, q)
                s = ts(hs[:, :], h[:, tb, :], st[:, 2 + tb:3 + tb], None, ALU.mult, None, r, b0, done)
                t = to_xf(hs, 8, 0, tb, gain, s, b0)
                done = [t, PE.last()]
                b0 = [b0, t]
            return hilo(0, 8, b0, bar())

        def add_norm(src, row, row_tok, tb, tok, after=None):
            q = [act(junk[:, 512 * i:512 * i + 512], src[i], ACT.Square, tok, after,
                     accum_out=st[:, 4 + 2 * tb + i:5 + 2 * tb + i]) for i in range(2)]
            a = tt(st[:, 8 + tb:9 + tb], st[:, 4 + 2 * tb:5 + 2 * tb], st[:, 5 + 2 * tb:6 + 2 * tb], ALU.add, q)
            r = rstd(st[:, 10 + tb:11 + tb], st[:, 8 + tb:9 + tb], 1024, a)
            ends = []
            for i in range(2):
                c = slice(512 * i, 512 * i + 512)
                m = stt(hs[:, c], src[i], st[:, 10 + tb:11 + tb], row[:, c], ALU.mult, ALU.mult, r, row_tok, after)
                ends.append(m)
                e = tt(h[:, tb, c], h[:, tb, c], hs[:, c], ALU.add, m)
            return ends, e

        def proj_out(sl, tok):
            bk = [[take() for _ in range(2)] for _ in range(2)]
            fr = [x[1] for y in bk for x in y]
            for i in range(4):
                d = tok_mm(sl[i], [[(ps[bk[tb][c][0]][:, :], slice(512 * c, 512 * c + 512)) for c in range(2)]
                                   for tb in range(2)], tok, fr, k0=2 * i, first=(i == 0), final=(i == 3))
            return bk, d

        def add_banks(bk, d):
            for tb in range(2):
                for c in range(2):
                    o = h[:, tb, 512 * c:512 * c + 512]
                    e = tt(o, o, ps[bk[tb][c][0]][:, :], ALU.add, d)
                    give(bk[tb][c][0], e)
            return e

        def softplus(x, a, u, w, l, tok, *more):
            t = act(a, x, ACT.Abs, tok, *more)
            t = act(u, a, ACT.Exp, t, *more, scale=-1.0)
            t1 = ts(w, u, 1.0, None, ALU.add, None, t)
            t2 = act(l, w, ACT.Ln, t1, *more)
            t = ts(a, w, -1.0, None, ALU.add, None, t1)
            t = tt(a, u, a, ALU.subtract, t)
            t2 = vec(lambda e: e.reciprocal(w, w), t2)
            t = tt(a, a, w, ALU.mult, t, t2)
            t = tt(a, a, l, ALU.add, t)
            return stt(x, x, 0.0, a, ALU.max, ALU.add, t)

        class Scratch:
            def __init__(self):
                self.at = 0

            def __call__(self, *dims):
                n = int(np.prod(dims))
                v = SC[:, self.at:self.at + n]
                self.at += n
                assert self.at <= SCN, self.at
                if len(dims) == 2:
                    v = v.rearrange("p (a b) -> p a b", a=dims[0])
                if len(dims) == 3:
                    v = v.rearrange("p (a b c) -> p a b c", a=dims[0], b=dims[1])
                return v

        t_h = [dma(f"h{tb}", h[:, tb, :], D["x"][128 * tb:128 * tb + 128, :]) for tb in range(2)]
        t_p = dma("prm", prm[:, :], D["prm"])
        t_c = dma("cst", cst[:, :], D["cst"])
        for i in range(NRAW):
            load(i)
        t_r0 = dma("row0", rows[:, 0, :], D["g_mix_post"].partition_broadcast(128), q=GP)
        t_r1 = dma("row1", rows[:, 1, :], D["g_mlp_post"].partition_broadcast(128), q=GP)
        t_sr = dma("srow", srow[:, :], D["srow"].partition_broadcast(128), q=GP)
        t_m = [act(o[:, :], C(c), ACT.Copy, t_c) for o, c in ((idb, C_ID), (mab, C_MA), (mtb, C_MT))]

        sc = Scratch()
        wf = sc(8, 36)
        band = sc(4, 2, 256)
        wpw = sc(2, 256)
        wpb = sc(2, 128)
        upad = sc(2, 30 + 256)
        cacc = sc(2, 256)
        csq = sc(2, 256)
        sg = sc(512)
        qm = sc(4, 256)
        kT = sc(2, 256)
        vs = sc(2, 256)
        hsb = sc(512)
        cpad = sc(2, 2 + 256)
        scv = sc(2, 256)
        pv = sc(2, 256)
        dT = sc(2, 256)
        NCt = sc(256)
        CQ = sc(256)
        rk = sc(256)
        ft = sc(4, 256)
        Pm = sc(3, 384)
        PT = sc(2, 384)
        z1 = [pool(lambda e: e.memset(wf, 0.0)), pool(lambda e: e.memset(wpb, 0.0)), pool(lambda e: e.memset(upad, 0.0)),
              pool(lambda e: e.memset(qm, 0.0)), pool(lambda e: e.memset(cpad, 0.0)), pool(lambda e: e.memset(NCt, 0.0)),
              pool(lambda e: e.memset(CQ, 0.0))]
        wfv = w_in[:, 1280:1284].rearrange("(k p) n -> p k n", p=128)
        t_wf = [dma("wf0", wf[:, :, 0:4], wfv, z1, q=GP), dma("wf1", wf[:, :, 32:36], wfv, z1, q=GP)]
        t_bd = dma("band", band, D["band"], q=GP)
        t_pw = dma("pw", wpw, D["w_conf_pw"].rearrange("(k p) n -> p k n", p=128), q=GP)
        t_wp = [dma(f"wp{g}", wpb[64 * (g % 2):64 * (g % 2) + 64, g // 2, 64 * (g % 2):64 * (g % 2) + 64],
                    D["w_pool"][g], z1, q=GP) for g in range(4)]

        t_x = norm_t(P("g_mix_pre", 0, 8), [t_h, t_p])

        def bank_feat(sl, tok):
            b, fr = take()
            return b, feat_mm(sl, ps[b], tok, fr)

        def bank_mm(name):
            return bank_feat(S[name], t_x)

        def bank_tok(sl, n, tok=None):
            b, fr = take()
            d = tok_mm(sl, [[(ps[b][:, 256 * tb:256 * tb + n], slice(0, n))] for tb in range(2)], tok or t_x, fr)
            return b, d

        ba, da = bank_mm("a")
        bb, db = bank_mm("b")
        t1 = act(sg, ps[bb][:, :], ACT.Sigmoid, db)
        give(bb, t1)
        t_u = tt(upad[:, :, 30:286], ps[ba][:, :].rearrange("p (t n) -> p t n", t=2),
                 sg.rearrange("p (t n) -> p t n", t=2), ALU.mult, t1, da, z1)
        give(ba, t_u)

        conv_tok = [t_u, t_u]

        def conv_steps():
            for k in range(TAPS):
                for t in range(2):
                    src, w = upad[:, t, k:k + 256], P("dw", TAPS * t + k)
                    if k == 0:
                        conv_tok[t] = ts(cacc[:, t, :], src, w, None, ALU.mult, None, conv_tok[t])
                    else:
                        conv_tok[t] = stt(cacc[:, t, :], src, w, cacc[:, t, :], ALU.mult, ALU.add, conv_tok[t])
                    yield

        conv = conv_steps()

        def advance(gen, n):
            for _ in range(n):
                if next(gen, 0) is None:
                    continue
                return

        b, fr = take()
        for k in range(8):
            d = mm(ps[b][0:36, 0:256], wf[:, k, :], xf[:, k, :], k == 0, k == 7, t_wf, t_x, fr, inc=(k == 7))
        R = slice(0, 36)
        fx, fa, fu, fw = (ft[R, i, :] for i in range(4))
        t1 = ts(fx, ps[b][R, 0:256], P("bf")[R], -1.0, ALU.add, ALU.mult, d)
        give(b, t1)
        logf = softplus(fx, fa, fu, fw, junk[R, 0:256], t1, bar())
        t1 = ts(fx, fx, -1.0, None, ALU.mult, None, logf)
        t2 = vec(lambda e: e.memset(fu, 1.0), logf)
        t_scan = vec(lambda e: e.tensor_tensor_scan(fa, fu, fx, 0.0, ALU.mult, ALU.add), t1, t2)
        F4, G4 = slice(0, 4), slice(32, 36)
        t_cq = [vcopy(CQ[F4, :], ft[F4, 1, :], t_scan, z1),
                vec(lambda e: e.memset(CQ[G4, :], 1.0), z1),
                ts(NCt[G4, :], ft[G4, 1, :], -1.0, None, ALU.mult, None, t_scan, z1),
                vec(lambda e: e.memset(NCt[F4, :], 1.0), z1)]
        advance(conv, 8)

        b, d = bank_mm("q")
        t_q = []
        for i in range(2):
            pr = slice(64 * i, 64 * i + 64)
            t_q.append(act(qm.rearrange("p (t i) n -> p t i n", i=2)[pr, :, i, :],
                           ps[b][pr, :].rearrange("p (t n) -> p t n", t=2), ACT.Copy, d, z1, scale=0.125))
        give(b, t_q[-1])
        advance(conv, 9)
        b, d = bank_mm("k")
        t_k = act(kT, ps[b][:, :].rearrange("p (t n) -> p t n", t=2), ACT.Copy, d)
        give(b, t_k)
        advance(conv, 9)
        b, d = bank_tok(S["v"], 256)
        t_v = act(vs, ps[b][:, :].rearrange("p (t n) -> p t n", t=2), ACT.Copy, d)
        give(b, t_v)
        advance(conv, 9)
        b, d = bank_mm("h")
        t_hs = act(hsb, ps[b][:, :], ACT.Copy, d)
        give(b, t_hs)
        advance(conv, 9)
        b, d = bank_mm("c")
        t_c3 = tt(cpad[:, :, 2:258], ps[b][:, :].rearrange("p (t n) -> p t n", t=2),
                  hsb.rearrange("p (t n) -> p t n", t=2), ALU.mult, t_hs, d, z1)
        give(b, t_c3)
        t3 = []
        for t in range(2):
            a = ts(scv[:, t, :], cpad[:, t, 0:256], P("sc", 3 * t), None, ALU.mult, None, t_c3)
            for k in (1, 2):
                a = stt(scv[:, t, :], cpad[:, t, k:k + 256], P("sc", 3 * t + k), scv[:, t, :], ALU.mult, ALU.add, a)
            t3.append(a)
        advance(conv, 9)
        bsb, dsb = bank_mm("sb")
        advance(conv, 9)
        bp, dp = bank_tok(S["p"], 256)
        x_gone = PE.last()
        t_sc = tt(xf[:, 4:6, :], ps[bsb][:, :].rearrange("p (t n) -> p t n", t=2), scv, ALU.mult, dsb, t3, x_gone)
        give(bsb, t_sc)
        t_pv = act(pv, ps[bp][:, :].rearrange("p (t n) -> p t n", t=2), ACT.Copy, dp)
        give(bp, t_pv)
        advance(conv, 99)

        b, fr = take()
        for t in range(2):
            d = mm(ps[b][:, 0:256], C(C_ONE), cacc[:, t, :], t == 0, t == 1, conv_tok, fr, t_c, inc=(t == 1))
        t1 = tt(cacc, cacc, ps[b][:, 0:256].unsqueeze(1).to_broadcast([128, 2, 256]), ALU.subtract, d)
        give(b, t1)
        t2 = tt(csq, cacc, cacc, ALU.mult, t1)
        b, fr = take()
        for t in range(2):
            d = mm(ps[b][:, 0:256], C(C_ONE), csq[:, t, :], t == 0, t == 1, t2, fr, inc=(t == 1))
        t1 = act(sg[:, 0:256], ps[b][:, 0:256], ACT.Ln, d, bias=epsc)
        give(b, t1)
        t1 = act(sg[:, 0:256], sg[:, 0:256], ACT.Exp, t1, scale=-0.5)
        t1 = tt(cacc, cacc, sg[:, 0:256].unsqueeze(1).to_broadcast([128, 2, 256]), ALU.mult, t1)
        t2 = [act(csq[:, t, :], cacc[:, t, :], ACT.Silu, t1, scale=P("ln_g", t), bias=P("ln_b", t)) for t in range(2)]
        b, fr = take()
        for t in range(2):
            for k in range(2):
                d = mm(ps[b][:, 256 * t:256 * t + 256], wpw[:, k, 128 * t:128 * t + 128], csq[:, k, :], k == 0, k == 1,
                       t2, fr, t_pw, inc=(t == 1 and k == 1))
        t_conf = act(xf[:, 0:2, :], ps[b][:, :].rearrange("p (t n) -> p t n", t=2), ACT.Copy, d, x_gone)
        give(b, t_conf)

        t_d = []
        for t in range(2):
            b, fr = take()
            for i in range(2):
                for tb in range(2):
                    d = mm(ps[b][:, 256 * i:256 * i + 256], pv[:, tb, 128 * t:128 * t + 128], band[:, 2 * t + i, tb, :],
                           tb == 0, tb == 1, t_pv, t_bd, fr, inc=(i == 1 and tb == 1))
            for i in range(2):
                pr = slice(64 * i, 64 * i + 64)
                t_d.append(vcopy(dT[pr, t, :], ps[b][pr, 256 * i:256 * i + 256], d))
            give(b, t_d[-1])
        b, fr = take()
        for t in range(2):
            d = mm(ps[b][:, 256 * t:256 * t + 256], wpb[:, t, :], dT[:, t, :], True, True, t_d, t_wp, fr, inc=(t == 1))
        for t in range(2):
            t_pool = ts(xf[:, 6 + t, :], ps[b][:, 256 * t:256 * t + 256], P("pool_scale", t), None, ALU.mult, None, d, x_gone)
        give(b, t_pool)

        def attention(n, scores, scale, finish, Pm, PT, base):
            state = {}
            gone = {}

            def soft(i):
                b, d = state.pop(i)
                p, c = Pm[:, i % 3, :], 12 + 6 * (i % 3)
                m = []
                for q in range(2):
                    lo, hi = (0, 128) if q == 0 else (128, 384)
                    m.append(vec(lambda e, q=q, lo=lo, hi=hi: e.tensor_reduce(st[:, c + q:c + q + 1], ps[b][:, lo:hi], AX,
                                                                              ALU.max, negate=True), d, base, gone.get(i - 3)))
                s = ts(st[:, c:c + 2], st[:, c:c + 2], scale, None, ALU.mult, None, m) if scale != 1.0 else m
                x = []
                for q in range(2):
                    lo, hi = (0, 128) if q == 0 else (128, 384)
                    x.append(act(p[:, lo:hi], ps[b][:, lo:hi], ACT.Exp, s, gone.get(i - 3), base, scale=scale,
                                 bias=st[:, c + q:c + q + 1], accum_out=st[:, c + 2 + q:c + 3 + q]))
                give(b, x[-1])
                r = vec(lambda e: e.reciprocal(st[:, c + 4:c + 6], st[:, c + 2:c + 4]), x)
                return p, st[:, c + 4:c + 6], r

            for i in range(n + 2):
                if i < n:
                    b, fr = take()
                    state[i] = (b, scores(i, ps[b], [fr, base]))
                if 1 <= i <= n:
                    gone[i - 1] = finish(i - 1, *soft(i - 1))

        def norm_p(p, r, tok):
            a = ts(p[:, 0:128], p[:, 0:128], r[:, 0:1], None, ALU.mult, None, tok)
            return ts(p[:, 128:384], p[:, 128:384], r[:, 1:2], None, ALU.mult, None, a, tok)

        def turn(p, o, tok, *w):
            b, fr = take()
            for j in range(3):
                d = pe(lambda e, j=j: e.transpose(ps[b][:, 128 * j:128 * j + 128], p[:, 128 * j:128 * j + 128], C(C_ID)),
                       tok, fr, inc=(j == 2))
            t = act(o, ps[b][:, 0:384], ACT.Copy, d, *w)
            give(b, t)
            return d, t

        def logits(o, qh, kh, fr, w, extra=None):
            for q in range(2):
                lo, n = (0, 128) if q == 0 else (128, 256)
                mm(o[:, lo:lo + n], qh[:, 128 * q:128 * q + 128], kh[:, 0:n], True, False, fr, w)
                if extra:
                    mm(o[:, lo:lo + n], extra[0][:, 128 * q:128 * q + 128], extra[1][:, 0:n], False, False, extra[2])
                d = mm(o[:, lo + n - 128:lo + n], idb[:, :], mab[:, :], False, True, t_m, inc=(q == 1))
            return d

        fo_pv, fo_rk = [], [None]

        def fo_scores(i, o, fr):
            t = ts(rk, NCt, P("fsel", i), None, ALU.mult, None, t_cq, fo_rk[0])
            fo_rk[0] = logits(o, qm[:, i, :], kT[:, i // 2, :], fr, [t_q, t_k], (CQ, rk, [t, t_cq]))
            return fo_rk[0]

        def fo_finish(i, p, r, tok):
            n = norm_p(p, r, tok)
            o = PT[:, i % 2, :]
            d, t = turn(p, o, n, fo_pv[-2:-1])
            b, fr = take()
            c = slice(128 * (i // 2), 128 * (i // 2) + 128)
            mm(ps[b][:, 0:128], vs[:, 0, c], o[:, 0:128], True, True, t, t_v, fr)
            mm(ps[b][:, 128:256], vs[:, 0, c], o[:, 128:256], True, False)
            e = mm(ps[b][:, 128:256], vs[:, 1, c], o[:, 256:384], False, True, inc=True)
            fo_pv.append(e)
            pr = slice(64 * (i % 2), 64 * (i % 2) + 64)
            x = act(xf[pr, 2 + i // 2, :], ps[b][pr, 0:256], ACT.Copy, e, x_gone)
            give(b, x)
            return [d, x]

        attention(4, fo_scores, 1.0, fo_finish, Pm, PT, None)
        t_x = hilo(0, 8, [bar()])
        bk, d = proj_out(S["out"], t_x)
        for tb in range(2):
            ends, e = add_norm([ps[bk[tb][c][0]][:, :] for c in range(2)], rows[:, 0, :], t_r0, tb, d, bar())
            for c in range(2):
                give(bk[tb][c][0], ends[c])

        t_r0 = dma("row0", rows[:, 0, :], D["g_ple_post"].partition_broadcast(128), bar(), q=GP)

        def ffn(sl, gain, gated):
            b0 = bar()
            t_x = norm_t(gain, b0)
            rb = SC[:, 0:1024].rearrange("p (a b) -> p a b", a=2)
            fb = SC[:, 1024:2048].rearrange("p (a b) -> p a b", a=2)
            bk = [[take() for _ in range(2)] for _ in range(2)]
            fr = [x[1] for y in bk for x in y]
            n = len(sl)
            dn, rd = {}, {}
            for j in range(n + 1):
                if j < n:
                    p = j % 2
                    b, f1 = take()
                    d = feat_mm(sl[j][0], ps[b], t_x, f1)
                    if gated:
                        b2, f2 = take()
                        d2 = feat_mm(sl[j][1], ps[b2], t_x, f2)
                        r = act(rb[:, p, :], ps[b][:, :], ACT.Silu, d, b0, rd.get(j - 2))
                        give(b, r)
                        f = tt(fb[:, p, :], ps[b2][:, :], rb[:, p, :], ALU.mult, r, d2, b0, rd.get(j - 2))
                        give(b2, f)
                    else:
                        r = act(rb[:, p, :], ps[b][:, :], ACT.Relu, d, b0, rd.get(j - 2))
                        f = stt(fb[:, p, :], ps[b][:, :], 0.0, rb[:, p, :], ALU.max, ALU.mult, r, b0, rd.get(j - 2))
                        give(b, f)
                    a = act(fh[:, p, :], fb[:, p, :], ACT.Copy, f, dn.get(j - 2))
                    l = tt(fl[:, p, :], fb[:, p, :], fh[:, p, :].bitcast(F32), ALU.subtract, a, f, dn.get(j - 2))
                    rd[j] = [a, l]
                if j >= 1:
                    i = j - 1
                    v = [x[:, i % 2, :].rearrange("p (k n) -> p k n", k=2) for x in (fh, fl)]
                    dn[i] = tok_mm(sl[i][-1], [[(ps[bk[tb][c][0]][:, :], slice(512 * c, 512 * c + 512))
                                                for c in range(2)] for tb in range(2)],
                                   rd[i], fr, first=(i == 0), final=(i == n - 1), a=v)
            return bk, dn[n - 1]

        bk, d = ffn(S["ff"], P("g_mlp_pre", 0, 8), False)
        for tb in range(2):
            ends, e = add_norm([ps[bk[tb][c][0]][:, :] for c in range(2)], rows[:, 1, :], t_r1, tb, d, bar())
            for c in range(2):
                give(bk[tb][c][0], ends[c])

        t_r1 = dma("row1", rows[:, 1, :], D["norm_final_2"].partition_broadcast(128), bar(), q=GP)
        b0 = bar()
        pT = SC[:, 0:512].rearrange("p (k n) -> p k n", k=2)
        e0 = SC[:, 512:1536]
        sgm = SC[:, 1536:2560]
        t_pT = dma("pT", pT, D["pT"].rearrange("(k p) n -> p k n", p=128), b0, q=GP)
        ph, pl = (x[:, 0, :].rearrange("p (k n) -> p k n", k=2) for x in (fh, fl))
        a = act(ph, pT, ACT.Copy, t_pT, b0)
        l = tt(pl, pT, ph.bitcast(F32), ALU.subtract, a)
        bkp = [[take() for _ in range(2)] for _ in range(2)]
        dp = tok_mm(S["proj"], [[(ps[bkp[tb][c][0]][:, :], slice(512 * c, 512 * c + 512)) for c in range(2)]
                                for tb in range(2)], [a, l], [x[1] for y in bkp for x in y], a=(ph, pl))
        es = SC[:, 2560:2560 + 2048].rearrange("p (a b) -> p a b", a=2)
        t_es = [vcopy(es[:, tb, 512 * c:512 * c + 512], ps[bkp[tb][c][0]][:, :], dp, b0) for tb in range(2) for c in range(2)]
        for i, (tb, c) in enumerate(((0, 0), (0, 1), (1, 0), (1, 1))):
            give(bkp[tb][c][0], t_es[i])
        t_x = norm_t(P("g_ple_pre", 0, 8), b0)
        bk, d = proj_out(S["gate"], t_x)
        for tb in range(2):
            for c in range(2):
                cc = slice(512 * c, 512 * c + 512)
                a = act(sgm[:, cc], ps[bk[tb][c][0]][:, :], ACT.Sigmoid, d, bar())
                give(bk[tb][c][0], a)
                m = tt(e0[:, cc], es[:, tb, cc], sgm[:, cc], ALU.mult, a, t_es)
            add_norm([e0[:, 0:512], e0[:, 512:1024]], rows[:, 0, :], t_r0, tb, m, bar())

        t_x = norm_t(P("nm0", 0, 8), bar())
        b0 = bar()
        sc = Scratch()
        dqm = sc(8, 256)
        dkT = sc(4, 256)
        dvs = sc(2, 512)
        roped = sc(2, 2, 512)
        cqs = sc(2, 384)
        cks = sc(2, 256)
        krs = sc(2, 32)
        tmp = sc(4, 256)
        Pm = sc(3, 384)
        PT = sc(2, 384)
        lam = sc(64)

        z2 = pool(lambda e: e.memset(dqm, 0.0), b0)

        def wide(sl, kt=4):
            bk = [take() for _ in range(2)]
            for i in range(2):
                d = tok_mm(sl[i], [[(ps[bk[tb][0]][:, :], slice(0, 512))] for tb in range(2)], t_x,
                           [x[1] for x in bk], k0=4 * i, first=(i == 0), final=(i == 1))
            return bk, d

        def rope(dst, src, tb, nh, half, at, d, *w):
            n = nh * half
            co = cst[:, at + 96 * tb:at + 96 * tb + half].unsqueeze(1).to_broadcast([128, nh, half])
            si = cst[:, at + 96 * tb + half:at + 96 * tb + 2 * half].unsqueeze(1).to_broadcast([128, nh, half])
            x1, x2 = src[:, :, 0:half], src[:, :, half:2 * half]
            u = [tmp[:, i, 0:n].rearrange("p (a b) -> p a b", a=nh) for i in range(4)]
            b = bar()
            a = [tt(u[0], x1, co, ALU.mult, d, b), tt(u[1], x2, si, ALU.mult, d), tt(u[2], x2, co, ALU.mult, d),
                 tt(u[3], x1, si, ALU.mult, d)]
            return [a, tt(dst[:, :, 0:half], u[0], u[1], ALU.subtract, a, *w),
                    tt(dst[:, :, half:2 * half], u[2], u[3], ALU.add, a, *w)]

        t_rp = []
        for j, n in enumerate(("dq", "dk")):
            bk, d = wide(S[n])
            for tb in range(2):
                r = rope(roped[:, j, tb, :].rearrange("p (a b) -> p a b", a=8),
                         ps[bk[tb][0]][:, :].rearrange("p (a b) -> p a b", a=8), tb, 8, 32, C_ROPE + 32, d, b0)
                give(bk[tb][0], r[0][-1])
                t_rp.append(r)
        bk, d = wide(S["dv"])
        t_dv = []
        for tb in range(2):
            t_dv.append(act(dvs[:, tb, :], ps[bk[tb][0]][:, :], ACT.Copy, d, b0))
            give(bk[tb][0], t_dv[-1])
        t_cq = []
        for i, (sl, o, n) in enumerate(((S["cq"][0], cqs[:, :, 0:256], 256), (S["cq"][1], cqs[:, :, 256:384], 128),
                                        (S["ckv"], cks, 256), (S["kr"], krs, 32))):
            b, d = bank_tok(sl, n)
            t_cq.append(act(o, ps[b][:, :].rearrange("p (t n) -> p t n", t=2)[:, :, 0:n], ACT.Copy, d, b0))
            give(b, t_cq[-1])
        x_gone = PE.last()
        krr = hs[:, 0:64].rearrange("p (t n) -> p t n", t=2)
        t_kr = [rope(krr[:, tb, :].unsqueeze(1), krs[:, tb, :].unsqueeze(1), tb, 1, 16, C_ROPE, t_cq[3], bar())
                for tb in range(2)]
        t_dq, t_dk = [], []
        for j in range(2):
            for tb in range(2):
                b, fr = take()
                for k in range(4):
                    d = pe(lambda e, j=j, tb=tb, k=k, b=b: e.transpose(ps[b][:, 128 * k:128 * k + 128],
                                                                       roped[:, j, tb, 128 * k:128 * k + 128], C(C_ID)),
                           t_rp, fr, inc=(k == 3))
                s = slice(128 * tb, 128 * tb + 128)
                v = ps[b][:, :].rearrange("p (k n) -> p k n", k=4)
                if j == 0:
                    for i in range(2):
                        pr = slice(64 * i, 64 * i + 64)
                        t_dq.append(act(dqm.rearrange("p (k i) n -> p k i n", i=2)[pr, :, i, s], v[pr], ACT.Copy, d, z2))
                    give(b, t_dq[-1])
                else:
                    t_dk.append(act(dkT[:, :, s], v, ACT.Copy, d, b0))
                    give(b, t_dk[-1])

        t_n = []
        for tb in range(2):
            for i, (src, n) in enumerate(((cqs, 384), (cks, 256))):
                c = 36 + 4 * tb + 2 * i
                q = act(junk[:, 0:n], src[:, tb, :], ACT.Square, t_cq, b0, accum_out=st[:, c:c + 1])
                r = rstd(st[:, c + 1:c + 2], st[:, c:c + 1], n, q)
                m = ts(src[:, tb, :], src[:, tb, :], st[:, c + 1:c + 2], None, ALU.mult, None, r, q)
                t_n.append(to_xf(src[:, tb, :], n // 128, 0 if i == 0 else 3, tb, P("qn", 0, 3) if i == 0 else P("kvn", 0, 2),
                                 m, x_gone, bar()))
        t_lat = hilo(0, 5, t_n, x_gone)
        lat_gone = bar()

        la = []
        for i in range(2):
            a = tt(lam[:, 0:64], srow[:, 8 + 128 * i:72 + 128 * i], srow[:, 72 + 128 * i:136 + 128 * i], ALU.mult, t_sr, b0, la)
            r = vec(lambda e, i=i: e.tensor_reduce(st[:, 48 + i:49 + i], lam[:, 0:64], AX, ALU.add), a)
            la = [r]
        a = act(st[:, 50:52], st[:, 48:50], ACT.Exp, la)
        a = tt(st[:, 52:53], st[:, 50:51], st[:, 51:52], ALU.subtract, a)
        a = ts(st[:, 52:53], st[:, 52:53], LAMBDA0, None, ALU.add, None, a)
        b_ = act(st[:, 53:54], st[:, 52:53], ACT.Abs, a)
        b_ = ts(st[:, 53:54], st[:, 53:54], 1.0, None, ALU.max, None, b_)
        b_ = vec(lambda e: e.reciprocal(st[:, 54:55], st[:, 53:54]), b_)
        b_ = stt(st[:, 55:56], st[:, 52:53], -1.0, st[:, 54:55], ALU.mult, ALU.mult, b_)
        t_lam = stt(st[:, 56:57], st[:, 54:55], EPS, st[:, 54:55], ALU.mult, ALU.mult, b_)

        D0 = {}
        df_pv = []
        df_o = []

        def df_scores(i, o, fr):
            return logits(o, dqm[:, i, :], dkT[:, i // 2, :], fr, [t_dq, t_dk])

        def df_finish(i, p, r, tok):
            f = 54 + i % 2
            s = ts(r, r, st[:, f:f + 1], None, ALU.mult, None, tok, t_lam)
            n = norm_p(p, r, s)
            if i % 2 == 0:
                D0[i] = (p, n)
                return None
            p0, n0 = D0.pop(i - 1)
            n = tt(p, p, p0, ALU.add, n, n0)
            g = i // 2
            o = PT[:, g % 2, :]
            d, t = turn(p, o, n, df_pv[-2:-1])
            b, fr = take()
            c = slice(128 * g, 128 * g + 128)
            mm(ps[b][:, 0:128], o[:, 0:128], dvs[:, 0, c], True, True, t, t_dv, fr)
            mm(ps[b][:, 128:256], o[:, 128:256], dvs[:, 0, c], True, False)
            e = mm(ps[b][:, 128:256], o[:, 256:384], dvs[:, 1, c], False, True, inc=True)
            df_pv.append(e)
            w = bar()
            on = roped[:, g % 2, 0, 0:256]
            q = [act(junk[:, 128 * tb:128 * tb + 128], ps[b][:, 128 * tb:128 * tb + 128], ACT.Square, e, w,
                     accum_out=st[:, 57 + tb:58 + tb]) for tb in range(2)]
            y = act(st[:, 59:61], st[:, 57:59], ACT.Ln, q, t_lam, scale=1.0 / 128, bias=st[:, 56:57])
            y = act(st[:, 59:61], st[:, 59:61], ACT.Exp, y, scale=-0.5)
            m = [ts(on[:, 128 * tb:128 * tb + 128], ps[b][:, 128 * tb:128 * tb + 128], st[:, 59 + tb:60 + tb], 1.0 - LAMBDA0,
                    ALU.mult, ALU.mult, y, w) for tb in range(2)]
            give(b, m)
            for tb in range(2):
                df_o.append(to_xf(on[:, 128 * tb:128 * tb + 128], 1, 4 + g, tb, P("subln"), m, lat_gone, t_lat))
            return [d, n]

        attention(8, df_scores, 0.125, df_finish, Pm, PT, b0)

        b0 = bar()
        sc = Scratch()
        qf = sc(2, 768)
        kf = sc(2, 768)
        vm = sc(2, 512)
        qT = sc(8, 256)
        kT2 = sc(8, 256)
        tmp = sc(4, 256)
        Pm = sc(3, 384)
        PT = sc(2, 384)
        t_qf = []
        bq = [[take() for _ in range(2)] for _ in range(2)]
        fr = [x[1] for y in bq for x in y]
        for i in range(2):
            d = tok_mm(S["uq"][i], [[(ps[bq[tb][i][0]][:, 0:384], slice(0, 384))] for tb in range(2)], t_lat, fr)
            for tb in range(2):
                v = ps[bq[tb][i][0]][:, 0:384].rearrange("p (a b) -> p a b", a=4)
                o = qf[:, tb, 384 * i:384 * i + 384].rearrange("p (a b) -> p a b", a=4)
                a = act(o[:, :, 0:64], v[:, :, 0:64], ACT.Copy, d, b0)
                r = rope(o[:, :, 64:96], v[:, :, 64:96], tb, 4, 16, C_ROPE, [d, a], b0)
                give(bq[tb][i][0], r[0][-1])
                t_qf.append([a, r])
        wH, wL, tok = use(S["ukv"])
        bkk = [take() for _ in range(2)]
        bvv = [take() for _ in range(2)]
        fr = [x[1] for x in bkk + bvv]
        for tb in range(2):
            s = slice(128 * tb, 128 * tb + 128)
            for o, c in ((ps[bkk[tb][0]], 0), (ps[bvv[tb][0]], 64)):
                for k in range(2):
                    sel = [x[:, k, :].rearrange("p (a b) -> p a b", a=8)[:, :, c:c + 64] for x in (wH, wL)]
                    d = mm3(o[:, :].rearrange("p (a b) -> p a b", a=8), xh[:, 3 + k, s], xl[:, 3 + k, s], sel[0], sel[1],
                            k == 0, k == 1, tok, t_lat, fr, inc=(tb == 1 and c == 64 and k == 1))
        used[S["ukv"]] = d
        lat_done = PE.last()
        t_kf, t_vm = [], []
        for tb in range(2):
            kv = kf[:, tb, :].rearrange("p (a b) -> p a b", a=8)
            a = act(kv[:, :, 0:64], ps[bkk[tb][0]][:, :].rearrange("p (a b) -> p a b", a=8), ACT.Copy, d, b0)
            give(bkk[tb][0], a)
            v = act(vm[:, tb, :], ps[bvv[tb][0]][:, :], ACT.Copy, d, b0)
            give(bvv[tb][0], v)
            t_vm.append(v)
            t_kf.append(a)
        for tb in range(2):
            kv = kf[:, tb, :].rearrange("p (a b) -> p a b", a=8)
            t_kf.append(vcopy(kv[:, :, 64:96], krr[:, tb, :].unsqueeze(1).to_broadcast([128, 8, 32]), t_kr, b0))
        t_qT = []
        for src, dst, tk in ((qf, qT, t_qf), (kf, kT2, t_kf)):
            for tb in range(2):
                for c in range(2):
                    b, fr = take()
                    for k in range(4):
                        hd = 4 * c + k
                        d = pe(lambda e, src=src, tb=tb, hd=hd, k=k, b=b: e.transpose(
                            ps[b][0:96, 128 * k:128 * k + 128], src[:, tb, 96 * hd:96 * hd + 96], C(C_ID)),
                            tk, fr, inc=(k == 3))
                    a = act(dst[0:96, 4 * c:4 * c + 4, 128 * tb:128 * tb + 128],
                            ps[b][0:96, :].rearrange("p (k n) -> p k n", k=4), ACT.Copy, d, b0)
                    give(b, a)
                    t_qT.append(a)

        ml_pv = []

        def ml_scores(i, o, fr):
            return logits(o, qT[0:96, i, :], kT2[0:96, i, :], fr, t_qT)

        def ml_finish(i, p, r, tok):
            n = norm_p(p, r, tok)
            o = PT[:, i % 2, :]
            d, t = turn(p, o, n, ml_pv[-2:-1], b0)
            b, fr = take()
            c = slice(128 * (i // 2), 128 * (i // 2) + 128)
            mm(ps[b][:, 0:128], vm[:, 0, c], o[:, 0:128], True, True, t, t_vm, fr)
            mm(ps[b][:, 128:256], vm[:, 0, c], o[:, 128:256], True, False)
            e = mm(ps[b][:, 128:256], vm[:, 1, c], o[:, 256:384], False, True, inc=True)
            ml_pv.append(e)
            pr = slice(64 * (i % 2), 64 * (i % 2) + 64)
            x = act(xf[pr, i // 2, :], ps[b][pr, 0:256], ACT.Copy, e, lat_gone)
            give(b, x)
            return [d, x]

        attention(8, ml_scores, 96.0 ** -0.5, ml_finish, Pm, PT, b0)
        t_x = hilo(0, 8, bar())
        bk, d = proj_out(S["aout"], t_x)
        add_banks(bk, d)
        bk, d = ffn(S["f0"], P("nf0", 0, 8), True)
        add_banks(bk, d)

        t_x = norm_t(P("nm1", 0, 8), bar())
        b0 = bar()
        sc = Scratch()
        xp = sc(8, 259)
        xb = sc(8, 256)
        xs = sc(2, 512)
        sz = sc(2, 512)
        cbs = sc(2, 384)
        Eb = sc(2, 384)
        Mb = sc(2, 384)
        At = sc(2, 40)
        dr = sc(4, 256)
        T2 = sc(256)
        y = sc(2, 512)
        wdt = sc(8, 8)
        z3 = [pool(lambda e: e.memset(xp[:, :, 0:3], 0.0), b0), pool(lambda e: e.memset(T2, 0.0), b0)]
        t_wd = dma("wdt", wdt, sw[:, 1536:1544].rearrange("(k p) n -> p k n", p=128), b0, q=GP)

        bk, d = wide(S["z"])
        t_sz = []
        for tb in range(2):
            t_sz.append(act(sz[:, tb, :], ps[bk[tb][0]][:, :], ACT.Silu, d, b0))
            give(bk[tb][0], t_sz[-1])
        b, fr = take()
        for k in range(8):
            d = mm(ps[b][0:8, 0:256], wdt[:, k, :], xf[:, k, :], k == 0, k == 7, t_wd, t_x, fr, inc=(k == 7))
        R = slice(0, 8)
        t1 = ts(dr[R, 0, :], ps[b][R, 0:256], P("dtb")[R], None, ALU.add, None, d, b0)
        give(b, t1)
        t_dt = softplus(dr[R, 0, :], dr[R, 1, :], dr[R, 2, :], dr[R, 3, :], junk[R, 0:256], t1, bar())
        t1 = act(st[R, 61:62], P("alog")[R], ACT.Exp, b0)
        t1 = ts(dr[R, 1, :], dr[R, 0, :], st[R, 61:62], -1.0, ALU.mult, ALU.mult, t1, t_dt)
        t2 = vec(lambda e: e.memset(dr[R, 2, :], 1.0), t_dt)
        t_A = [vec(lambda e: e.tensor_tensor_scan(T2[R, :], dr[R, 2, :], dr[R, 1, :], 0.0, ALU.mult, ALU.add), t1, t2, z3),
               vcopy(T2[32:40, :], dr[R, 0, :], t_dt, z3)]
        t_xb = []
        for i in range(4):
            b, d = bank_feat(S["xbc"][i], t_x)
            a = act(xp[:, 2 * i:2 * i + 2, 3:259], ps[b][:, :].rearrange("p (t n) -> p t n", t=2), ACT.Copy, d, z3)
            give(b, a)
            for t in (2 * i, 2 * i + 1):
                c = ts(xb[:, t, :], xp[:, t, 0:256], P("cw", 4 * t), None, ALU.mult, None, a, b0)
                for k in (1, 2, 3):
                    c = stt(xb[:, t, :], xp[:, t, k:k + 256], P("cw", 4 * t + k), xb[:, t, :], ALU.mult, ALU.add, c)
                t_xb.append(act(xb[:, t, :], xb[:, t, :], ACT.Silu, c, bias=P("cb", t)))
        t_at, t_xs = [], []
        for tb in range(2):
            b, fr = take()
            s = slice(128 * tb, 128 * tb + 128)
            d = pe(lambda e, b=b, s=s: e.transpose(ps[b][:, 0:128], T2[:, s], C(C_ID)), t_A, fr)
            a = ts(At[:, tb, 0:8], ps[b][:, 0:8], -1.0, None, ALU.mult, None, d, b0)
            a = vcopy(At[:, tb, 32:40], ps[b][:, 32:40], d)
            give(b, a)
            t_at.append(a)
            b, fr = take()
            for k in range(4):
                d = pe(lambda e, b=b, s=s, k=k: e.transpose(ps[b][:, 128 * k:128 * k + 128], xb[:, k, s], C(C_ID)),
                       t_xb, fr, inc=(k == 3))
            a = act(xs[:, tb, :], ps[b][:, :], ACT.Copy, d, b0)
            give(b, a)
            t_xs.append(a)
        t_cb = []
        for g in range(2):
            b, fr = take()
            mm(ps[b][:, 0:256], xb[:, 4 + g, 0:128], xb[:, 6 + g, :], True, True, t_xb, fr)
            d = mm(ps[b][:, 256:384], xb[:, 4 + g, 128:256], xb[:, 6 + g, 128:256], True, True, inc=True)
            a = act(cbs[:, g, :], ps[b][:, 0:384], ACT.Copy, d, b0)
            give(b, a)
            t_cb.append(a)
        by = [take() for _ in range(2)]
        fry = [x[1] for x in by]
        seg, m_gone = {}, {}

        def ssd_seg(i):
            b, fr = take()
            sel = cst[:, C_SEL + 128 * i:C_SEL + 128 * i + 128]
            o = ps[b]
            mm(o[:, 0:256], sel, T2, True, False, t_A, fr)
            mm(o[:, 0:128], idb[:, :], mtb[:, :], False, True, t_m)
            mm(o[:, 256:384], sel, T2[:, 128:256], True, False)
            d = mm(o[:, 256:384], idb[:, :], mtb[:, :], False, True, inc=True)
            a = [act(Eb[:, i % 2, 0:256], o[:, 0:256], ACT.Exp, d, t_at, b0, m_gone.get(i - 2), bias=At[:, 0, i:i + 1]),
                 act(Eb[:, i % 2, 256:384], o[:, 256:384], ACT.Exp, bias=At[:, 1, i:i + 1])]
            give(b, a[-1])
            return a

        def ssd_out(i, a):
            e, m, g = Eb[:, i % 2, :], Mb[:, i % 2, :], i // 4
            k = [stt(m[:, 0:256], e[:, 0:256], At[:, 0, 32 + i:33 + i], cbs[:, g, 0:256], ALU.mult, ALU.mult, a, t_cb, t_at,
                     m_gone.get(i - 2)),
                 stt(m[:, 256:384], e[:, 256:384], At[:, 1, 32 + i:33 + i], cbs[:, g, 256:384], ALU.mult, ALU.mult, a)]
            c = slice(64 * i, 64 * i + 64)
            mm(ps[by[0][0]][:, c], m[:, 0:128], xs[:, 0, c], True, True, k, t_xs, fry)
            mm(ps[by[1][0]][:, c], m[:, 128:256], xs[:, 0, c], True, False)
            d = mm(ps[by[1][0]][:, c], m[:, 256:384], xs[:, 1, c], False, True, inc=True)
            m_gone[i] = [k, d]
            return d

        for i in range(9):
            if i < 8:
                seg[i] = ssd_seg(i)
            if i >= 1:
                d = ssd_out(i - 1, seg.pop(i - 1))
        x_used = bar()
        for tb in range(2):
            yt = y[:, tb, :]
            a = tt(yt.rearrange("p (a b) -> p a b", a=8), xs[:, tb, :].rearrange("p (a b) -> p a b", a=8),
                   srow[:, 0:8].unsqueeze(2).to_broadcast([128, 8, 64]), ALU.mult, t_xs, t_sr, b0)
            a = tt(yt, yt, ps[by[tb][0]][:, :], ALU.add, a, d)
            give(by[tb][0], a)
            a = tt(yt, yt, sz[:, tb, :], ALU.mult, a, t_sz)
            q = [act(junk[:, 256 * g:256 * g + 256], yt[:, 256 * g:256 * g + 256], ACT.Square, a, x_used,
                     accum_out=st[:, 2 * tb + g:2 * tb + g + 1]) for g in range(2)]
            r = rstd(st[:, 4 + 2 * tb:6 + 2 * tb], st[:, 2 * tb:2 * tb + 2], 256, q)
            a = tt(yt.rearrange("p (a b) -> p a b", a=2), yt.rearrange("p (a b) -> p a b", a=2),
                   st[:, 4 + 2 * tb:6 + 2 * tb].unsqueeze(2).to_broadcast([128, 2, 256]), ALU.mult, r)
            t_y = to_xf(yt, 4, 0, tb, P("s_norm", 0, 4), a, x_used)

        b0 = bar()
        sc = Scratch()
        hq = sc(4, 256)
        hk = sc(4, 256)
        G = sc(4, 256)
        hiv = sc(2, 512)
        shg = sc(2, 512)
        Dd = sc(4, 256)
        QK = sc(2, 1024)
        STt = sc(8, 128)
        tm = sc(8, 128)
        ST2 = sc(4, 128)
        ov = sc(2, 512)
        hm = sc(8, 128)
        t_hm = dma("hm", hm, D["hmask"], b0, q=GP)
        lb = tt(st[:, 12:16], P("lb1", 0, 4), P("lb0", 0, 4), ALU.subtract, b0)
        lb = act(st[:, 8:12], st[:, 12:16], ACT.Sigmoid, lb, b0)
        lb = [lb, act(st[:, 16:20], st[:, 12:16], ACT.Sigmoid, lb, scale=-1.0)]
        t_hq, t_hf = [], []
        for i in range(2):
            b, d = bank_feat(S["hq"][i], t_x)
            t_hq.append(act(hq[:, 2 * i:2 * i + 2, :], ps[b][:, :].rearrange("p (t n) -> p t n", t=2), ACT.Silu, d, b0))
            give(b, t_hq[-1])
        for i in range(2):
            b, d = bank_feat(S["hf"][i], t_x)
            v = ps[b][:, :].rearrange("p (t n) -> p t n", t=2)
            a = act(G[:, 2 * i:2 * i + 2, :], v, ACT.Sigmoid, d, b0)
            a2 = act(hk[:, 2 * i:2 * i + 2, :], v, ACT.Sigmoid, d, b0, scale=-1.0)
            give(b, a2)
            for t in (2 * i, 2 * i + 1):
                t_hf.append(ts(G[:, t, :], G[:, t, :], st[:, 16 + t:17 + t], st[:, 8 + t:9 + t], ALU.mult, ALU.add, a, lb))
                t_hf.append(ts(hk[:, t, :], hk[:, t, :], st[:, 16 + t:17 + t], None, ALU.mult, None, a2, lb))
        bk, d = wide(S["hi"])
        t_hi = []
        for tb in range(2):
            t_hi.append(act(hiv[:, tb, :], ps[bk[tb][0]][:, :], ACT.Copy, d, b0))
            give(bk[tb][0], t_hi[-1])
        bk, d = wide(S["hg"])
        t_hg = []
        for tb in range(2):
            t_hg.append(act(shg[:, tb, :], ps[bk[tb][0]][:, :], ACT.Silu, d, b0))
            give(bk[tb][0], t_hg[-1])
        x_gone = PE.last()
        a = ts(G, G, 1e-18, None, ALU.max, None, t_hf)
        a = act(Dd, G, ACT.Ln, a, b0)
        o1 = vec(lambda e: e.memset(tm.rearrange("p a b -> p (a b)")[:, 0:256], 1.0), b0)
        t_G = [vec(lambda e, t=t: e.tensor_tensor_scan(G[:, t, :], tm.rearrange("p a b -> p (a b)")[:, 0:256], Dd[:, t, :],
                                                       0.0, ALU.mult, ALU.add), a, o1) for t in range(4)]
        qk_gone = {}
        qk_free = [None, None]
        Gf, Df, qf_, kf_ = (x.rearrange("p a b -> p (a b)") for x in (G, Dd, hq, hk))
        d_gone = [t_G]
        acc = None
        t_s2 = None
        for n, m in enumerate([128] + LEVELS + [0]):
            if m:
                nb = 1024 // (2 * m)
                g3, d3, q3, k3 = (x.rearrange("p (b m) -> p b m", m=2 * m) for x in (Gf, Df, qf_, kf_))
                o = QK[:, n % 2, :]
                o3 = o.rearrange("p (b m) -> p b m", m=2 * m)
                ref = g3[:, :, m - 1:m].to_broadcast([128, nb, m])
                a = [tt(d3[:, :, 0:m], ref, g3[:, :, 0:m], ALU.subtract, t_G, d_gone),
                     tt(d3[:, :, m:2 * m], g3[:, :, m:2 * m], ref, ALU.subtract, t_G, d_gone)]
                x = act(Df, Df, ACT.Exp, a)
                k = [tt(o3[:, :, 0:m], k3[:, :, 0:m], d3[:, :, 0:m], ALU.mult, x, t_hf, qk_free[n % 2], b0),
                     tt(o3[:, :, m:2 * m], q3[:, :, m:2 * m], d3[:, :, m:2 * m], ALU.mult, x, t_hq)]
                d_gone = k
                s_, l_ = o.rearrange("p (h n) -> p h n", h=4), o.rearrange("p (h n) -> p h n", h=4)
            else:
                s_, l_, k = hk, hq, [t_hq, t_hf]
            if m == 128:
                b, fr = take()
                for hd in range(4):
                    d = mm(ps[b][:, 128 * hd:128 * hd + 128], s_[:, hd, 0:128], l_[:, hd, 128:256], True, True, k, fr,
                           inc=(hd == 3))
                t_s2 = act(ST2, ps[b][:, :].rearrange("p (h n) -> p h n", h=4), ACT.Copy, d, b0)
                give(b, t_s2)
                qk_free[n % 2] = d
                continue
            for tb in range(2):
                b, fr = take()
                c = slice(128 * tb, 128 * tb + 128)
                for hd in range(4):
                    d = mm(ps[b][:, 128 * hd:128 * hd + 128], s_[:, hd, c], l_[:, hd, c], True, True, k, fr, inc=(hd == 3))
                v = ps[b][:, :].rearrange("p (h n) -> p h n", h=4)
                mk = hm[:, n - 1, :].unsqueeze(1).to_broadcast([128, 4, 128])
                z = slice(4 * tb, 4 * tb + 4)
                if n == 1:
                    acc_n = tt(STt[:, z, :], v, mk, ALU.mult, d, t_hm, b0)
                    give(b, acc_n)
                else:
                    a = tt(tm[:, z, :], v, mk, ALU.mult, d, t_hm, t_G, acc)
                    give(b, a)
                    acc_n = tt(STt[:, z, :], STt[:, z, :], tm[:, z, :], ALU.add, a, acc)
                acc = [acc, acc_n]
            acc = acc_n
            qk_free[n % 2] = d
        bo = [take() for _ in range(2)]
        fro = [x[1] for x in bo]
        for hd in range(4):
            c = slice(128 * hd, 128 * hd + 128)
            mm(ps[bo[0][0]][:, c], STt[:, hd, :], hiv[:, 0, c], True, True, acc, t_hi, fro, t_s2)
            mm(ps[bo[1][0]][:, c], ST2[:, hd, :], hiv[:, 0, c], True, False)
            d = mm(ps[bo[1][0]][:, c], STt[:, 4 + hd, :], hiv[:, 1, c], False, True, inc=True)
        w = bar()
        for tb in range(2):
            v = ps[bo[tb][0]][:, :]
            q = act(ov[:, tb, :], v, ACT.Square, d, b0)
            r = vec(lambda e, tb=tb: e.tensor_reduce(st[:, 20 + 4 * tb:24 + 4 * tb],
                                                     ov[:, tb, :].rearrange("p (a b) -> p a b", a=4), AX, ALU.add), q, w)
            r = rstd(st[:, 28 + 4 * tb:32 + 4 * tb], st[:, 20 + 4 * tb:24 + 4 * tb], 128, r, w)
            a = tt(ov[:, tb, :].rearrange("p (a b) -> p a b", a=4), v.rearrange("p (a b) -> p a b", a=4),
                   st[:, 28 + 4 * tb:32 + 4 * tb].unsqueeze(2).to_broadcast([128, 4, 128]), ALU.mult, r)
            give(bo[tb][0], a)
            a = tt(ov[:, tb, :], ov[:, tb, :], shg[:, tb, :], ALU.mult, a, t_hg)
            t_o = to_xf(ov[:, tb, :], 4, 4, tb, P("g_norm"), a, w)
        t_x = hilo(0, 8, bar())
        bk, d = proj_out(S["sout"], t_x)
        add_banks(bk, d)
        bk, d = ffn(S["f1"], P("nf1", 0, 8), True)
        t_f = add_banks(bk, d)

        w = bar()
        t_out = []
        for tb in range(2):
            q = act(junk[:, :], h[:, tb, :], ACT.Square, w, accum_out=st[:, tb:tb + 1])
            r = rstd(st[:, 2 + tb:3 + tb], st[:, tb:tb + 1], 1024, q)
            o = SC[:, 4096 + 1024 * tb:5120 + 1024 * tb]
            m = stt(o, h[:, tb, :], st[:, 2 + tb:3 + tb], rows[:, 1, :], ALU.mult, ALU.mult, r, t_r1, w)
            t_out.append(dma(f"out{tb}", out[128 * tb:128 * tb + 128, :], o, m))
        assert len(used) == len(slots), (len(used), len(slots))

        block = ctx.enter_context(nc.Block())

        @block.sync
        def _(eng):
            SP.replay(eng)
            for s, c in t_out:
                eng.wait_ge(s, c)

        @block.tensor
        def _(eng):
            PE.replay(eng)

        @block.scalar
        def _(eng):
            AC.replay(eng)

        @block.vector
        def _(eng):
            VE.replay(eng)

        @block.gpsimd
        def _(eng):
            GP.replay(eng)


def constants():
    f = np.float32
    i = np.arange(128)
    c = np.zeros((128, C_N), f)
    c[:, C_ID:C_ID + 128] = np.eye(128, dtype=f)
    c[:, C_MA:C_MA + 128] = np.where(i[None, :] > i[:, None], f(NEG), f(0))
    c[:, C_MT:C_MT + 128] = np.where(i[None, :] < i[:, None], f(NEG), f(0))
    c[:, C_ONE:C_ONE + 128] = f(1.0 / 256)
    for n in range(8):
        c[n, C_SEL + 128 * n:C_SEL + 128 * n + 128] = 1
    pos = np.arange(256, dtype=f)
    for dim, at in ((32, 0), (64, 32)):
        inv = (f(1) / np.power(f(10000.0), np.arange(0, dim, 2, dtype=f) / f(dim))).astype(f)
        ang = (pos[:, None] * inv[None, :]).astype(f)
        for tb in range(2):
            a = ang[128 * tb:128 * tb + 128]
            o = C_ROPE + 96 * tb + at
            c[:, o:o + dim // 2] = np.cos(a)
            c[:, o + dim // 2:o + dim] = np.sin(a)
    t = np.arange(256)
    band = np.zeros((256, 4, 256), f)
    for g, w in enumerate((2, 4, 8, 16)):
        inside = (t[:, None] <= t[None, :]) & (t[:, None] > t[None, :] - w)
        band[:, g, :] = np.where(inside, f(1) / np.minimum(t + 1, w).astype(f)[None, :], f(0)) - np.eye(256, dtype=f)
    band = np.ascontiguousarray(band.reshape(2, 128, 4, 256).transpose(1, 2, 0, 3))
    hm = np.zeros((128, 8, 128), f)
    for n, m in enumerate(LEVELS):
        same = i[:, None] // (2 * m) == i[None, :] // (2 * m)
        hm[:, n, :] = same & ((i[:, None] // m) % 2 == 0) & ((i[None, :] // m) % 2 == 1)
    hm[:, 7, :] = np.eye(128)
    return c, band, hm


def kernel(**inputs):
    import concourse.bacc as bacc
    from concourse.bass_utils import run_bass_kernel_spmd as run

    a = {k: np.asarray(v) for k, v in inputs.items()}
    prm = np.zeros((128, P_N), np.float32)

    def put(name, v, j=0):
        v = np.asarray(v)
        prm[0:v.shape[0], P_AT[name] + j:P_AT[name] + j + v.shape[1]] = v

    def tiles(v):
        return v.reshape(-1, 128).T

    for name, src in (("g_mix_pre", a["g_mix_pre"][0]), ("g_mlp_pre", a["g_mlp_pre"][0]), ("g_ple_pre", a["g_ple_pre"][0]),
                      ("nm0", a["norm_mix_2"][0]), ("nm1", a["norm_mix_2"][1]), ("nf0", a["norm_ffn_2"][0]),
                      ("nf1", a["norm_ffn_2"][1]), ("ln_g", a["conf_ln_g"][0]), ("ln_b", a["conf_ln_b"][0]),
                      ("pool_scale", a["pool_scale"][0]), ("cb", a["s_conv_b_2"][0]), ("qn", a["a_q_norm_2"][0]),
                      ("kvn", a["a_kv_norm_2"][0]), ("subln", a["a_subln_2"][0]), ("s_norm", a["s_norm_2"][0]),
                      ("g_norm", a["h_g_norm_2"][0]), ("lb0", a["h_lower_bound_2"][0]), ("lb1", a["h_lower_bound_2"][1])):
        put(name, tiles(src))
    for name, src in (("dw", a["w_conf_dw"][0]), ("sc", a["w_sc"][0]), ("cw", a["s_conv_w_2"][0])):
        k, n = src.shape
        put(name, src.reshape(k, n // 128, 128).transpose(2, 1, 0).reshape(128, -1))
    prm[0:4, P_AT["bf"]] = a["b_forget"][0]
    prm[32:36, P_AT["bf"]] = a["b_forget"][0]
    prm[0:8, P_AT["dtb"]] = a["s_dt_bias_2"][0]
    prm[0:8, P_AT["alog"]] = a["s_a_log_2"][0]
    for i in range(4):
        prm[i, P_AT["fsel"] + i] = prm[32 + i, P_AT["fsel"] + i] = 1
    prm[:, P_AT["eps"]] = EPS
    srow = np.concatenate([a["s_d_2"][0], a["a_lq1_2"][0], a["a_lk1_2"][0], a["a_lq2_2"][0], a["a_lk2_2"][0]])
    cst, band, hm = constants()
    arrays = {"x": a["x"][0], "pT": np.ascontiguousarray(a["p"][0, 0].T), "prm": prm, "srow": srow, "cst": cst,
              "band": band, "hmask": hm, "w_pool": a["w_pool"][0], "norm_final_2": a["norm_final_2"]}
    for n in ("w_in", "w_conf_pw", "w_out", "w_up", "w_down", "w_ple_gate", "w_ple_proj", "g_mix_post", "g_mlp_post",
              "g_ple_post", "a_w_in_2", "a_w_uq_2", "a_w_ukv_2", "a_w_out_2", "s_w_in_2", "s_w_out_2"):
        arrays[n] = a[n][0]
    for n in ("ffn_gate", "ffn_up", "ffn_down"):
        for l in range(2):
            arrays[f"{n}_{l}"] = a[n + "_2"][l]
    nc = bacc.Bacc("TRN2", target_bir_lowering=False, num_devices=1)
    D, feed = {}, {}
    for n, v in arrays.items():
        v = np.ascontiguousarray(v)
        D[n] = nc.dram_tensor("in_" + n, v.shape, F32, kind="ExternalInput").ap()
        feed["in_" + n] = v
    out = nc.dram_tensor("out_0", (256, 1024), F32, kind="ExternalOutput").ap()
    program(nc, D, out)
    r = run(nc, [feed], core_ids=[0])
    return r.results[0]["out_0"].reshape(1, 256, 1024)
```

```python
from collections import namedtuple
from contextlib import ExitStack

import numpy as np

import concourse.bass as bass
from concourse import mybir

ALU = mybir.AluOpType
ACT = mybir.ActivationFunctionType
F32 = mybir.dt.float32
F32R = mybir.dt.float32r
BF16 = mybir.dt.bfloat16
AX = mybir.AxisListType.X

EPS = 1e-6
LAMBDA0 = 0.8 - 0.6 * float(np.exp(-0.3 * 0))
NEG = -1e30
NRAW = 3
NW = 4
SCN = 11136
LEVELS = [64, 32, 16, 8, 4, 2, 1]
TAPS = 31

C_ID, C_MA, C_MT, C_ONE, C_SEL, C_ROPE = 0, 128, 256, 384, 512, 1536
C_N = C_ROPE + 2 * 96

P_COLS = [("g_mix_pre", 8), ("g_mlp_pre", 8), ("g_ple_pre", 8), ("nm0", 8), ("nm1", 8), ("nf0", 8), ("nf1", 8),
          ("dw", 2 * TAPS), ("ln_g", 2), ("ln_b", 2), ("sc", 6), ("pool_scale", 2), ("cw", 32), ("cb", 8),
          ("qn", 3), ("kvn", 2), ("subln", 1), ("s_norm", 4), ("g_norm", 1), ("lb0", 4), ("lb1", 4),
          ("bf", 1), ("dtb", 1), ("alog", 1), ("fsel", 4), ("eps", 1), ("mhalf", 4)]
P_AT = {}
_at = 0
for _n, _c in P_COLS:
    P_AT[_n] = _at
    _at += _c
P_N = _at


Done = namedtuple("Done", "sem count")


class Queue:

    def __init__(self, sem):
        self.sem, self.n, self.items, self.seen = sem, 0, [], {}

    def emit(self, fn, waits, inc=True):
        need = []
        for sem, count in flat(waits):
            if self.seen.get(id(sem), 0) < count:
                self.seen[id(sem)] = count
                need.append((sem, count))
        if inc:
            self.n += 1
        self.items.append((need, fn, inc))
        return Done(self.sem, self.n)

    def last(self):
        return Done(self.sem, self.n) if self.n else None

    def replay(self, eng):
        for need, fn, inc in self.items:
            for sem, count in need:
                eng.wait_ge(sem, count)
            ins = fn(eng)
            if inc:
                ins.then_inc(self.sem, 1)


def flat(w):
    if w is None:
        return []
    if isinstance(w, Done):
        return [w]
    return [t for x in w for t in flat(x)]


def program(nc, D, out):
    with ExitStack() as ctx:
        def sb(name, shape, dt=F32):
            return ctx.enter_context(nc.sbuf_tensor(name, shape, dt))

        def sem(name):
            return ctx.enter_context(nc.semaphore(name))

        ps = [ctx.enter_context(nc.psum_tensor(f"ps{i}", [128, 512], F32)) for i in range(8)]
        cst = sb("cst", [128, C_N])
        prm = sb("prm", [128, P_N])
        rows = sb("rows", [128, 2, 1024])
        srow = sb("srow", [128, 264])
        h = sb("h", [128, 2, 1024])
        xf = sb("xf", [128, 8, 256])
        xh = sb("xh", [128, 8, 256], F32R)
        xl = sb("xl", [128, 8, 256], F32R)
        hs = sb("hs", [128, 2, 1024])
        hsf = hs[:, :, :].rearrange("p a b -> p (a b)")
        junk = sb("junk", [128, 1024])
        raw = [sb(f"raw{i}", [128, 2048]) for i in range(NRAW)]
        wh = [sb(f"wh{i}", [128, 2048], F32R) for i in range(NW)]
        wl = [sb(f"wl{i}", [128, 2048], F32R) for i in range(NW)]
        fh = sb("fh", [128, 3, 512], F32R)
        fl = sb("fl", [128, 3, 512], F32R)
        idb = sb("idb", [128, 128], BF16)
        mab = sb("mab", [128, 128], BF16)
        mtb = sb("mtb", [128, 128], BF16)
        st = sb("st", [128, 64])
        SC = sb("SC", [128, SCN])

        PE, AC, VE, GP = (Queue(sem(n)) for n in ("s_pe", "s_act", "s_dve", "s_pool"))
        SP = Queue(sem("s_sp"))
        s_raw = [sem(f"s_raw{i}") for i in range(NRAW)]
        s_misc = {}

        def pe(fn, *w, inc=True):
            return PE.emit(fn, w, inc)

        def act(o, i, f, *w, **kw):
            return AC.emit(lambda e: e.activation(o, i, f, **kw), w)

        def vec(fn, *w):
            return VE.emit(fn, w)

        def pool(fn, *w):
            return GP.emit(fn, w)

        def dma(name, dst, src, *w, q=None):
            if name not in s_misc:
                s_misc[name] = [sem("d_" + name), 0]
            box = s_misc[name]
            box[1] += 16
            (q or SP).emit(lambda e: e.dma_start(dst, src).then_inc(box[0], 16), w, inc=False)
            return Done(box[0], box[1])

        def tt(o, a, b, op, *w):
            return vec(lambda e: e.tensor_tensor(o, a, b, op), *w)

        def ts(o, a, s1, s2, o1, o2, *w):
            if o2 is None:
                return vec(lambda e: e.tensor_scalar(o, a, s1, None, o1), *w)
            return vec(lambda e: e.tensor_scalar(o, a, s1, s2, o1, o2), *w)

        def stt(o, a, s, b, o1, o2, *w):
            return vec(lambda e: e.scalar_tensor_tensor(o, a, s, b, o1, o2), *w)

        def vcopy(o, a, *w):
            return vec(lambda e: e.tensor_copy(o, a), *w)

        def bar():
            return [q.last() for q in (PE, AC, VE, GP) if q.last()]

        free = [(i, None) for i in range(8)]

        def take():
            return free.pop(0)

        def give(i, tok):
            free.append((i, tok))

        def P(name, i=0, n=1):
            return prm[:, P_AT[name] + i:P_AT[name] + i + n]

        def C(a, n=128):
            return cst[:, a:a + n]

        slots = []

        def slot(src, kt, n):
            slots.append((src, kt, n))
            return len(slots) - 1

        def cols(w, a, n):
            return slot(w.rearrange("(k p) n -> p k n", p=128)[:, :, a:a + n], w.shape[0] // 128, n)

        def krows(w, a, n):
            return slot(w[a * 128:(a + n) * 128, :].rearrange("(k p) n -> p k n", p=128), n, w.shape[1])

        def kcols(w, k, nk, a, n):
            return slot(w[k * 128:(k + nk) * 128, a:a + n].rearrange("(k p) n -> p k n", p=128), nk, n)

        w_in = D["w_in"]
        SEG = {"a": 0, "b": 256, "q": 512, "k": 768, "v": 1024, "h": 1284, "sb": 1540, "c": 1796, "p": 2052}
        S = {}
        for n in ("a", "b", "q", "k", "v", "h", "c", "sb", "p"):
            S[n] = cols(w_in, SEG[n], 256)
        S["out"] = [krows(D["w_out"], 2 * i, 2) for i in range(4)]

        def mlp_slots(n, ups, down):
            got = [[] for _ in range(n)]
            for j in range(n + 3):
                if j >= 3:
                    got[j - 3] += [krows(down, 2 * (j - 3), 2)]
                if j < n:
                    got[j] += [cols(w, 256 * j, 256) for w in ups]
            return got

        S["ff"] = mlp_slots(16, [D["w_up"]], D["w_down"])
        S["proj"] = krows(D["w_ple_proj"], 0, 2)
        S["gate"] = [krows(D["w_ple_gate"], 2 * i, 2) for i in range(4)]
        aw = D["a_w_in_2"]
        for n, c in (("dq", 672), ("dk", 1184), ("dv", 1696)):
            S[n] = [kcols(aw, 4 * i, 4, c, 512) for i in range(2)]
        S["cq"] = [cols(aw, 0, 256), cols(aw, 256, 128)]
        S["ckv"] = cols(aw, 384, 256)
        S["kr"] = cols(aw, 640, 32)
        S["uq"] = [cols(D["a_w_uq_2"], 384 * i, 384) for i in range(2)]
        S["ukv"] = krows(D["a_w_ukv_2"], 0, 2)
        S["aout"] = [krows(D["a_w_out_2"], 2 * i, 2) for i in range(4)]

        S["f0"] = mlp_slots(11, [D["ffn_gate_0"], D["ffn_up_0"]], D["ffn_down_0"])
        sw = D["s_w_in_2"]
        S["z"] = [kcols(sw, 4 * i, 4, 0, 512) for i in range(2)]
        S["xbc"] = [cols(sw, 512 + 256 * i, 256) for i in range(4)]
        S["hq"] = [cols(sw, 1544 + 256 * i, 256) for i in range(2)]
        S["hf"] = [cols(sw, 2056 + 256 * i, 256) for i in range(2)]
        S["hi"] = [kcols(sw, 4 * i, 4, 2568, 512) for i in range(2)]
        S["hg"] = [kcols(sw, 4 * i, 4, 3080, 512) for i in range(2)]
        S["sout"] = [krows(D["s_w_out_2"], 2 * i, 2) for i in range(4)]
        S["f1"] = mlp_slots(11, [D["ffn_gate_1"], D["ffn_up_1"]], D["ffn_down_1"])

        loaded, split_tok, used = [], [], {}

        def load(i):
            src, kt, n = slots[i]
            r = i % NRAW
            dst = raw[r][:, 0:kt * n].rearrange("p (k n) -> p k n", k=kt)
            free_at = split_tok[i - NRAW] if i >= NRAW else None
            SP.emit(lambda e: e.dma_start(dst, src).then_inc(s_raw[r], 16), [free_at], inc=False)
            loaded.append(Done(s_raw[r], 16 * (i // NRAW + 1)))

        def split(i):
            src, kt, n = slots[i]
            r, b, m = i % NRAW, i % NW, kt * n
            gone = used[i - NW] if i >= NW else None
            hi = act(wh[b][:, 0:m], raw[r][:, 0:m], ACT.Copy, loaded[i], gone)
            lo = tt(wl[b][:, 0:m], raw[r][:, 0:m], wh[b][:, 0:m].bitcast(F32), ALU.subtract, loaded[i], gone, hi)
            split_tok.append(lo)
            if i + NRAW < len(slots):
                load(i + NRAW)

        def prefetch():
            while len(split_tok) < len(slots) and (len(split_tok) < NW or len(split_tok) - NW in used):
                split(len(split_tok))

        def use(i):
            prefetch()
            _, kt, n = slots[i]
            b = i % NW
            v = [t[b][:, 0:kt * n].rearrange("p (k n) -> p k n", k=kt) for t in (wh, wl)]
            return v[0], v[1], split_tok[i]

        def end_use(i, tok):
            used[i] = tok
            prefetch()

        def mm3(o, a, al, b, bl, start, stop, *w, inc=False):
            pe(lambda e: e.matmul(o, a, b, start=start, stop=False, skip_group_check=True), *w, inc=False)
            pe(lambda e: e.matmul(o, al, b, start=False, stop=False, skip_group_check=True), inc=False)
            return pe(lambda e: e.matmul(o, a, bl, start=False, stop=stop, skip_group_check=True), inc=inc)

        def mm(o, a, b, start, stop, *w, inc=False):
            return pe(lambda e: e.matmul(o, a, b, start=start, stop=stop, skip_group_check=True), *w, inc=inc)

        def feat_mm(i, o, *w):
            wH, wL, tok = use(i)
            kt, nt = slots[i][1], slots[i][2] // 128
            for t in range(nt):
                c = slice(128 * t, 128 * t + 128)
                for k in range(kt):
                    done = mm3(o[:, 256 * t:256 * t + 256], wH[:, k, c], wL[:, k, c], xh[:, k, :], xl[:, k, :],
                               k == 0, k == kt - 1, tok, *w, inc=(t == nt - 1 and k == kt - 1))
            end_use(i, done)
            return done

        def tok_part(i, outs, tb, *w, k0=0, first=True, final=True, a=None):
            wH, wL, tok = use(i)
            kt = slots[i][1]
            ah, al = a or (xh, xl)
            s = slice(128 * tb, 128 * tb + 128)
            for n, (o, c) in enumerate(outs):
                for k in range(kt):
                    done = mm3(o, ah[:, k0 + k, s], al[:, k0 + k, s], wH[:, k, c], wL[:, k, c],
                               first and k == 0, final and k == kt - 1, tok, *w,
                               inc=(n == len(outs) - 1 and k == kt - 1))
            return done

        def tok_mm(i, outs, *w, **kw):
            for tb in range(2):
                done = tok_part(i, outs[tb], tb, *w, **kw)
            end_use(i, done)
            return done

        epsc = P("eps")

        def rstd(dst, ss, n, *w):
            k = ss.shape[1]
            a = ts(dst, ss, 1.0 / n, EPS, ALU.mult, ALU.add, *w)
            return pool(lambda e: e.tensor_tensor(dst, dst, P("mhalf", 0, k), ALU.pow), a, t_p)

        def hilo(t0, t1, tb, *w):
            s = slice(128 * tb, 128 * tb + 128)
            a = act(xh[:, t0:t1, s], xf[:, t0:t1, s], ACT.Copy, *w)
            b = tt(xl[:, t0:t1, s], xf[:, t0:t1, s], xh[:, t0:t1, s].bitcast(F32), ALU.subtract, a, *w)
            return [a, b]

        def hilo_all(*w):
            return [hilo(0, 8, tb, *w) for tb in range(2)]

        sq_last = [None, None]
        sq_n = [0]

        def square(src, acc, scale, *w):
            i = sq_n[0] % 2
            sq_n[0] += 1
            n = src.shape[1]
            sq_last[i] = act(junk[:, 512 * i:512 * i + n], src, ACT.Square, sq_last[i], *w, scale=scale, accum_out=acc)
            return sq_last[i]

        def rsqrt(dst, *w):
            k = dst.shape[1]
            return pool(lambda e: e.tensor_tensor(dst, dst, P("mhalf", 0, k), ALU.pow), t_p, *w)

        def to_xf(src, nt, t0, tb, gain, tok, *w):
            s = slice(128 * tb, 128 * tb + 128)
            done = []
            for c in range(0, nt, 4):
                m = min(4, nt - c)
                b, fr = take()
                for k in range(m):
                    t = pe(lambda e, k=k, c=c, b=b: e.transpose(ps[b][:, 128 * k:128 * k + 128],
                                                                src[:, 128 * (c + k):128 * (c + k) + 128],
                                                                C(C_ID)), tok, fr, t_c, inc=(k == m - 1))
                g = gain[:, c:c + m] if gain.shape[1] > 1 else gain.to_broadcast([128, m])
                g = g.unsqueeze(2).to_broadcast([128, m, 128])
                v = tt(xf[:, t0 + c:t0 + c + m, s], ps[b][:, 0:128 * m].rearrange("p (k n) -> p k n", k=m), g,
                       ALU.mult, t, *w)
                give(b, v)
                done.append(v)
            return done

        HALF = (slice(0, 512), slice(512, 1024))

        def rms_of(src, at, *w):
            q = [square(x, st[:, at + i:at + i + 1], 1.0 / 32, t, *w) for i, (x, t) in enumerate(src)]
            a = ts(st[:, at + 2:at + 3], st[:, at:at + 1], st[:, at + 1:at + 2], EPS, ALU.add, ALU.add, q)
            return rsqrt(st[:, at + 2:at + 3], a)

        def norm_a(tb, toks):
            r = rms_of([(h[:, tb, c], t) for c, t in zip(HALF, toks)], 3 * tb)
            return [ts(hs[:, tb, c], h[:, tb, c], st[:, 3 * tb + 2:3 * tb + 3], None, ALU.mult, None, r, toks) for c in HALF]

        def norm_b(gain, tb, toks, *w):
            out = []
            for i in range(2):
                t = to_xf(hs[:, tb, HALF[i]], 4, 4 * i, tb, gain[:, 4 * i:4 * i + 4], toks[i], *w)
                out.append(hilo(4 * i, 4 * i + 4, tb, t, *w))
            return out

        def add_norm(src, row, row_tok, tb, toks):
            at = 6 + 3 * tb
            r = rms_of(list(zip(src, toks)), at)
            m = [stt(hs[:, tb, c], x, st[:, at + 2:at + 3], row[:, c], ALU.mult, ALU.mult, r, row_tok)
                 for c, x in zip(HALF, src)]
            return m, [tt(h[:, tb, c], h[:, tb, c], hs[:, tb, c], ALU.add, t) for c, t in zip(HALF, m)]

        def proj_out(sl, x0, enter1, early, late):
            bk = [[take() for _ in range(2)] for _ in range(2)]
            x = x0
            for tb in range(2):
                if tb == 1:
                    x = enter1()
                for i in range(4):
                    d = tok_part(sl[i], [(ps[bk[tb][c][0]][:, :], HALF[c]) for c in range(2)], tb, x,
                                 [y[1] for y in bk[tb]], k0=2 * i, first=(i == 0), final=(i == 3))
                    if tb == 1:
                        end_use(sl[i], d)
                        if i == 1:
                            late(0)
                early(tb, bk[tb], d)

        def add_banks(tb, bk, d):
            out = []
            for c in range(2):
                o = h[:, tb, HALF[c]]
                out.append(tt(o, o, ps[bk[c][0]][:, :], ALU.add, d))
                give(bk[c][0], out[-1])
            return out

        class Step:

            def __init__(self, add, gain):
                self.add, self.gain, self.a, self.b = add, gain, {}, {}

            def early(self, tb, bk, d):
                self.a[tb] = norm_a(tb, self.add(tb, bk, d))

            def late(self, tb):
                if tb not in self.b:
                    self.b[tb] = norm_b(self.gain, tb, self.a[tb])
                return self.b[tb]

        def normed(row, row_tok):
            def add(tb, bk, d):
                m, t = add_norm([ps[bk[c][0]][:, :] for c in range(2)], row, row_tok, tb, [d, d])
                for c in range(2):
                    give(bk[c][0], m[c])
                return t
            return add

        def softplus(x, a, u, w, l, tok, *more):
            t = act(a, x, ACT.Abs, tok, *more)
            t = act(u, a, ACT.Exp, t, *more, scale=-1.0)
            t1 = ts(w, u, 1.0, None, ALU.add, None, t)
            t2 = act(l, w, ACT.Ln, t1, *more)
            t = ts(a, w, -1.0, None, ALU.add, None, t1)
            t = tt(a, u, a, ALU.subtract, t)
            t2 = vec(lambda e: e.reciprocal(w, w), t2)
            t = tt(a, a, w, ALU.mult, t, t2)
            t = tt(a, a, l, ALU.add, t)
            return stt(x, x, 0.0, a, ALU.max, ALU.add, t)

        class Scratch:
            def __init__(self):
                self.at = 0

            def __call__(self, *dims):
                n = int(np.prod(dims))
                v = SC[:, self.at:self.at + n]
                self.at += n
                assert self.at <= SCN, self.at
                if len(dims) == 2:
                    v = v.rearrange("p (a b) -> p a b", a=dims[0])
                if len(dims) == 3:
                    v = v.rearrange("p (a b c) -> p a b c", a=dims[0], b=dims[1])
                return v

        t_h = [dma(f"h{tb}", h[:, tb, :], D["x"][128 * tb:128 * tb + 128, :]) for tb in range(2)]
        t_p = dma("prm", prm[:, :], D["prm"])
        t_c = dma("cst", cst[:, :], D["cst"])
        for i in range(NRAW):
            load(i)
        t_r0 = dma("row0", rows[:, 0, :], D["g_mix_post"].partition_broadcast(128), q=GP)
        t_r1 = dma("row1", rows[:, 1, :], D["g_mlp_post"].partition_broadcast(128), q=GP)
        t_sr = dma("srow", srow[:, :], D["srow"].partition_broadcast(128), q=GP)
        t_m = [act(o[:, :], C(c), ACT.Copy, t_c) for o, c in ((idb, C_ID), (mab, C_MA), (mtb, C_MT))]

        sc = Scratch()
        wf = sc(8, 36)
        band = sc(4, 2, 256)
        wpw = sc(2, 256)
        wpb = sc(2, 128)
        upad = sc(2, 30 + 256)
        cacc = sc(2, 256)
        csq = sc(2, 256)
        sg = sc(512)
        qm = sc(4, 256)
        kT = sc(2, 256)
        vs = sc(2, 256)
        hsb = sc(512)
        cpad = sc(2, 2 + 256)
        scv = sc(2, 256)
        pv = sc(2, 256)
        dT = sc(2, 256)
        NCt = sc(256)
        CQ = sc(256)
        rk = sc(256)
        ft = hsf[:, 0:1024].rearrange("p (a b) -> p a b", a=4)
        Pm = hsf[:, 0:1152].rearrange("p (a b) -> p a b", a=3)
        PT = hsf[:, 1152:1920].rearrange("p (a b) -> p a b", a=2)
        z1 = [pool(lambda e: e.memset(wf, 0.0)), pool(lambda e: e.memset(wpb, 0.0)), pool(lambda e: e.memset(upad, 0.0)),
              pool(lambda e: e.memset(qm, 0.0)), pool(lambda e: e.memset(cpad, 0.0)), pool(lambda e: e.memset(NCt, 0.0)),
              pool(lambda e: e.memset(CQ, 0.0))]
        wfv = w_in[:, 1280:1284].rearrange("(k p) n -> p k n", p=128)
        t_wf = [dma("wf0", wf[:, :, 0:4], wfv, z1, q=GP), dma("wf1", wf[:, :, 32:36], wfv, z1, q=GP)]
        t_bd = dma("band", band, D["band"], q=GP)
        t_pw = dma("pw", wpw, D["w_conf_pw"].rearrange("(k p) n -> p k n", p=128), q=GP)
        t_wp = [dma(f"wp{g}", wpb[64 * (g % 2):64 * (g % 2) + 64, g // 2, 64 * (g % 2):64 * (g % 2) + 64],
                    D["w_pool"][g], z1, q=GP) for g in range(4)]

        def bank_feat(sl, *w):
            b, fr = take()
            return b, feat_mm(sl, ps[b], *w, fr)

        def bank_mm(name):
            return bank_feat(S[name], t_x)

        def bank_tok(sl, n, *w):
            b, fr = take()
            return b, tok_mm(sl, [[(ps[b][:, 256 * tb:256 * tb + n], slice(0, n))] for tb in range(2)], *w, fr)

        def both(x):
            return [x.late(0), x.late(1)]

        stp = Step(lambda tb, bk, d: [t_h[tb], t_h[tb]], P("g_mix_pre", 0, 8))
        for tb in range(2):
            stp.early(tb, None, None)
        t_x = both(stp)
        ba, da = bank_mm("a")
        bb, db = bank_mm("b")
        t1 = act(sg, ps[bb][:, :], ACT.Sigmoid, db)
        give(bb, t1)
        t_u = tt(upad[:, :, 30:286], ps[ba][:, :].rearrange("p (t n) -> p t n", t=2),
                 sg.rearrange("p (t n) -> p t n", t=2), ALU.mult, t1, da, z1)
        give(ba, t_u)
        bq, dq_ = bank_mm("q")
        t_q = []
        for i in range(2):
            pr = slice(64 * i, 64 * i + 64)
            t_q.append(act(qm.rearrange("p (t i) n -> p t i n", i=2)[pr, :, i, :],
                           ps[bq][pr, :].rearrange("p (t n) -> p t n", t=2), ACT.Copy, dq_, z1, scale=0.125))
        give(bq, t_q[-1])
        bk_, dk_ = bank_mm("k")
        t_k = act(kT, ps[bk_][:, :].rearrange("p (t n) -> p t n", t=2), ACT.Copy, dk_)
        give(bk_, t_k)

        conv_tok = [t_u, t_u]

        def conv_steps():
            for k in range(TAPS):
                for t in range(2):
                    src, w = upad[:, t, k:k + 256], P("dw", TAPS * t + k)
                    if k == 0:
                        conv_tok[t] = ts(cacc[:, t, :], src, w, None, ALU.mult, None, conv_tok[t])
                    else:
                        conv_tok[t] = stt(cacc[:, t, :], src, w, cacc[:, t, :], ALU.mult, ALU.add, conv_tok[t])
                    yield

        conv = conv_steps()

        def advance(gen, n):
            for _ in range(n):
                if next(gen, 0) is None:
                    continue
                return

        b, fr = take()
        for k in range(8):
            d = mm(ps[b][0:36, 0:256], wf[:, k, :], xf[:, k, :], k == 0, k == 7, t_wf, t_x, fr, inc=(k == 7))
        R = slice(0, 36)
        fx, fa, fu, fw = (ft[R, i, :] for i in range(4))
        t1 = ts(fx, ps[b][R, 0:256], P("bf")[R], -1.0, ALU.add, ALU.mult, d)
        give(b, t1)
        logf = softplus(fx, fa, fu, fw, junk[R, 0:256], t1, bar())
        t1 = ts(fx, fx, -1.0, None, ALU.mult, None, logf)
        t2 = vec(lambda e: e.memset(fu, 1.0), logf)
        t_scan = vec(lambda e: e.tensor_tensor_scan(fa, fu, fx, 0.0, ALU.mult, ALU.add), t1, t2)
        F4, G4 = slice(0, 4), slice(32, 36)
        t_cq = [vcopy(CQ[F4, :], ft[F4, 1, :], t_scan, z1),
                vec(lambda e: e.memset(CQ[G4, :], 1.0), z1),
                ts(NCt[G4, :], ft[G4, 1, :], -1.0, None, ALU.mult, None, t_scan, z1),
                vec(lambda e: e.memset(NCt[F4, :], 1.0), z1)]
        advance(conv, 8)

        advance(conv, 9)
        b, d = bank_tok(S["v"], 256, t_x)
        t_v = act(vs, ps[b][:, :].rearrange("p (t n) -> p t n", t=2), ACT.Copy, d)
        give(b, t_v)
        advance(conv, 9)
        b, d = bank_mm("h")
        t_hs = act(hsb, ps[b][:, :], ACT.Copy, d)
        give(b, t_hs)
        advance(conv, 9)
        b, d = bank_mm("c")
        t_c3 = tt(cpad[:, :, 2:258], ps[b][:, :].rearrange("p (t n) -> p t n", t=2),
                  hsb.rearrange("p (t n) -> p t n", t=2), ALU.mult, t_hs, d, z1)
        give(b, t_c3)
        t3 = []
        for t in range(2):
            a = ts(scv[:, t, :], cpad[:, t, 0:256], P("sc", 3 * t), None, ALU.mult, None, t_c3)
            for k in (1, 2):
                a = stt(scv[:, t, :], cpad[:, t, k:k + 256], P("sc", 3 * t + k), scv[:, t, :], ALU.mult, ALU.add, a)
            t3.append(a)
        advance(conv, 9)
        bsb, dsb = bank_mm("sb")
        advance(conv, 9)
        bp, dp = bank_tok(S["p"], 256, t_x)
        x_gone = PE.last()
        t_sc = tt(xf[:, 4:6, :], ps[bsb][:, :].rearrange("p (t n) -> p t n", t=2), scv, ALU.mult, dsb, t3, x_gone)
        give(bsb, t_sc)
        t_pv = act(pv, ps[bp][:, :].rearrange("p (t n) -> p t n", t=2), ACT.Copy, dp)
        give(bp, t_pv)
        advance(conv, 99)

        b, fr = take()
        for t in range(2):
            d = mm(ps[b][:, 0:256], C(C_ONE), cacc[:, t, :], t == 0, t == 1, conv_tok, fr, t_c, inc=(t == 1))
        t1 = tt(cacc, cacc, ps[b][:, 0:256].unsqueeze(1).to_broadcast([128, 2, 256]), ALU.subtract, d)
        give(b, t1)
        t2 = tt(csq, cacc, cacc, ALU.mult, t1)
        b, fr = take()
        for t in range(2):
            d = mm(ps[b][:, 0:256], C(C_ONE), csq[:, t, :], t == 0, t == 1, t2, fr, inc=(t == 1))
        t1 = act(sg[:, 0:256], ps[b][:, 0:256], ACT.Sqrt, d, bias=epsc)
        give(b, t1)
        t1 = vec(lambda e: e.reciprocal(sg[:, 0:256], sg[:, 0:256]), t1)
        t1 = tt(cacc, cacc, sg[:, 0:256].unsqueeze(1).to_broadcast([128, 2, 256]), ALU.mult, t1)
        t2 = [act(csq[:, t, :], cacc[:, t, :], ACT.Silu, t1, scale=P("ln_g", t), bias=P("ln_b", t)) for t in range(2)]
        b, fr = take()
        for t in range(2):
            for k in range(2):
                d = mm(ps[b][:, 256 * t:256 * t + 256], wpw[:, k, 128 * t:128 * t + 128], csq[:, k, :], k == 0, k == 1,
                       t2, fr, t_pw, inc=(t == 1 and k == 1))
        t_conf = act(xf[:, 0:2, :], ps[b][:, :].rearrange("p (t n) -> p t n", t=2), ACT.Copy, d, x_gone)
        give(b, t_conf)

        t_d = []
        for t in range(2):
            b, fr = take()
            for i in range(2):
                for tb in range(2):
                    d = mm(ps[b][:, 256 * i:256 * i + 256], pv[:, tb, 128 * t:128 * t + 128], band[:, 2 * t + i, tb, :],
                           tb == 0, tb == 1, t_pv, t_bd, fr, inc=(i == 1 and tb == 1))
            for i in range(2):
                pr = slice(64 * i, 64 * i + 64)
                t_d.append(vcopy(dT[pr, t, :], ps[b][pr, 256 * i:256 * i + 256], d))
            give(b, t_d[-1])
        b, fr = take()
        for t in range(2):
            d = mm(ps[b][:, 256 * t:256 * t + 256], wpb[:, t, :], dT[:, t, :], True, True, t_d, t_wp, fr, inc=(t == 1))
        for t in range(2):
            t_pool = ts(xf[:, 6 + t, :], ps[b][:, 256 * t:256 * t + 256], P("pool_scale", t), None, ALU.mult, None, d, x_gone)
        give(b, t_pool)

        def attention(n, scores, scale, finish, Pm, PT, base):
            state = {}
            gone = {}

            def soft(i):
                b, d = state.pop(i)
                p, c = Pm[:, i % 3, :], 12 + 6 * (i % 3)
                m = []
                for q in range(2):
                    lo, hi = (0, 128) if q == 0 else (128, 384)
                    m.append(vec(lambda e, q=q, lo=lo, hi=hi: e.tensor_reduce(st[:, c + q:c + q + 1], ps[b][:, lo:hi], AX,
                                                                              ALU.max, negate=True), d, base, gone.get(i - 3)))
                s = ts(st[:, c:c + 2], st[:, c:c + 2], scale, None, ALU.mult, None, m) if scale != 1.0 else m
                x = []
                for q in range(2):
                    lo, hi = (0, 128) if q == 0 else (128, 384)
                    x.append(act(p[:, lo:hi], ps[b][:, lo:hi], ACT.Exp, s, gone.get(i - 3), base, scale=scale,
                                 bias=st[:, c + q:c + q + 1], accum_out=st[:, c + 2 + q:c + 3 + q]))
                give(b, x[-1])
                r = vec(lambda e: e.reciprocal(st[:, c + 4:c + 6], st[:, c + 2:c + 4]), x)
                return p, st[:, c + 4:c + 6], r

            for i in range(n + 2):
                if i < n:
                    b, fr = take()
                    state[i] = (b, scores(i, ps[b], [fr, base]))
                if 1 <= i <= n:
                    gone[i - 1] = finish(i - 1, *soft(i - 1))

        def norm_p(p, r, tok):
            a = ts(p[:, 0:128], p[:, 0:128], r[:, 0:1], None, ALU.mult, None, tok)
            return ts(p[:, 128:384], p[:, 128:384], r[:, 1:2], None, ALU.mult, None, a, tok)

        def turn(p, o, tok, *w):
            b, fr = take()
            for j in range(3):
                d = pe(lambda e, j=j: e.transpose(ps[b][:, 128 * j:128 * j + 128], p[:, 128 * j:128 * j + 128], C(C_ID)),
                       tok, fr, inc=(j == 2))
            t = act(o, ps[b][:, 0:384], ACT.Copy, d, *w)
            give(b, t)
            return d, t

        def logits(o, qh, kh, fr, w, extra=None):
            for q in range(2):
                lo, n = (0, 128) if q == 0 else (128, 256)
                mm(o[:, lo:lo + n], qh[:, 128 * q:128 * q + 128], kh[:, 0:n], True, False, fr, w)
                if extra:
                    mm(o[:, lo:lo + n], extra[0][:, 128 * q:128 * q + 128], extra[1][:, 0:n], False, False, extra[2])
                d = mm(o[:, lo + n - 128:lo + n], idb[:, :], mab[:, :], False, True, t_m, inc=(q == 1))
            return d

        fo_pv, fo_rk = [], [None]

        def fo_scores(i, o, fr):
            t = ts(rk, NCt, P("fsel", i), None, ALU.mult, None, t_cq, fo_rk[0])
            fo_rk[0] = logits(o, qm[:, i, :], kT[:, i // 2, :], fr, [t_q, t_k], (CQ, rk, [t, t_cq]))
            return fo_rk[0]

        def fo_finish(i, p, r, tok):
            n = norm_p(p, r, tok)
            o = PT[:, i % 2, :]
            d, t = turn(p, o, n, fo_pv[-2:-1])
            b, fr = take()
            c = slice(128 * (i // 2), 128 * (i // 2) + 128)
            mm(ps[b][:, 0:128], vs[:, 0, c], o[:, 0:128], True, True, t, t_v, fr)
            mm(ps[b][:, 128:256], vs[:, 0, c], o[:, 128:256], True, False)
            e = mm(ps[b][:, 128:256], vs[:, 1, c], o[:, 256:384], False, True, inc=True)
            fo_pv.append(e)
            pr = slice(64 * (i % 2), 64 * (i % 2) + 64)
            x = act(xf[pr, 2 + i // 2, :], ps[b][pr, 0:256], ACT.Copy, e, x_gone)
            give(b, x)
            return [d, x]

        attention(4, fo_scores, 1.0, fo_finish, Pm, PT, None)
        t_x = hilo_all(bar())
        stp = Step(normed(rows[:, 0, :], t_r0), P("g_mlp_pre", 0, 8))
        proj_out(S["out"], t_x[0], lambda: t_x[1], stp.early, stp.late)

        t_r0 = dma("row0", rows[:, 0, :], D["g_ple_post"].partition_broadcast(128), bar(), q=GP)

        def ffn(sl, gated, x, nxt):
            b0 = bar()
            rb = SC[:, 0:1024].rearrange("p (a b) -> p a b", a=2)
            fb = SC[:, 1024:2048].rearrange("p (a b) -> p a b", a=2)
            n = len(sl)
            dn, rd = {}, {}

            def evacuate(j, banks):
                p = j % 2
                r_gone, f_gone = rd.get(j - 2), dn.get(j - 3)
                (b, d), (b2, d2) = banks[0], banks[-1]
                r = act(rb[:, p, :], ps[b][:, :], ACT.Silu if gated else ACT.Relu, d, b0, r_gone)
                if gated:
                    give(b, r)
                    f = tt(fb[:, p, :], ps[b2][:, :], rb[:, p, :], ALU.mult, r, d2, b0, r_gone)
                else:
                    f = stt(fb[:, p, :], ps[b][:, :], 0.0, rb[:, p, :], ALU.max, ALU.mult, r, b0, r_gone)
                give(b2, f)
                a = act(fh[:, j % 3, :], fb[:, p, :], ACT.Copy, f, f_gone)
                l = tt(fl[:, j % 3, :], fb[:, p, :], fh[:, j % 3, :].bitcast(F32), ALU.subtract, a, f, f_gone)
                rd[j] = [a, l]

            def down(i, tb):
                v = [y[:, i % 3, :].rearrange("p (k n) -> p k n", k=2) for y in (fh, fl)]
                return tok_part(sl[i][-1], [(ps[acc[tb][c][0]][:, :], HALF[c]) for c in range(2)], tb, rd[i],
                                [y[1] for y in acc[tb]], first=(i == 0), final=(i == n - 1), a=v)

            ups = [y[:-1] for y in sl]
            t_x = both(x)
            acc = None
            for j in range(n):
                if j >= 3:
                    if acc is None:
                        acc = [[take() for _ in range(2)] for _ in range(2)]
                    down(j - 3, 0)
                    dn[j - 3] = down(j - 3, 1)
                    end_use(sl[j - 3][-1], dn[j - 3])
                banks = []
                for i in ups[j]:
                    b, fr = take()
                    banks.append((b, feat_mm(i, ps[b], t_x, fr)))
                evacuate(j, banks)
            for tb in range(2):
                for i in range(n - 3, n):
                    d = down(i, tb)
                    if tb == 1:
                        end_use(sl[i][-1], d)
                        if i == n - 2:
                            nxt.late(0)
                nxt.early(tb, acc[tb], d)

        nxt = Step(normed(rows[:, 1, :], t_r1), P("g_ple_pre", 0, 8))
        ffn(S["ff"], False, stp, nxt)
        stp = nxt

        t_r1 = dma("row1", rows[:, 1, :], D["norm_final_2"].partition_broadcast(128), bar(), q=GP)
        b0 = bar()
        pT = SC[:, 0:512].rearrange("p (k n) -> p k n", k=2)
        e0 = SC[:, 512:2560].rearrange("p (a b) -> p a b", a=2)
        sgm = SC[:, 2560:4608].rearrange("p (a b) -> p a b", a=2)
        t_pT = dma("pT", pT, D["pT"].rearrange("(k p) n -> p k n", p=128), b0, q=GP)
        ph, pl = (x[:, 0, :].rearrange("p (k n) -> p k n", k=2) for x in (fh, fl))
        a = act(ph, pT, ACT.Copy, t_pT, b0)
        l = tt(pl, pT, ph.bitcast(F32), ALU.subtract, a)
        bkp = [[take() for _ in range(2)] for _ in range(2)]
        dp = tok_mm(S["proj"], [[(ps[bkp[tb][c][0]][:, :], HALF[c]) for c in range(2)]
                                for tb in range(2)], [a, l], [x[1] for y in bkp for x in y], a=(ph, pl))
        t_es = {}
        for tb in range(2):
            for c in range(2):
                t_es[tb, c] = vcopy(e0[:, tb, HALF[c]], ps[bkp[tb][c][0]][:, :], dp, b0)
                give(bkp[tb][c][0], t_es[tb, c])

        def gated(tb, bk, d):
            m = []
            for c in range(2):
                a = act(sgm[:, tb, HALF[c]], ps[bk[c][0]][:, :], ACT.Sigmoid, d, b0)
                give(bk[c][0], a)
                m.append(tt(e0[:, tb, HALF[c]], e0[:, tb, HALF[c]], sgm[:, tb, HALF[c]], ALU.mult, a, t_es[tb, c]))
            return add_norm([e0[:, tb, c] for c in HALF], rows[:, 0, :], t_r0, tb, m)[1]

        nxt = Step(gated, P("nm0", 0, 8))
        proj_out(S["gate"], stp.late(0), lambda: stp.late(1), nxt.early, nxt.late)
        stp = nxt

        b0 = bar()
        sc = Scratch()
        dqm = sc(8, 256)
        dkT = sc(4, 256)
        dvs = sc(2, 512)
        roped = sc(2, 2, 512)
        cqs = sc(2, 384)
        cks = sc(2, 256)
        krs = sc(2, 32)
        tmp = sc(4, 256)
        Pm = sc(3, 384)
        PT = sc(2, 384)
        lam = sc(64)

        z2 = pool(lambda e: e.memset(dqm, 0.0), b0)

        def wide(names, x0, enter1):
            bk = {n: [take() for _ in range(2)] for n in names}
            out = {n: [None, None] for n in names}
            x = x0
            for tb in range(2):
                if tb == 1:
                    x = enter1()
                for n in names:
                    for i in range(2):
                        d = tok_part(S[n][i], [(ps[bk[n][tb][0]][:, :], slice(0, 512))], tb, x, bk[n][tb][1],
                                     k0=4 * i, first=(i == 0), final=(i == 1))
                        if tb == 1:
                            end_use(S[n][i], d)
                    out[n][tb] = (bk[n][tb][0], d)
            return out, [x0, x]

        def rope(dst, src, tb, nh, half, at, d, *w):
            n = nh * half
            co = cst[:, at + 96 * tb:at + 96 * tb + half].unsqueeze(1).to_broadcast([128, nh, half])
            si = cst[:, at + 96 * tb + half:at + 96 * tb + 2 * half].unsqueeze(1).to_broadcast([128, nh, half])
            x1, x2 = src[:, :, 0:half], src[:, :, half:2 * half]
            u = [tmp[:, i, 0:n].rearrange("p (a b) -> p a b", a=nh) for i in range(4)]
            b = bar()
            a = [tt(u[0], x1, co, ALU.mult, d, b), tt(u[1], x2, si, ALU.mult, d), tt(u[2], x2, co, ALU.mult, d),
                 tt(u[3], x1, si, ALU.mult, d)]
            return [a, tt(dst[:, :, 0:half], u[0], u[1], ALU.subtract, a, *w),
                    tt(dst[:, :, half:2 * half], u[2], u[3], ALU.add, a, *w)]

        t_rp = []
        w_dqk, t_x = wide(["dq", "dk"], stp.late(0), lambda: stp.late(1))
        b0 = [b0, bar()]
        for tb in range(2):
            for j, n in enumerate(("dq", "dk")):
                b, d = w_dqk[n][tb]
                r = rope(roped[:, j, tb, :].rearrange("p (a b) -> p a b", a=8),
                         ps[b][:, :].rearrange("p (a b) -> p a b", a=8), tb, 8, 32, C_ROPE + 32, d, b0)
                give(b, r[0][-1])
                t_rp.append(r)
        w_dv, _ = wide(["dv"], t_x, lambda: t_x)
        t_dv = []
        for tb in range(2):
            b, d = w_dv["dv"][tb]
            t_dv.append(act(dvs[:, tb, :], ps[b][:, :], ACT.Copy, d, b0))
            give(b, t_dv[-1])
        t_cq = []
        for i, (sl, o, n) in enumerate(((S["cq"][0], cqs[:, :, 0:256], 256), (S["cq"][1], cqs[:, :, 256:384], 128),
                                        (S["ckv"], cks, 256), (S["kr"], krs, 32))):
            b, d = bank_tok(sl, n, t_x)
            t_cq.append(act(o, ps[b][:, :].rearrange("p (t n) -> p t n", t=2)[:, :, 0:n], ACT.Copy, d, b0))
            give(b, t_cq[-1])
        x_gone = PE.last()
        krr = hsf[:, 0:64].rearrange("p (t n) -> p t n", t=2)
        t_kr = [rope(krr[:, tb, :].unsqueeze(1), krs[:, tb, :].unsqueeze(1), tb, 1, 16, C_ROPE, t_cq[3], bar())
                for tb in range(2)]
        t_dq, t_dk = [], []
        for j in range(2):
            for tb in range(2):
                b, fr = take()
                for k in range(4):
                    d = pe(lambda e, j=j, tb=tb, k=k, b=b: e.transpose(ps[b][:, 128 * k:128 * k + 128],
                                                                       roped[:, j, tb, 128 * k:128 * k + 128], C(C_ID)),
                           t_rp, fr, inc=(k == 3))
                s = slice(128 * tb, 128 * tb + 128)
                v = ps[b][:, :].rearrange("p (k n) -> p k n", k=4)
                if j == 0:
                    for i in range(2):
                        pr = slice(64 * i, 64 * i + 64)
                        t_dq.append(act(dqm.rearrange("p (k i) n -> p k i n", i=2)[pr, :, i, s], v[pr], ACT.Copy, d, z2))
                    give(b, t_dq[-1])
                else:
                    t_dk.append(act(dkT[:, :, s], v, ACT.Copy, d, b0))
                    give(b, t_dk[-1])

        t_n = []
        for tb in range(2):
            for i, (src, n) in enumerate(((cqs, 384), (cks, 256))):
                c = 36 + 4 * tb + 2 * i
                q = square(src[:, tb, :], st[:, c:c + 1], 1.0, t_cq, b0)
                r = rstd(st[:, c + 1:c + 2], st[:, c:c + 1], n, q)
                m = ts(src[:, tb, :], src[:, tb, :], st[:, c + 1:c + 2], None, ALU.mult, None, r, q)
                t_n.append(to_xf(src[:, tb, :], n // 128, 0 if i == 0 else 3, tb, P("qn", 0, 3) if i == 0 else P("kvn", 0, 2),
                                 m, x_gone, bar()))
        t_lat = [hilo(0, 5, tb, t_n, x_gone) for tb in range(2)]
        lat_gone = bar()

        la = []
        for i in range(2):
            a = tt(lam[:, 0:64], srow[:, 8 + 128 * i:72 + 128 * i], srow[:, 72 + 128 * i:136 + 128 * i], ALU.mult, t_sr, b0, la)
            r = vec(lambda e, i=i: e.tensor_reduce(st[:, 48 + i:49 + i], lam[:, 0:64], AX, ALU.add), a)
            la = [r]
        a = act(st[:, 50:52], st[:, 48:50], ACT.Exp, la)
        a = tt(st[:, 52:53], st[:, 50:51], st[:, 51:52], ALU.subtract, a)
        a = ts(st[:, 52:53], st[:, 52:53], LAMBDA0, None, ALU.add, None, a)
        b_ = act(st[:, 53:54], st[:, 52:53], ACT.Abs, a)
        b_ = ts(st[:, 53:54], st[:, 53:54], 1.0, None, ALU.max, None, b_)
        b_ = vec(lambda e: e.reciprocal(st[:, 54:55], st[:, 53:54]), b_)
        b_ = stt(st[:, 55:56], st[:, 52:53], -1.0, st[:, 54:55], ALU.mult, ALU.mult, b_)
        t_lam = stt(st[:, 56:57], st[:, 54:55], EPS, st[:, 54:55], ALU.mult, ALU.mult, b_)

        D0 = {}
        df_pv = []
        df_o = []

        def df_scores(i, o, fr):
            return logits(o, dqm[:, i, :], dkT[:, i // 2, :], fr, [t_dq, t_dk])

        def df_finish(i, p, r, tok):
            f = 54 + i % 2
            s = ts(r, r, st[:, f:f + 1], None, ALU.mult, None, tok, t_lam)
            n = norm_p(p, r, s)
            if i % 2 == 0:
                D0[i] = (p, n)
                return None
            p0, n0 = D0.pop(i - 1)
            n = tt(p, p, p0, ALU.add, n, n0)
            g = i // 2
            o = PT[:, g % 2, :]
            d, t = turn(p, o, n, df_pv[-2:-1])
            b, fr = take()
            c = slice(128 * g, 128 * g + 128)
            mm(ps[b][:, 0:128], o[:, 0:128], dvs[:, 0, c], True, True, t, t_dv, fr)
            mm(ps[b][:, 128:256], o[:, 128:256], dvs[:, 0, c], True, False)
            e = mm(ps[b][:, 128:256], o[:, 256:384], dvs[:, 1, c], False, True, inc=True)
            df_pv.append(e)
            w = bar()
            on = roped[:, g % 2, 0, 0:256]
            q = [square(ps[b][:, 128 * tb:128 * tb + 128], st[:, 57 + tb:58 + tb], 1.0, e, w) for tb in range(2)]
            y = ts(st[:, 59:61], st[:, 57:59], 1.0 / 128, st[:, 56:57], ALU.mult, ALU.add, q, t_lam, w)
            y = pool(lambda e: e.tensor_tensor(st[:, 59:61], st[:, 59:61], P("mhalf", 0, 2), ALU.pow), y)
            m = [ts(on[:, 128 * tb:128 * tb + 128], ps[b][:, 128 * tb:128 * tb + 128], st[:, 59 + tb:60 + tb], 1.0 - LAMBDA0,
                    ALU.mult, ALU.mult, y, w) for tb in range(2)]
            give(b, m)
            for tb in range(2):
                df_o.append(to_xf(on[:, 128 * tb:128 * tb + 128], 1, 4 + g, tb, P("subln"), m, lat_gone, t_lat))
            return [d, n]

        attention(8, df_scores, 0.125, df_finish, Pm, PT, b0)

        b0 = bar()
        sc = Scratch()
        qf = sc(2, 768)
        kf = sc(2, 768)
        vm = sc(2, 512)
        qT = sc(8, 256)
        kT2 = sc(8, 256)
        tmp = sc(4, 256)
        Pm = sc(3, 384)
        PT = sc(2, 384)
        t_qf = []
        bq = [[take() for _ in range(2)] for _ in range(2)]
        fr = [x[1] for y in bq for x in y]
        for i in range(2):
            d = tok_mm(S["uq"][i], [[(ps[bq[tb][i][0]][:, 0:384], slice(0, 384))] for tb in range(2)], t_lat, fr)
            for tb in range(2):
                v = ps[bq[tb][i][0]][:, 0:384].rearrange("p (a b) -> p a b", a=4)
                o = qf[:, tb, 384 * i:384 * i + 384].rearrange("p (a b) -> p a b", a=4)
                a = act(o[:, :, 0:64], v[:, :, 0:64], ACT.Copy, d, b0)
                r = rope(o[:, :, 64:96], v[:, :, 64:96], tb, 4, 16, C_ROPE, [d, a], b0)
                give(bq[tb][i][0], r[0][-1])
                t_qf.append([a, r])
        wH, wL, tok = use(S["ukv"])
        bkk = [take() for _ in range(2)]
        bvv = [take() for _ in range(2)]
        fr = [x[1] for x in bkk + bvv]
        for tb in range(2):
            s = slice(128 * tb, 128 * tb + 128)
            for o, c in ((ps[bkk[tb][0]], 0), (ps[bvv[tb][0]], 64)):
                for k in range(2):
                    sel = [x[:, k, :].rearrange("p (a b) -> p a b", a=8)[:, :, c:c + 64] for x in (wH, wL)]
                    d = mm3(o[:, :].rearrange("p (a b) -> p a b", a=8), xh[:, 3 + k, s], xl[:, 3 + k, s], sel[0], sel[1],
                            k == 0, k == 1, tok, t_lat, fr, inc=(tb == 1 and c == 64 and k == 1))
        used[S["ukv"]] = d
        lat_done = PE.last()
        t_kf, t_vm = [], []
        for tb in range(2):
            kv = kf[:, tb, :].rearrange("p (a b) -> p a b", a=8)
            a = act(kv[:, :, 0:64], ps[bkk[tb][0]][:, :].rearrange("p (a b) -> p a b", a=8), ACT.Copy, d, b0)
            give(bkk[tb][0], a)
            v = act(vm[:, tb, :], ps[bvv[tb][0]][:, :], ACT.Copy, d, b0)
            give(bvv[tb][0], v)
            t_vm.append(v)
            t_kf.append(a)
        for tb in range(2):
            kv = kf[:, tb, :].rearrange("p (a b) -> p a b", a=8)
            t_kf.append(vcopy(kv[:, :, 64:96], krr[:, tb, :].unsqueeze(1).to_broadcast([128, 8, 32]), t_kr, b0))
        t_qT = []
        for src, dst, tk in ((qf, qT, t_qf), (kf, kT2, t_kf)):
            for tb in range(2):
                for c in range(2):
                    b, fr = take()
                    for k in range(4):
                        hd = 4 * c + k
                        d = pe(lambda e, src=src, tb=tb, hd=hd, k=k, b=b: e.transpose(
                            ps[b][0:96, 128 * k:128 * k + 128], src[:, tb, 96 * hd:96 * hd + 96], C(C_ID)),
                            tk, fr, inc=(k == 3))
                    a = act(dst[0:96, 4 * c:4 * c + 4, 128 * tb:128 * tb + 128],
                            ps[b][0:96, :].rearrange("p (k n) -> p k n", k=4), ACT.Copy, d, b0)
                    give(b, a)
                    t_qT.append(a)

        ml_pv = []

        def ml_scores(i, o, fr):
            return logits(o, qT[0:96, i, :], kT2[0:96, i, :], fr, t_qT)

        def ml_finish(i, p, r, tok):
            n = norm_p(p, r, tok)
            o = PT[:, i % 2, :]
            d, t = turn(p, o, n, ml_pv[-2:-1], b0)
            b, fr = take()
            c = slice(128 * (i // 2), 128 * (i // 2) + 128)
            mm(ps[b][:, 0:128], vm[:, 0, c], o[:, 0:128], True, True, t, t_vm, fr)
            mm(ps[b][:, 128:256], vm[:, 0, c], o[:, 128:256], True, False)
            e = mm(ps[b][:, 128:256], vm[:, 1, c], o[:, 256:384], False, True, inc=True)
            ml_pv.append(e)
            pr = slice(64 * (i % 2), 64 * (i % 2) + 64)
            x = act(xf[pr, i // 2, :], ps[b][pr, 0:256], ACT.Copy, e, lat_gone)
            give(b, x)
            return [d, x]

        attention(8, ml_scores, 96.0 ** -0.5, ml_finish, Pm, PT, b0)
        t_x = hilo_all(bar())
        stp = Step(add_banks, P("nf0", 0, 8))
        proj_out(S["aout"], t_x[0], lambda: t_x[1], stp.early, stp.late)
        nxt = Step(add_banks, P("nm1", 0, 8))
        ffn(S["f0"], True, stp, nxt)
        stp = nxt

        b0 = bar()
        sc = Scratch()
        xp = sc(8, 259)
        xb = sc(8, 256)
        xs = sc(2, 512)
        sz = sc(2, 512)
        cbs = sc(2, 384)
        Eb = hsf[:, 0:768].rearrange("p (a b) -> p a b", a=2)
        Mb = hsf[:, 768:1536].rearrange("p (a b) -> p a b", a=2)
        At = sc(2, 40)
        dr = sc(4, 256)
        T2 = sc(256)
        y = sc(2, 512)
        wdt = sc(8, 8)
        z3 = [pool(lambda e: e.memset(xp[:, :, 0:3], 0.0), b0), pool(lambda e: e.memset(T2, 0.0), b0)]
        t_wd = dma("wdt", wdt, sw[:, 1536:1544].rearrange("(k p) n -> p k n", p=128), b0, q=GP)

        w_z, t_x = wide(["z"], stp.late(0), lambda: stp.late(1))
        x_in = bar()
        t_sz = []
        for tb in range(2):
            b, d = w_z["z"][tb]
            t_sz.append(act(sz[:, tb, :], ps[b][:, :], ACT.Silu, d, b0))
            give(b, t_sz[-1])
        b, fr = take()
        for k in range(8):
            d = mm(ps[b][0:8, 0:256], wdt[:, k, :], xf[:, k, :], k == 0, k == 7, t_wd, t_x, fr, inc=(k == 7))
        R = slice(0, 8)
        t1 = ts(dr[R, 0, :], ps[b][R, 0:256], P("dtb")[R], None, ALU.add, None, d, b0)
        give(b, t1)
        t_dt = softplus(dr[R, 0, :], dr[R, 1, :], dr[R, 2, :], dr[R, 3, :], junk[R, 0:256], t1, bar())
        t1 = act(st[R, 61:62], P("alog")[R], ACT.Exp, b0)
        t1 = ts(dr[R, 1, :], dr[R, 0, :], st[R, 61:62], -1.0, ALU.mult, ALU.mult, t1, t_dt)
        t2 = vec(lambda e: e.memset(dr[R, 2, :], 1.0), t_dt)
        t_A = [vec(lambda e: e.tensor_tensor_scan(T2[R, :], dr[R, 2, :], dr[R, 1, :], 0.0, ALU.mult, ALU.add), t1, t2, z3),
               vcopy(T2[32:40, :], dr[R, 0, :], t_dt, z3)]
        t_xb = []
        for i in range(4):
            b, d = bank_feat(S["xbc"][i], t_x)
            a = act(xp[:, 2 * i:2 * i + 2, 3:259], ps[b][:, :].rearrange("p (t n) -> p t n", t=2), ACT.Copy, d, z3)
            give(b, a)
            for t in (2 * i, 2 * i + 1):
                c = ts(xb[:, t, :], xp[:, t, 0:256], P("cw", 4 * t), None, ALU.mult, None, a, b0)
                for k in (1, 2, 3):
                    c = stt(xb[:, t, :], xp[:, t, k:k + 256], P("cw", 4 * t + k), xb[:, t, :], ALU.mult, ALU.add, c)
                t_xb.append(act(xb[:, t, :], xb[:, t, :], ACT.Silu, c, bias=P("cb", t)))
        t_at, t_xs = [], []
        for tb in range(2):
            b, fr = take()
            s = slice(128 * tb, 128 * tb + 128)
            d = pe(lambda e, b=b, s=s: e.transpose(ps[b][:, 0:128], T2[:, s], C(C_ID)), t_A, fr)
            a = ts(At[:, tb, 0:8], ps[b][:, 0:8], -1.0, None, ALU.mult, None, d, b0)
            a = vcopy(At[:, tb, 32:40], ps[b][:, 32:40], d)
            give(b, a)
            t_at.append(a)
            b, fr = take()
            for k in range(4):
                d = pe(lambda e, b=b, s=s, k=k: e.transpose(ps[b][:, 128 * k:128 * k + 128], xb[:, k, s], C(C_ID)),
                       t_xb, fr, inc=(k == 3))
            a = act(xs[:, tb, :], ps[b][:, :], ACT.Copy, d, b0)
            give(b, a)
            t_xs.append(a)
        t_cb = []
        for g in range(2):
            b, fr = take()
            mm(ps[b][:, 0:256], xb[:, 4 + g, 0:128], xb[:, 6 + g, :], True, True, t_xb, fr)
            d = mm(ps[b][:, 256:384], xb[:, 4 + g, 128:256], xb[:, 6 + g, 128:256], True, True, inc=True)
            a = act(cbs[:, g, :], ps[b][:, 0:384], ACT.Copy, d, b0)
            give(b, a)
            t_cb.append(a)
        by = [take() for _ in range(2)]
        fry = [x[1] for x in by]
        seg, m_gone = {}, {}

        def ssd_seg(i):
            b, fr = take()
            sel = cst[:, C_SEL + 128 * i:C_SEL + 128 * i + 128]
            o = ps[b]
            mm(o[:, 0:256], sel, T2, True, False, t_A, fr)
            mm(o[:, 0:128], idb[:, :], mtb[:, :], False, True, t_m)
            mm(o[:, 256:384], sel, T2[:, 128:256], True, False)
            d = mm(o[:, 256:384], idb[:, :], mtb[:, :], False, True, inc=True)
            a = [act(Eb[:, i % 2, 0:256], o[:, 0:256], ACT.Exp, d, t_at, x_in, m_gone.get(i - 2), bias=At[:, 0, i:i + 1]),
                 act(Eb[:, i % 2, 256:384], o[:, 256:384], ACT.Exp, bias=At[:, 1, i:i + 1])]
            give(b, a[-1])
            return a

        def ssd_out(i, a):
            e, m, g = Eb[:, i % 2, :], Mb[:, i % 2, :], i // 4
            k = [stt(m[:, 0:256], e[:, 0:256], At[:, 0, 32 + i:33 + i], cbs[:, g, 0:256], ALU.mult, ALU.mult, a, t_cb, t_at,
                     m_gone.get(i - 2)),
                 stt(m[:, 256:384], e[:, 256:384], At[:, 1, 32 + i:33 + i], cbs[:, g, 256:384], ALU.mult, ALU.mult, a)]
            c = slice(64 * i, 64 * i + 64)
            mm(ps[by[0][0]][:, c], m[:, 0:128], xs[:, 0, c], True, True, k, t_xs, fry)
            mm(ps[by[1][0]][:, c], m[:, 128:256], xs[:, 0, c], True, False)
            d = mm(ps[by[1][0]][:, c], m[:, 256:384], xs[:, 1, c], False, True, inc=True)
            m_gone[i] = [k, d]
            return d

        for i in range(9):
            if i < 8:
                seg[i] = ssd_seg(i)
            if i >= 1:
                d = ssd_out(i - 1, seg.pop(i - 1))
        x_used = bar()
        for tb in range(2):
            yt = y[:, tb, :]
            a = tt(yt.rearrange("p (a b) -> p a b", a=8), xs[:, tb, :].rearrange("p (a b) -> p a b", a=8),
                   srow[:, 0:8].unsqueeze(2).to_broadcast([128, 8, 64]), ALU.mult, t_xs, t_sr, b0)
            a = tt(yt, yt, ps[by[tb][0]][:, :], ALU.add, a, d)
            give(by[tb][0], a)
            a = tt(yt, yt, sz[:, tb, :], ALU.mult, a, t_sz)
            q = [square(yt[:, 256 * g:256 * g + 256], st[:, 2 * tb + g:2 * tb + g + 1], 1.0, a, x_used) for g in range(2)]
            r = rstd(st[:, 4 + 2 * tb:6 + 2 * tb], st[:, 2 * tb:2 * tb + 2], 256, q)
            a = tt(yt.rearrange("p (a b) -> p a b", a=2), yt.rearrange("p (a b) -> p a b", a=2),
                   st[:, 4 + 2 * tb:6 + 2 * tb].unsqueeze(2).to_broadcast([128, 2, 256]), ALU.mult, r)
            t_y = to_xf(yt, 4, 0, tb, P("s_norm", 0, 4), a, x_used)

        b0 = bar()
        sc = Scratch()
        hq = sc(4, 256)
        hk = sc(4, 256)
        G = sc(4, 256)
        hiv = sc(2, 512)
        shg = sc(2, 512)
        Dd = sc(4, 256)
        QK = sc(2, 1024)
        STt = sc(8, 128)
        tm = hs[:, 0, :].rearrange("p (a b) -> p a b", a=8)
        ST2 = sc(4, 128)
        ov = sc(2, 512)
        hm = hs[:, 1, :].rearrange("p (a b) -> p a b", a=8)
        t_hm = dma("hm", hm, D["hmask"], b0, q=GP)
        lb = tt(st[:, 12:16], P("lb1", 0, 4), P("lb0", 0, 4), ALU.subtract, b0)
        lb = act(st[:, 8:12], st[:, 12:16], ACT.Sigmoid, lb, b0)
        lb = [lb, act(st[:, 16:20], st[:, 12:16], ACT.Sigmoid, lb, scale=-1.0)]
        t_hq, t_hf = [], []
        for i in range(2):
            b, d = bank_feat(S["hq"][i], t_x)
            t_hq.append(act(hq[:, 2 * i:2 * i + 2, :], ps[b][:, :].rearrange("p (t n) -> p t n", t=2), ACT.Silu, d, b0))
            give(b, t_hq[-1])
        for i in range(2):
            b, d = bank_feat(S["hf"][i], t_x)
            v = ps[b][:, :].rearrange("p (t n) -> p t n", t=2)
            a = act(G[:, 2 * i:2 * i + 2, :], v, ACT.Sigmoid, d, b0)
            a2 = act(hk[:, 2 * i:2 * i + 2, :], v, ACT.Sigmoid, d, b0, scale=-1.0)
            give(b, a2)
            for t in (2 * i, 2 * i + 1):
                t_hf.append(ts(G[:, t, :], G[:, t, :], st[:, 16 + t:17 + t], st[:, 8 + t:9 + t], ALU.mult, ALU.add, a, lb))
                t_hf.append(ts(hk[:, t, :], hk[:, t, :], st[:, 16 + t:17 + t], None, ALU.mult, None, a2, lb))
        w_hi, _ = wide(["hi"], t_x, lambda: t_x)
        t_hi = []
        for tb in range(2):
            b, d = w_hi["hi"][tb]
            t_hi.append(act(hiv[:, tb, :], ps[b][:, :], ACT.Copy, d, b0))
            give(b, t_hi[-1])
        w_hg, _ = wide(["hg"], t_x, lambda: t_x)
        t_hg = []
        for tb in range(2):
            b, d = w_hg["hg"][tb]
            t_hg.append(act(shg[:, tb, :], ps[b][:, :], ACT.Silu, d, b0))
            give(b, t_hg[-1])
        x_gone = PE.last()
        a = ts(G, G, 1e-18, None, ALU.max, None, t_hf)
        a = act(Dd, G, ACT.Ln, a, b0)
        o1 = vec(lambda e: e.memset(tm.rearrange("p a b -> p (a b)")[:, 0:256], 1.0), b0)
        t_G = [vec(lambda e, t=t: e.tensor_tensor_scan(G[:, t, :], tm.rearrange("p a b -> p (a b)")[:, 0:256], Dd[:, t, :],
                                                       0.0, ALU.mult, ALU.add), a, o1) for t in range(4)]
        qk_gone = {}
        qk_free = [None, None]
        Gf, Df, qf_, kf_ = (x.rearrange("p a b -> p (a b)") for x in (G, Dd, hq, hk))
        d_gone = [t_G]
        acc = None
        t_s2 = None
        for n, m in enumerate([128] + LEVELS + [0]):
            if m:
                nb = 1024 // (2 * m)
                g3, d3, q3, k3 = (x.rearrange("p (b m) -> p b m", m=2 * m) for x in (Gf, Df, qf_, kf_))
                o = QK[:, n % 2, :]
                o3 = o.rearrange("p (b m) -> p b m", m=2 * m)
                ref = g3[:, :, m - 1:m].to_broadcast([128, nb, m])
                a = [tt(d3[:, :, 0:m], ref, g3[:, :, 0:m], ALU.subtract, t_G, d_gone),
                     tt(d3[:, :, m:2 * m], g3[:, :, m:2 * m], ref, ALU.subtract, t_G, d_gone)]
                x = act(Df, Df, ACT.Exp, a)
                k = [tt(o3[:, :, 0:m], k3[:, :, 0:m], d3[:, :, 0:m], ALU.mult, x, t_hf, qk_free[n % 2], b0),
                     tt(o3[:, :, m:2 * m], q3[:, :, m:2 * m], d3[:, :, m:2 * m], ALU.mult, x, t_hq)]
                d_gone = k
                s_, l_ = o.rearrange("p (h n) -> p h n", h=4), o.rearrange("p (h n) -> p h n", h=4)
            else:
                s_, l_, k = hk, hq, [t_hq, t_hf]
            if m == 128:
                b, fr = take()
                for hd in range(4):
                    d = mm(ps[b][:, 128 * hd:128 * hd + 128], s_[:, hd, 0:128], l_[:, hd, 128:256], True, True, k, fr,
                           inc=(hd == 3))
                t_s2 = act(ST2, ps[b][:, :].rearrange("p (h n) -> p h n", h=4), ACT.Copy, d, b0)
                give(b, t_s2)
                qk_free[n % 2] = d
                continue
            for tb in range(2):
                b, fr = take()
                c = slice(128 * tb, 128 * tb + 128)
                for hd in range(4):
                    d = mm(ps[b][:, 128 * hd:128 * hd + 128], s_[:, hd, c], l_[:, hd, c], True, True, k, fr, inc=(hd == 3))
                v = ps[b][:, :].rearrange("p (h n) -> p h n", h=4)
                mk = hm[:, n - 1, :].unsqueeze(1).to_broadcast([128, 4, 128])
                z = slice(4 * tb, 4 * tb + 4)
                if n == 1:
                    acc_n = tt(STt[:, z, :], v, mk, ALU.mult, d, t_hm, b0)
                    give(b, acc_n)
                else:
                    a = tt(tm[:, z, :], v, mk, ALU.mult, d, t_hm, t_G, acc)
                    give(b, a)
                    acc_n = tt(STt[:, z, :], STt[:, z, :], tm[:, z, :], ALU.add, a, acc)
                acc = [acc, acc_n]
            acc = acc_n
            qk_free[n % 2] = d
        bo = [take() for _ in range(2)]
        fro = [x[1] for x in bo]
        for hd in range(4):
            c = slice(128 * hd, 128 * hd + 128)
            mm(ps[bo[0][0]][:, c], STt[:, hd, :], hiv[:, 0, c], True, True, acc, t_hi, fro, t_s2)
            mm(ps[bo[1][0]][:, c], ST2[:, hd, :], hiv[:, 0, c], True, False)
            d = mm(ps[bo[1][0]][:, c], STt[:, 4 + hd, :], hiv[:, 1, c], False, True, inc=True)
        w = bar()
        for tb in range(2):
            v = ps[bo[tb][0]][:, :]
            q = act(ov[:, tb, :], v, ACT.Square, d, b0)
            r = vec(lambda e, tb=tb: e.tensor_reduce(st[:, 20 + 4 * tb:24 + 4 * tb],
                                                     ov[:, tb, :].rearrange("p (a b) -> p a b", a=4), AX, ALU.add), q, w)
            r = rstd(st[:, 28 + 4 * tb:32 + 4 * tb], st[:, 20 + 4 * tb:24 + 4 * tb], 128, r, w)
            a = tt(ov[:, tb, :].rearrange("p (a b) -> p a b", a=4), v.rearrange("p (a b) -> p a b", a=4),
                   st[:, 28 + 4 * tb:32 + 4 * tb].unsqueeze(2).to_broadcast([128, 4, 128]), ALU.mult, r)
            give(bo[tb][0], a)
            a = tt(ov[:, tb, :], ov[:, tb, :], shg[:, tb, :], ALU.mult, a, t_hg)
            t_o = to_xf(ov[:, tb, :], 4, 4, tb, P("g_norm"), a, w)
        t_x = hilo_all(bar())
        stp = Step(add_banks, P("nf1", 0, 8))
        proj_out(S["sout"], t_x[0], lambda: t_x[1], stp.early, stp.late)

        t_out = []

        class Last:
            def late(self, tb):
                pass

            def early(self, tb, bk, d):
                toks = add_banks(tb, bk, d)
                r = rms_of([(h[:, tb, c], t) for c, t in zip(HALF, toks)], 3 * tb)
                for i, c in enumerate(HALF):
                    m = stt(hs[:, tb, c], h[:, tb, c], st[:, 3 * tb + 2:3 * tb + 3], rows[:, 1, c], ALU.mult, ALU.mult,
                            r, t_r1, toks)
                    t_out.append(dma(f"out{tb}{i}", out[128 * tb:128 * tb + 128, c], hs[:, tb, c], m))

        ffn(S["f1"], True, stp, Last())
        assert len(used) == len(slots), (len(used), len(slots))

        block = ctx.enter_context(nc.Block())

        @block.sync
        def _(eng):
            SP.replay(eng)
            for s, c in t_out:
                eng.wait_ge(s, c)

        @block.tensor
        def _(eng):
            PE.replay(eng)

        @block.scalar
        def _(eng):
            AC.replay(eng)

        @block.vector
        def _(eng):
            VE.replay(eng)

        @block.gpsimd
        def _(eng):
            GP.replay(eng)


def constants():
    f = np.float32
    i = np.arange(128)
    c = np.zeros((128, C_N), f)
    c[:, C_ID:C_ID + 128] = np.eye(128, dtype=f)
    c[:, C_MA:C_MA + 128] = np.where(i[None, :] > i[:, None], f(NEG), f(0))
    c[:, C_MT:C_MT + 128] = np.where(i[None, :] < i[:, None], f(NEG), f(0))
    c[:, C_ONE:C_ONE + 128] = f(1.0 / 256)
    for n in range(8):
        c[n, C_SEL + 128 * n:C_SEL + 128 * n + 128] = 1
    pos = np.arange(256, dtype=f)
    for dim, at in ((32, 0), (64, 32)):
        inv = (f(1) / np.power(f(10000.0), np.arange(0, dim, 2, dtype=f) / f(dim))).astype(f)
        ang = (pos[:, None] * inv[None, :]).astype(f)
        for tb in range(2):
            a = ang[128 * tb:128 * tb + 128]
            o = C_ROPE + 96 * tb + at
            c[:, o:o + dim // 2] = np.cos(a)
            c[:, o + dim // 2:o + dim] = np.sin(a)
    t = np.arange(256)
    band = np.zeros((256, 4, 256), f)
    for g, w in enumerate((2, 4, 8, 16)):
        inside = (t[:, None] <= t[None, :]) & (t[:, None] > t[None, :] - w)
        band[:, g, :] = np.where(inside, f(1) / np.minimum(t + 1, w).astype(f)[None, :], f(0)) - np.eye(256, dtype=f)
    band = np.ascontiguousarray(band.reshape(2, 128, 4, 256).transpose(1, 2, 0, 3))
    hm = np.zeros((128, 8, 128), f)
    for n, m in enumerate(LEVELS):
        same = i[:, None] // (2 * m) == i[None, :] // (2 * m)
        hm[:, n, :] = same & ((i[:, None] // m) % 2 == 0) & ((i[None, :] // m) % 2 == 1)
    hm[:, 7, :] = np.eye(128)
    return c, band, hm


def kernel(**inputs):
    import concourse.bacc as bacc
    from concourse.bass_utils import run_bass_kernel_spmd as run

    a = {k: np.asarray(v) for k, v in inputs.items()}
    prm = np.zeros((128, P_N), np.float32)

    def put(name, v, j=0):
        v = np.asarray(v)
        prm[0:v.shape[0], P_AT[name] + j:P_AT[name] + j + v.shape[1]] = v

    def tiles(v):
        return v.reshape(-1, 128).T

    for name, src in (("g_mix_pre", a["g_mix_pre"][0]), ("g_mlp_pre", a["g_mlp_pre"][0]), ("g_ple_pre", a["g_ple_pre"][0]),
                      ("nm0", a["norm_mix_2"][0]), ("nm1", a["norm_mix_2"][1]), ("nf0", a["norm_ffn_2"][0]),
                      ("nf1", a["norm_ffn_2"][1]), ("ln_g", a["conf_ln_g"][0]), ("ln_b", a["conf_ln_b"][0]),
                      ("pool_scale", a["pool_scale"][0]), ("cb", a["s_conv_b_2"][0]), ("qn", a["a_q_norm_2"][0]),
                      ("kvn", a["a_kv_norm_2"][0]), ("subln", a["a_subln_2"][0]), ("s_norm", a["s_norm_2"][0]),
                      ("g_norm", a["h_g_norm_2"][0]), ("lb0", a["h_lower_bound_2"][0]), ("lb1", a["h_lower_bound_2"][1])):
        put(name, tiles(src))
    for name, src in (("dw", a["w_conf_dw"][0]), ("sc", a["w_sc"][0]), ("cw", a["s_conv_w_2"][0])):
        k, n = src.shape
        put(name, src.reshape(k, n // 128, 128).transpose(2, 1, 0).reshape(128, -1))
    prm[0:4, P_AT["bf"]] = a["b_forget"][0]
    prm[32:36, P_AT["bf"]] = a["b_forget"][0]
    prm[0:8, P_AT["dtb"]] = a["s_dt_bias_2"][0]
    prm[0:8, P_AT["alog"]] = a["s_a_log_2"][0]
    for i in range(4):
        prm[i, P_AT["fsel"] + i] = prm[32 + i, P_AT["fsel"] + i] = 1
    prm[:, P_AT["eps"]] = EPS
    prm[:, P_AT["mhalf"]:P_AT["mhalf"] + 4] = -0.5
    srow = np.concatenate([a["s_d_2"][0], a["a_lq1_2"][0], a["a_lk1_2"][0], a["a_lq2_2"][0], a["a_lk2_2"][0]])
    cst, band, hm = constants()
    arrays = {"x": a["x"][0], "pT": np.ascontiguousarray(a["p"][0, 0].T), "prm": prm, "srow": srow, "cst": cst,
              "band": band, "hmask": hm, "w_pool": a["w_pool"][0], "norm_final_2": a["norm_final_2"]}
    for n in ("w_in", "w_conf_pw", "w_out", "w_up", "w_down", "w_ple_gate", "w_ple_proj", "g_mix_post", "g_mlp_post",
              "g_ple_post", "a_w_in_2", "a_w_uq_2", "a_w_ukv_2", "a_w_out_2", "s_w_in_2", "s_w_out_2"):
        arrays[n] = a[n][0]
    for n in ("ffn_gate", "ffn_up", "ffn_down"):
        for l in range(2):
            arrays[f"{n}_{l}"] = a[n + "_2"][l]
    nc = bacc.Bacc("TRN2", target_bir_lowering=False, num_devices=1)
    D, feed = {}, {}
    for n, v in arrays.items():
        v = np.ascontiguousarray(v)
        D[n] = nc.dram_tensor("in_" + n, v.shape, F32, kind="ExternalInput").ap()
        feed["in_" + n] = v
    out = nc.dram_tensor("out_0", (256, 1024), F32, kind="ExternalOutput").ap()
    program(nc, D, out)
    r = run(nc, [feed], core_ids=[0])
    return r.results[0]["out_0"].reshape(1, 256, 1024)
```

```python
from collections import namedtuple
from contextlib import ExitStack

import numpy as np

import concourse.bass as bass
from concourse import mybir

ALU = mybir.AluOpType
ACT = mybir.ActivationFunctionType
F32 = mybir.dt.float32
F32R = mybir.dt.float32r
BF16 = mybir.dt.bfloat16
I32 = mybir.dt.int32
AX = mybir.AxisListType.X

EPS = 1e-6
LAMBDA0 = 0.8 - 0.6 * float(np.exp(-0.3 * 0))
NEG = -1e30
NRAW = 3
NW = 4
LAG = 1
SCN = 11136
LEVELS = [64, 32, 16, 8, 4, 2, 1]
SCHEDULE = "LPLPLPLPLSPLPSLSLSLSLSLSLSSSESESEESS"
TAPS = 31

C_ID, C_MA, C_MT, C_ONE, C_SEL, C_ROPE = 0, 128, 256, 384, 512, 1536
C_N = C_ROPE + 2 * 96

P_COLS = [("g_mix_pre", 8), ("g_mlp_pre", 8), ("g_ple_pre", 8), ("nm0", 8), ("nm1", 8), ("nf0", 8), ("nf1", 8),
          ("dw", 2 * TAPS), ("ln_g", 2), ("ln_b", 2), ("sc", 6), ("pool_scale", 2), ("cw", 32), ("cb", 8),
          ("qn", 3), ("kvn", 2), ("subln", 1), ("s_norm", 4), ("g_norm", 1), ("lb0", 4), ("lb1", 4),
          ("bf", 1), ("dtb", 1), ("alog", 1), ("fsel", 4), ("eps", 1), ("mhalf", 4)]
P_AT = {}
_at = 0
for _n, _c in P_COLS:
    P_AT[_n] = _at
    _at += _c
P_N = _at


Done = namedtuple("Done", "sem count")


class Queue:

    def __init__(self, sem):
        self.sem, self.n, self.items, self.seen = sem, 0, [], {}

    def emit(self, fn, waits, inc=True):
        need = []
        for sem, count in flat(waits):
            if self.seen.get(id(sem), 0) < count:
                self.seen[id(sem)] = count
                need.append((sem, count))
        if inc:
            self.n += 1
        self.items.append((need, fn, inc))
        return Done(self.sem, self.n)

    def last(self):
        return Done(self.sem, self.n) if self.n else None

    def replay(self, eng):
        for need, fn, inc in self.items:
            for sem, count in need:
                eng.wait_ge(sem, count)
            ins = fn(eng)
            if inc:
                ins.then_inc(self.sem, 1)


def flat(w):
    if w is None:
        return []
    if isinstance(w, Done):
        return [w]
    return [t for x in w for t in flat(x)]


def program(nc, D, out):
    with ExitStack() as ctx:
        def sb(name, shape, dt=F32):
            return ctx.enter_context(nc.sbuf_tensor(name, shape, dt))

        def sem(name):
            return ctx.enter_context(nc.semaphore(name))

        ps = [ctx.enter_context(nc.psum_tensor(f"ps{i}", [128, 512], F32)) for i in range(8)]
        cst = sb("cst", [128, C_N])
        prm = sb("prm", [128, P_N])
        rows = sb("rows", [128, 2, 1024])
        srow = sb("srow", [128, 264])
        h = sb("h", [128, 2, 1024])
        xf = sb("xf", [128, 8, 256])
        xh = sb("xh", [128, 8, 256], F32R)
        xl = sb("xl", [128, 8, 256], F32R)
        hs = sb("hs", [128, 2, 1024])
        hsf = hs[:, :, :].rearrange("p a b -> p (a b)")
        junk = sb("junk", [128, 1024])
        raw = [sb(f"raw{i}", [128, 2048]) for i in range(NRAW)]
        wh = [sb(f"wh{i}", [128, 2048], F32R) for i in range(NW)]
        wl = [sb(f"wl{i}", [128, 2048], F32R) for i in range(NW)]
        at_f = nc.sbuf_base
        fh = sb("fh", [128, 3, 512], F32R)
        fl = sb("fl", [128, 3, 512], F32R)
        fh_f, fl_f = (nc.alloc_sbuf_tensor_at(f"fs{i}", [128, 1536], F32, offset=at_f + 6144 * i) for i in range(2))
        idb = sb("idb", [128, 128], BF16)
        mab = sb("mab", [128, 128], BF16)
        mtb = sb("mtb", [128, 128], BF16)
        st = sb("st", [128, 96])
        at_s = nc.sbuf_base
        SC = sb("SC", [128, SCN])
        phl = [nc.alloc_sbuf_tensor_at(f"ph{i}", [128, 2, 256], F32R, offset=at_s + 4 * (2560 + 512 * i)) for i in range(2)]

        PE, AC, VE, GP = (Queue(sem(n)) for n in ("s_pe", "s_act", "s_dve", "s_pool"))
        SP = Queue(sem("s_sp"))
        s_raw = [sem(f"s_raw{i}") for i in range(NRAW)]
        s_misc = {}

        def pe(fn, *w, inc=True):
            return PE.emit(fn, w, inc)

        def act(o, i, f, *w, **kw):
            return AC.emit(lambda e: e.activation(o, i, f, **kw), w)

        def vec(fn, *w):
            return VE.emit(fn, w)

        def pool(fn, *w):
            return GP.emit(fn, w)

        def dma(name, dst, src, *w, q=None):
            if name not in s_misc:
                s_misc[name] = [sem("d_" + name), 0]
            box = s_misc[name]
            box[1] += 16
            (q or SP).emit(lambda e: e.dma_start(dst, src).then_inc(box[0], 16), w, inc=False)
            return Done(box[0], box[1])

        def tt(o, a, b, op, *w):
            return vec(lambda e: e.tensor_tensor(o, a, b, op), *w)

        def ts(o, a, s1, s2, o1, o2, *w):
            if o2 is None:
                return vec(lambda e: e.tensor_scalar(o, a, s1, None, o1), *w)
            return vec(lambda e: e.tensor_scalar(o, a, s1, s2, o1, o2), *w)

        def stt(o, a, s, b, o1, o2, *w):
            return vec(lambda e: e.scalar_tensor_tensor(o, a, s, b, o1, o2), *w)

        def vcopy(o, a, *w):
            return vec(lambda e: e.tensor_copy(o, a), *w)

        def bar():
            return [q.last() for q in (PE, AC, VE, GP) if q.last()]

        free = [(i, None) for i in range(8)]

        def take():
            return free.pop(0)

        def give(i, tok):
            free.append((i, tok))

        def P(name, i=0, n=1):
            return prm[:, P_AT[name] + i:P_AT[name] + i + n]

        def C(a, n=128):
            return cst[:, a:a + n]

        slots = []

        def slot(src, kt, n):
            slots.append((src, kt, n))
            return len(slots) - 1

        def cols(w, a, n):
            return slot(w.rearrange("(k p) n -> p k n", p=128)[:, :, a:a + n], w.shape[0] // 128, n)

        def krows(w, a, n):
            return slot(w[a * 128:(a + n) * 128, :].rearrange("(k p) n -> p k n", p=128), n, w.shape[1])

        def kcols(w, k, nk, a, n):
            return slot(w[k * 128:(k + nk) * 128, a:a + n].rearrange("(k p) n -> p k n", p=128), nk, n)

        w_in = D["w_in"]
        SEG = {"a": 0, "b": 256, "q": 512, "k": 768, "v": 1024, "h": 1284, "sb": 1540, "c": 1796, "p": 2052}
        S = {}
        for n in ("a", "b", "q", "k", "v", "p", "h", "c", "sb"):
            S[n] = cols(w_in, SEG[n], 256)
        S["out"] = {i: krows(D["w_out"], 2 * i, 2) for i in (3, 2, 0, 1)}

        def mlp_slots(n, ups, down):
            got = [[] for _ in range(n)]
            for j in range(n + 3):
                if j < n:
                    got[j] += [cols(w, 256 * j, 256) for w in ups]
                if j >= 3:
                    got[j - 3] += [krows(down, 2 * (j - 3), 2)]
            return got

        S["ff"] = mlp_slots(16, [D["w_up"]], D["w_down"])
        S["proj"] = krows(D["w_ple_proj"], 0, 2)
        S["gate"] = [krows(D["w_ple_gate"], 2 * i, 2) for i in range(4)]
        aw = D["a_w_in_2"]
        for n, c in (("dq", 672), ("dk", 1184)):
            S[n] = [kcols(aw, 4 * i, 4, c, 512) for i in range(2)]
        S["lat"] = [kcols(aw, 2 * i, 2, 0, 672) for i in range(4)]
        S["dv"] = [kcols(aw, 4 * i, 4, 1696, 512) for i in range(2)]
        S["uq"] = [cols(D["a_w_uq_2"], 384 * i, 384) for i in range(2)]
        S["ukv"] = krows(D["a_w_ukv_2"], 0, 2)
        S["aout"] = {i: krows(D["a_w_out_2"], 2 * i, 2) for i in (2, 3, 0, 1)}

        S["f0"] = mlp_slots(11, [D["ffn_gate_0"], D["ffn_up_0"]], D["ffn_down_0"])
        sw = D["s_w_in_2"]
        S["z"] = [kcols(sw, 4 * i, 4, 0, 512) for i in range(2)]
        S["hi"] = [kcols(sw, 4 * i, 4, 2568, 512) for i in range(2)]
        S["hq"] = [cols(sw, 1544 + 256 * i, 256) for i in range(2)]
        S["hf"] = [cols(sw, 2056 + 256 * i, 256) for i in range(2)]
        S["xbc"] = [cols(sw, 512 + 256 * i, 256) for i in range(4)]
        S["hg"] = [kcols(sw, 4 * i, 4, 3080, 512) for i in range(2)]
        S["sout"] = {i: krows(D["s_w_out_2"], 2 * i, 2) for i in (2, 3, 0, 1)}
        S["f1"] = mlp_slots(11, [D["ffn_gate_1"], D["ffn_up_1"]], D["ffn_down_1"])

        loaded, split_tok, used = [], [], {}
        on_pool = (set(S["uq"]) | set(S["dv"]) | set(S["hg"]) | {S["ukv"], S["aout"][2], S["aout"][3], S["sout"][2], S["sout"][0],
                   S["xbc"][1], S["xbc"][3]})

        def load(i):
            src, kt, n = slots[i]
            r = i % NRAW
            dst = raw[r][:, 0:kt * n].rearrange("p (k n) -> p k n", k=kt)
            free_at = split_tok[i - NRAW] if i >= NRAW else None
            SP.emit(lambda e: e.dma_start(dst, src).then_inc(s_raw[r], 16), [free_at], inc=False)
            loaded.append(Done(s_raw[r], 16 * (i // NRAW + 1)))

        def split(i):
            src, kt, n = slots[i]
            r, b, m = i % NRAW, i % NW, kt * n
            gone = used[i - NW] if i >= NW else None
            hi = act(wh[b][:, 0:m], raw[r][:, 0:m], ACT.Copy, loaded[i], gone)
            lo = (pool if i in on_pool else vec)(lambda e: e.tensor_tensor(
                wl[b][:, 0:m], raw[r][:, 0:m], wh[b][:, 0:m].bitcast(F32), ALU.subtract), loaded[i], gone, hi)
            split_tok.append(lo)
            if i + NRAW < len(slots):
                load(i + NRAW)

        def prefetch(upto):
            while len(split_tok) < min(len(slots), upto + 1):
                split(len(split_tok))

        def flush():
            while len(split_tok) < len(slots) and (len(split_tok) < NW or len(split_tok) - NW in used):
                split(len(split_tok))

        def use(i):
            prefetch(i)
            _, kt, n = slots[i]
            b = i % NW
            v = [t[b][:, 0:kt * n].rearrange("p (k n) -> p k n", k=kt) for t in (wh, wl)]
            return v[0], v[1], split_tok[i]

        def end_use(i, tok):
            used[i] = tok
            prefetch(i - LAG + NW)

        def mm3(o, a, al, b, bl, start, stop, *w, inc=False):
            pe(lambda e: e.matmul(o, a, b, start=start, stop=False, skip_group_check=True), *w, inc=False)
            pe(lambda e: e.matmul(o, al, b, start=False, stop=False, skip_group_check=True), inc=False)
            return pe(lambda e: e.matmul(o, a, bl, start=False, stop=stop, skip_group_check=True), inc=inc)

        def mm(o, a, b, start, stop, *w, inc=False):
            return pe(lambda e: e.matmul(o, a, b, start=start, stop=stop, skip_group_check=True), *w, inc=inc)

        def feat_mm(i, o, *w):
            wH, wL, tok = use(i)
            kt, nt = slots[i][1], slots[i][2] // 128
            for t in range(nt):
                c = slice(128 * t, 128 * t + 128)
                for k in range(kt):
                    done = mm3(o[:, 256 * t:256 * t + 256], wH[:, k, c], wL[:, k, c], xh[:, k, :], xl[:, k, :],
                               k == 0, k == kt - 1, tok, *w, inc=(t == nt - 1 and k == kt - 1))
            end_use(i, done)
            return done

        def tok_part(i, outs, tb, *w, k0=0, first=True, final=True, a=None):
            wH, wL, tok = use(i)
            kt = slots[i][1]
            ah, al = a or (xh, xl)
            s = slice(128 * tb, 128 * tb + 128)
            for n, (o, c) in enumerate(outs):
                for k in range(kt):
                    done = mm3(o, ah[:, k0 + k, s], al[:, k0 + k, s], wH[:, k, c], wL[:, k, c],
                               first and k == 0, final and k == kt - 1, tok, *w,
                               inc=(n == len(outs) - 1 and k == kt - 1))
            return done

        def tok_mm(i, outs, *w, **kw):
            for tb in range(2):
                done = tok_part(i, outs[tb], tb, *w, **kw)
            end_use(i, done)
            return done

        epsc = P("eps")

        def rstd(dst, ss, n, *w):
            k = ss.shape[1]
            a = ts(dst, ss, 1.0 / n, EPS, ALU.mult, ALU.add, *w)
            return pool(lambda e: e.tensor_tensor(dst, dst, P("mhalf", 0, k), ALU.pow), a, t_p)

        def hilo(t0, t1, tb, *w):
            s = slice(128 * tb, 128 * tb + 128)
            a = act(xh[:, t0:t1, s], xf[:, t0:t1, s], ACT.Copy, *w)
            b = tt(xl[:, t0:t1, s], xf[:, t0:t1, s], xh[:, t0:t1, s].bitcast(F32), ALU.subtract, a, *w)
            return [a, b]

        sq_last = [None, None]
        sq_n = [0]

        def square(src, acc, scale, *w):
            i = sq_n[0] % 2
            sq_n[0] += 1
            n = src.shape[1]
            sq_last[i] = act(junk[:, 512 * i:512 * i + n], src, ACT.Square, sq_last[i], *w, scale=scale, accum_out=acc)
            return sq_last[i]

        def rsqrt(dst, *w):
            k = dst.shape[1]
            return pool(lambda e: e.tensor_tensor(dst, dst, P("mhalf", 0, k), ALU.pow), t_p, *w)

        def to_xf(src, nt, t0, tb, gain, tok, *w):
            s = slice(128 * tb, 128 * tb + 128)
            done = []
            for c in range(0, nt, 4):
                m = min(4, nt - c)
                b, fr = take()
                for k in range(m):
                    t = pe(lambda e, k=k, c=c, b=b: e.transpose(ps[b][:, 128 * k:128 * k + 128],
                                                                src[:, 128 * (c + k):128 * (c + k) + 128],
                                                                C(C_ID)), tok, fr, t_c, inc=(k == m - 1))
                g = gain[:, c:c + m] if gain.shape[1] > 1 else gain.to_broadcast([128, m])
                g = g.unsqueeze(2).to_broadcast([128, m, 128])
                v = tt(xf[:, t0 + c:t0 + c + m, s], ps[b][:, 0:128 * m].rearrange("p (k n) -> p k n", k=m), g,
                       ALU.mult, t, *w)
                give(b, v)
                done.append(v)
            return done

        HALF = (slice(0, 512), slice(512, 1024))

        def rms_of(src, at, *w):
            q = [square(x, st[:, at + i:at + i + 1], 1.0 / 32, t, *w) for i, (x, t) in enumerate(src)]
            a = ts(st[:, at + 2:at + 3], st[:, at:at + 1], st[:, at + 1:at + 2], EPS, ALU.add, ALU.add, q)
            return rsqrt(st[:, at + 2:at + 3], a)

        def norm_a(tb, toks):
            r = rms_of([(h[:, tb, c], t) for c, t in zip(HALF, toks)], 3 * tb)
            return [ts(hs[:, tb, c], h[:, tb, c], st[:, 3 * tb + 2:3 * tb + 3], None, ALU.mult, None, r, toks) for c in HALF]

        def norm_b(gain, tb, toks, *w):
            t = [to_xf(hs[:, tb, HALF[i]], 4, 4 * i, tb, gain[:, 4 * i:4 * i + 4], toks[i], *w) for i in range(2)]
            return [hilo(4 * i, 4 * i + 4, tb, t[i], *w) for i in range(2)]

        def add_norm(src, row, row_tok, tb, toks):
            at = 6 + 3 * tb
            r = rms_of(list(zip(src, toks)), at)
            m = [stt(hs[:, tb, c], x, st[:, at + 2:at + 3], row[:, c], ALU.mult, ALU.mult, r, row_tok)
                 for c, x in zip(HALF, src)]
            return m, [tt(h[:, tb, c], h[:, tb, c], hs[:, tb, c], ALU.add, t) for c, t in zip(HALF, m)]

        def proj_out(sl, x0, enter1, early, late):
            bk = [[take() for _ in range(2)] for _ in range(2)]
            x = [x0, None]
            for tb in range(2):
                for i in range(4):
                    if (tb, i) == (0, 3):
                        x[1] = enter1()
                    d = tok_part(sl[i], [(ps[bk[tb][c][0]][:, :], HALF[c]) for c in range(2)], tb, x[tb],
                                 [y[1] for y in bk[tb]], k0=2 * i, first=(i == 0), final=(i == 3))
                    if tb == 1:
                        end_use(sl[i], d)
                        if i == 1:
                            late(0)
                if tb == 1:
                    flush()
                early(tb, bk[tb], d)

        class Split:

            def __init__(self, sl, step):
                self.sl, self.order, self.step, self.x = sl, list(sl), step, {}
                self.acc = [[take() for _ in range(2)] for _ in range(2)]

            def part(self, i, tb):
                acc = self.acc[tb]
                d = tok_part(self.sl[i], [(ps[acc[c][0]][:, :], HALF[c]) for c in range(2)], tb, self.x[i, tb],
                             [x[1] for x in acc], k0=2 * i, first=(i == self.order[0]), final=(i == self.order[-1]))
                if tb == 1:
                    end_use(self.sl[i], d)
                return d

            def finish(self):
                for tb in range(2):
                    for i in self.order[2:]:
                        d = self.part(i, tb)
                        if tb == 1 and i == self.order[2]:
                            self.step.late(0)
                    if tb == 1:
                        flush()
                    self.step.early(tb, self.acc[tb], d)

        def add_banks(tb, bk, d):
            out = []
            for c in range(2):
                o = h[:, tb, HALF[c]]
                out.append(tt(o, o, ps[bk[c][0]][:, :], ALU.add, d))
                give(bk[c][0], out[-1])
            return out

        class Step:

            def __init__(self, add, gain):
                self.add, self.gain, self.a, self.b = add, gain, {}, {}

            def early(self, tb, bk, d):
                self.a[tb] = norm_a(tb, self.add(tb, bk, d))

            def late(self, tb):
                if tb not in self.b:
                    self.b[tb] = norm_b(self.gain, tb, self.a[tb])
                return self.b[tb]

        def normed(row, row_tok):
            def add(tb, bk, d):
                m, t = add_norm([ps[bk[c][0]][:, :] for c in range(2)], row, row_tok, tb, [d, d])
                for c in range(2):
                    give(bk[c][0], m[c])
                return t
            return add

        def softplus(x, a, u, w, l, tok, *more):
            t = act(a, x, ACT.Abs, tok, *more)
            t = act(u, a, ACT.Exp, t, *more, scale=-1.0)
            t1 = ts(w, u, 1.0, None, ALU.add, None, t)
            t2 = act(l, w, ACT.Ln, t1, *more)
            t = ts(a, w, -1.0, None, ALU.add, None, t1)
            t = tt(a, u, a, ALU.subtract, t)
            t2 = vec(lambda e: e.reciprocal(w, w), t2)
            t = tt(a, a, w, ALU.mult, t, t2)
            t = tt(a, a, l, ALU.add, t)
            return stt(x, x, 0.0, a, ALU.max, ALU.add, t)

        class Scratch:
            def __init__(self):
                self.at = 0

            def __call__(self, *dims):
                n = int(np.prod(dims))
                v = SC[:, self.at:self.at + n]
                self.at += n
                assert self.at <= SCN, self.at
                if len(dims) == 2:
                    v = v.rearrange("p (a b) -> p a b", a=dims[0])
                if len(dims) == 3:
                    v = v.rearrange("p (a b c) -> p a b c", a=dims[0], b=dims[1])
                return v

        t_h = [dma(f"h{tb}", h[:, tb, :], D["x"][128 * tb:128 * tb + 128, :]) for tb in range(2)]
        t_p = dma("prm", prm[:, :], D["prm"])
        t_c = dma("ident", cst[:, 0:128], D["cst"][:, 0:128])
        for i in range(NRAW):
            load(i)
        sc = Scratch()
        wf = sc(8, 36)
        band = sc(4, 2, 256)
        wpw = sc(2, 256)
        wpb = sc(2, 128)
        upad = sc(2, 30 + 256)
        cacc = sc(2, 256)
        csq = sc(2, 256)
        sg = sc(512)
        qm = sc(4, 256)
        kT = sc(2, 256)
        vs = sc(2, 256)
        hsb = sc(512)
        cpad = sc(2, 2 + 256)
        scv = sc(2, 256)
        pv = sc(2, 256)
        dT = sc(2, 256)
        NCt = sc(256)
        CQ = sc(256)
        rk = sc(3, 256)
        ft = hsf[:, 0:1024].rearrange("p (a b) -> p a b", a=4)
        Pm = hsf[:, 0:1536].rearrange("p (a b) -> p a b", a=4)
        PT = fh_f[:, 0:1152].rearrange("p (a b) -> p a b", a=3)
        def bank_feat(sl, *w):
            b, fr = take()
            return b, feat_mm(sl, ps[b], *w, fr)

        def bank_mm(name):
            return bank_feat(S[name], t_x)

        def bank_tok(sl, n, *w):
            b, fr = take()
            return b, tok_mm(sl, [[(ps[b][:, 256 * tb:256 * tb + n], slice(0, n))] for tb in range(2)], *w, fr)

        def both(x):
            return [x.late(0), x.late(1)]

        stp = Step(lambda tb, bk, d: [t_h[tb], t_h[tb]], P("g_mix_pre", 0, 8))
        for tb in range(2):
            stp.early(tb, None, None)
        t_k = dma("cst", cst[:, 128:C_N], D["cst"][:, 128:C_N], q=GP)
        z1 = [pool(lambda e: e.memset(wf, 0.0)), pool(lambda e: e.memset(wpb, 0.0)), pool(lambda e: e.memset(upad, 0.0)),
              pool(lambda e: e.memset(qm, 0.0)), pool(lambda e: e.memset(cpad, 0.0)), pool(lambda e: e.memset(NCt, 0.0)),
              pool(lambda e: e.memset(CQ, 0.0))]
        wfv = w_in[:, 1280:1284].rearrange("(k p) n -> p k n", p=128)
        t_wf = [dma("wf0", wf[:, :, 0:4], wfv, z1, q=GP), dma("wf1", wf[:, :, 32:36], wfv, z1, q=GP)]
        t_bd = dma("band", band, D["band"], q=GP)
        t_pw = dma("pw", wpw, D["w_conf_pw"].rearrange("(k p) n -> p k n", p=128), q=GP)
        t_wp = [dma(f"wp{g}", wpb[64 * (g % 2):64 * (g % 2) + 64, g // 2, 64 * (g % 2):64 * (g % 2) + 64],
                    D["w_pool"][g], z1, q=GP) for g in range(4)]

        t_r0 = dma("row0", rows[:, 0, :], D["g_mix_post"].partition_broadcast(128), q=GP)
        t_r1 = dma("row1", rows[:, 1, :], D["g_mlp_post"].partition_broadcast(128), q=GP)
        t_sr = dma("srow", srow[:, :], D["srow"].partition_broadcast(128), q=GP)
        stp.late(0)
        prefetch(0)
        t_x = both(stp)
        ba, da = bank_mm("a")
        bb, db = bank_mm("b")
        t_m = [act(o[:, :], C(c), ACT.Copy, t_c, t_k) for o, c in ((idb, C_ID), (mab, C_MA), (mtb, C_MT))]
        t1 = act(sg, ps[bb][:, :], ACT.Sigmoid, db)
        give(bb, t1)
        t_u = tt(upad[:, :, 30:286], ps[ba][:, :].rearrange("p (t n) -> p t n", t=2),
                 sg.rearrange("p (t n) -> p t n", t=2), ALU.mult, t1, da, z1)
        give(ba, t_u)
        conv_tok = [t_u, t_u]

        def conv_steps():
            cut = 25
            g, a, gone, g0 = None, None, {}, None
            ring = fl_f[:, 0:1536].rearrange("p (a b) -> p a b", a=6)

            def src(t, k):
                return upad[:, t, k:k + 256], P("dw", TAPS * t + k)

            for k in range(TAPS):
                x, w = src(1, k)
                o = cacc[:, 1, :] if k == 0 else ring[:, k % 6, :]
                a = act(o, x, ACT.Identity, t_u, t_p, gone.get(k - 6), scale=w)
                if k:
                    g = pool(lambda e, o=o: e.tensor_tensor(cacc[:, 1, :], cacc[:, 1, :], o, ALU.add), a, g, first)
                    gone[k] = g
                else:
                    first = a
                if k < cut:
                    x, w = src(0, k)
                    o = cacc[:, 0, :]
                    if k == 0:
                        v = ts(o, x, w, None, ALU.mult, None, t_u, t_p)
                    else:
                        v = stt(o, x, w, o, ALU.mult, ALU.add, v)
                if k % 5 == 4:
                    kk = cut + k // 5
                    x, w = src(0, kk)
                    o = csq[:, min(1, kk - cut), :]
                    g0 = pool(lambda e, x=x, w=w, o=o: e.tensor_scalar(o, x, w, None, ALU.mult), t_u, t_p, g0)
                    if kk > cut:
                        g0 = pool(lambda e: e.tensor_tensor(csq[:, 0, :], csq[:, 0, :], csq[:, 1, :], ALU.add), g0)
                yield
            conv_tok[1] = g
            conv_tok[0] = tt(cacc[:, 0, :], cacc[:, 0, :], csq[:, 0, :], ALU.add, v, g0)
            yield

        conv = conv_steps()

        def advance(gen, n):
            for _ in range(n):
                if next(gen, 0) is None:
                    continue
                return

        advance(conv, 5)
        b, fr = take()
        for k in range(8):
            d = mm(ps[b][0:36, 0:256], wf[:, k, :], xf[:, k, :], k == 0, k == 7, t_wf, t_x, fr, inc=(k == 7))
        R = slice(0, 36)
        fx, fa, fu, fw = (ft[R, i, :] for i in range(4))
        t1 = ts(fx, ps[b][R, 0:256], P("bf")[R], -1.0, ALU.add, ALU.mult, d)
        give(b, t1)
        logf = softplus(fx, fa, fu, fw, junk[R, 0:256], t1, sq_last[0], sq_last[1])
        t1 = ts(fx, fx, -1.0, None, ALU.mult, None, logf)
        t2 = vec(lambda e: e.memset(fu, 1.0), logf)
        t_scan = vec(lambda e: e.tensor_tensor_scan(fa, fu, fx, 0.0, ALU.mult, ALU.add), t1, t2)
        F4, G4 = slice(0, 4), slice(32, 36)
        t_cq = [vcopy(CQ[F4, :], ft[F4, 1, :], t_scan, z1),
                vec(lambda e: e.memset(CQ[G4, :], 1.0), z1),
                ts(NCt[G4, :], ft[G4, 1, :], -1.0, None, ALU.mult, None, t_scan, z1),
                vec(lambda e: e.memset(NCt[F4, :], 1.0), z1)]
        x_gone = PE.last()
        bq, dq_ = bank_mm("q")
        t_q = []
        for i in range(2):
            pr = slice(64 * i, 64 * i + 64)
            t_q.append(act(qm.rearrange("p (t i) n -> p t i n", i=2)[pr, :, i, :],
                           ps[bq][pr, :].rearrange("p (t n) -> p t n", t=2), ACT.Copy, dq_, z1, scale=0.125))
        give(bq, t_q[-1])
        advance(conv, 5)
        bk_, dk_ = bank_mm("k")
        t_k = act(kT, ps[bk_][:, :].rearrange("p (t n) -> p t n", t=2), ACT.Copy, dk_)
        give(bk_, t_k)
        advance(conv, 4)

        advance(conv, 5)
        b, d = bank_tok(S["v"], 256, t_x)
        t_v = act(vs, ps[b][:, :].rearrange("p (t n) -> p t n", t=2), ACT.Copy, d)
        give(b, t_v)
        advance(conv, 5)

        t_conf = []

        def conformer():
            yield
            b, fr = take()
            for t in range(2):
                d = mm(ps[b][:, 0:256], C(C_ONE), cacc[:, t, :], t == 0, t == 1, conv_tok, fr, t_m, inc=(t == 1))
            t1 = tt(cacc, cacc, ps[b][:, 0:256].unsqueeze(1).to_broadcast([128, 2, 256]), ALU.subtract, d)
            give(b, t1)
            t2 = tt(csq, cacc, cacc, ALU.mult, t1)
            yield
            b, fr = take()
            for t in range(2):
                d = mm(ps[b][:, 0:256], C(C_ONE), csq[:, t, :], t == 0, t == 1, t2, fr, inc=(t == 1))
            t1 = act(sg[:, 0:256], ps[b][:, 0:256], ACT.Sqrt, d, bias=epsc)
            give(b, t1)
            t1 = vec(lambda e: e.reciprocal(sg[:, 0:256], sg[:, 0:256]), t1)
            t1 = tt(cacc, cacc, sg[:, 0:256].unsqueeze(1).to_broadcast([128, 2, 256]), ALU.mult, t1)
            t2 = [act(csq[:, t, :], cacc[:, t, :], ACT.Silu, t1, scale=P("ln_g", t), bias=P("ln_b", t)) for t in range(2)]
            yield
            b, fr = take()
            for t in range(2):
                for k in range(2):
                    d = mm(ps[b][:, 256 * t:256 * t + 256], wpw[:, k, 128 * t:128 * t + 128], csq[:, k, :], k == 0, k == 1,
                           t2, fr, t_pw, inc=(t == 1 and k == 1))
            t_conf[:] = [act(xf[:, 0:2, :], ps[b][:, :].rearrange("p (t n) -> p t n", t=2), ACT.Copy, d, x_gone)]
            give(b, t_conf[0])

        def pipeline(heads, oldest_first=False):
            n = len(heads)
            for t in range(n + max(len(x) for x in heads)):
                for i in range(n) if oldest_first else range(n - 1, -1, -1):
                    if 0 <= t - i < len(heads[i]):
                        heads[i][t - i]()
                yield

        def softmax(i, scores, scale, Pm, ring, weight, base):
            r, s = i % Pm.shape[1], {}
            p, c = Pm[:, r, :], 64 + 6 * r
            QB = ((0, 128), (128, 384))

            def a():
                b, fr = take()
                s["b"], s["d"] = b, scores(ps[b], [fr, base])

            def b1():
                b, d, gone = s["b"], s["d"], ring.get(r)
                m = [vec(lambda e, q=q, lo=lo, hi=hi: e.tensor_reduce(st[:, c + q:c + q + 1], ps[b][:, lo:hi], AX,
                                                                      ALU.max, negate=True), d, base, gone)
                     for q, (lo, hi) in enumerate(QB)]
                if scale != 1.0:
                    m = ts(st[:, c:c + 2], st[:, c:c + 2], scale, None, ALU.mult, None, m)
                s["x"] = [act(p[:, lo:hi], ps[b][:, lo:hi], ACT.Exp, m, gone, base, scale=scale,
                              bias=st[:, c + q:c + q + 1], accum_out=st[:, c + 2 + q:c + 3 + q])
                          for q, (lo, hi) in enumerate(QB)]
                give(b, s["x"][-1])

            def b2():
                rc = st[:, c + 4:c + 6]
                t = vec(lambda e: e.reciprocal(rc, st[:, c + 2:c + 4]), s["x"])
                if weight:
                    t = ts(rc, rc, weight[0], None, ALU.mult, None, t, weight[1])
                s["n"] = [ts(p[:, lo:hi], p[:, lo:hi], rc[:, q:q + 1], None, ALU.mult, None, t, s["x"])
                          for q, (lo, hi) in enumerate(QB)]

            s["p"], s["key"] = p, r
            return s, [a, b1, b2]

        def turn(p, o, tok, *w):
            b, fr = take()
            for j in range(3):
                d = pe(lambda e, j=j: e.transpose(ps[b][:, 128 * j:128 * j + 128], p[:, 128 * j:128 * j + 128], C(C_ID)),
                       tok, fr, inc=(j == 2))
            t = act(o, ps[b][:, 0:384], ACT.Copy, d, *w)
            give(b, t)
            return d, t

        def plain_head(i, s, steps, ring, PT, pt, v, t_v, out, o_tok, *w):
            o, u = PT[:, i % PT.shape[1], :], {}

            def c():
                ring[s["key"]], u["t"] = turn(s["p"], o, s["n"], pt.get(i - PT.shape[1]), w)

            def d():
                b, fr = take()
                mm(ps[b][:, 0:128], v[0], o[:, 0:128], True, True, u["t"], t_v, fr)
                mm(ps[b][:, 128:256], v[0], o[:, 128:256], True, False)
                pt[i] = mm(ps[b][:, 128:256], v[1], o[:, 256:384], False, True, inc=True)
                pr = slice(64 * (i % 2), 64 * (i % 2) + 64)
                o_tok.append(act(out[pr, :], ps[b][pr, 0:256], ACT.Copy, pt[i], w))
                give(b, o_tok[-1])

            return steps + [c, d]

        def logits(o, qh, kh, fr, w, extra=None):
            for q in range(2):
                lo, n = (0, 128) if q == 0 else (128, 256)
                mm(o[:, lo:lo + n], qh[:, 128 * q:128 * q + 128], kh[:, 0:n], True, False, fr, w)
                if extra:
                    mm(o[:, lo:lo + n], extra[0][:, 128 * q:128 * q + 128], extra[1][:, 0:n], False, False, extra[2])
                d = mm(o[:, lo + n - 128:lo + n], idb[:, :], mab[:, :], False, True, t_m, inc=(q == 1))
            return d

        rk_gone, fo_pt, ring, t_att = {}, {}, {}, []
        t_hl = {}

        def fo_head(i):
            t = {}

            def bias():
                t["k"] = ts(rk[:, i % 3, :], NCt, P("fsel", i), None, ALU.mult, None, t_cq, rk_gone.get(i - 3))

            def scores(o, fr):
                rk_gone[i] = logits(o, qm[:, i, :], kT[:, i // 2, :], fr, [t_q, t_k], (CQ, rk[:, i % 3, :], [t["k"], t_cq]))
                return rk_gone[i]

            s, steps = softmax(i, scores, 1.0, Pm, ring, None, None)
            c = slice(128 * (i // 2), 128 * (i // 2) + 128)
            return [bias] + plain_head(i, s, steps, ring, PT, fo_pt, [vs[:, tb, c] for tb in range(2)], t_v, xf[:, 2 + i // 2, :], t_att,
                                       x_gone)

        heads = pipeline([fo_head(i) for i in range(4)])
        bp, dp = bank_tok(S["p"], 256, t_x)
        t_pv = act(pv, ps[bp][:, :].rearrange("p (t n) -> p t n", t=2), ACT.Copy, dp)
        give(bp, t_pv)
        next(heads)
        advance(conv, 4)
        b, d = bank_mm("h")
        t_hs = act(hsb, ps[b][:, :], ACT.Copy, d)
        give(b, t_hs)
        advance(conv, 2)
        t_d = []
        for t in range(2):
            b, fr = take()
            for i in range(2):
                for tb in range(2):
                    d = mm(ps[b][:, 256 * i:256 * i + 256], pv[:, tb, 128 * t:128 * t + 128], band[:, 2 * t + i, tb, :],
                           tb == 0, tb == 1, t_pv, t_bd, fr, inc=(i == 1 and tb == 1))
            for i in range(2):
                pr = slice(64 * i, 64 * i + 64)
                t_d.append(act(dT[pr, t, :], ps[b][pr, 256 * i:256 * i + 256], ACT.Copy, d))
            give(b, t_d[-1])
        next(heads)
        next(heads)
        b, d = bank_mm("c")
        t_c3 = tt(cpad[:, :, 2:258], ps[b][:, :].rearrange("p (t n) -> p t n", t=2),
                  hsb.rearrange("p (t n) -> p t n", t=2), ALU.mult, t_hs, d, z1)
        give(b, t_c3)
        t3 = []
        for t in range(2):
            a = ts(scv[:, t, :], cpad[:, t, 0:256], P("sc", 3 * t), None, ALU.mult, None, t_c3)
            for k in (1, 2):
                a = stt(scv[:, t, :], cpad[:, t, k:k + 256], P("sc", 3 * t + k), scv[:, t, :], ALU.mult, ALU.add, a)
            t3.append(a)
        next(heads)
        advance(conv, 1)
        b, fr = take()
        for t in range(2):
            d = mm(ps[b][:, 256 * t:256 * t + 256], wpb[:, t, :], dT[:, t, :], True, True, t_d, t_wp, fr, inc=(t == 1))
        for t in range(2):
            t_pool = ts(xf[:, 6 + t, :], ps[b][:, 256 * t:256 * t + 256], P("pool_scale", t), None, ALU.mult, None, d, x_gone)
        give(b, t_pool)
        b, d = bank_mm("sb")
        x_last = d
        for tb in range(2):
            t_hl[3, tb] = hilo(6, 8, tb, t_pool, x_last)
        t_sc = tt(xf[:, 4:6, :], ps[b][:, :].rearrange("p (t n) -> p t n", t=2), scv, ALU.mult, d, t3, x_gone)
        give(b, t_sc)
        for tb in range(2):
            t_hl[2, tb] = hilo(4, 6, tb, t_sc, x_last)
        advance(conv, 99)
        next(heads)
        stp = Step(normed(rows[:, 0, :], t_r0), P("g_mlp_pre", 0, 8))
        so = Split(S["out"], stp)
        so.x = t_hl
        cf = conformer()
        next(cf)
        for i in (3, 2):
            for tb in range(2):
                so.part(i, tb)
                next(heads, 0)
                next(cf, 0)
        for _ in cf:
            next(heads, 0)
        for tb in range(2):
            t_hl[0, tb] = hilo(0, 2, tb, t_conf)
        for _ in heads:
            pass
        for tb in range(2):
            t_hl[1, tb] = hilo(2, 4, tb, t_att)
        so.finish()

        t_r0 = dma("row0", rows[:, 0, :], D["g_ple_post"].partition_broadcast(128), bar(), q=GP)

        def ffn(sl, gated, x, nxt, late=None):
            b0 = bar()
            rb = SC[:, 0:1024].rearrange("p (a b) -> p a b", a=2)
            fb = SC[:, 1024:2048].rearrange("p (a b) -> p a b", a=2)
            n = len(sl)
            dn, rd = {}, {}

            def evacuate(j, banks):
                p = j % 2
                r_gone, f_gone = rd.get(j - 2), dn.get(j - 3)
                (b, d), (b2, d2) = banks[0], banks[-1]
                r = act(rb[:, p, :], ps[b][:, :], ACT.Silu if gated else ACT.Relu, d, b0, r_gone)
                if gated:
                    give(b, r)
                    f = tt(fb[:, p, :], ps[b2][:, :], rb[:, p, :], ALU.mult, r, d2, b0, r_gone)
                else:
                    f = stt(fb[:, p, :], ps[b][:, :], 0.0, rb[:, p, :], ALU.max, ALU.mult, r, b0, r_gone)
                give(b2, f)
                a = act(fh[:, j % 3, :], fb[:, p, :], ACT.Copy, f, f_gone)
                l = tt(fl[:, j % 3, :], fb[:, p, :], fh[:, j % 3, :].bitcast(F32), ALU.subtract, a, f, f_gone)
                rd[j] = [a, l]

            def down(i, tb):
                v = [y[:, i % 3, :].rearrange("p (k n) -> p k n", k=2) for y in (fh, fl)]
                return tok_part(sl[i][-1], [(ps[acc[tb][c][0]][:, :], HALF[c]) for c in range(2)], tb, rd[i],
                                [y[1] for y in acc[tb]], first=(i == 0), final=(i == n - 1), a=v)

            ups = [y[:-1] for y in sl]
            head = 2 if gated else 4
            f6, l6 = (y[:, :, :].rearrange("p a (k n) -> p (a k) n", k=2) for y in (fh, fl))

            hd = {}

            def head_up(tb):
                bk = [take() for _ in range(2)]
                for j in range(head):
                    for k, i in enumerate(ups[j]):
                        if (tb, j, k) == (0, head - 1, len(ups[j]) - 1):
                            x.late(1)
                        b, at = (bk[k], j) if gated else (bk[j // 2], j % 2)
                        d = tok_part(i, [(ps[b[0]][:, 256 * at:256 * at + 256], slice(0, 256))], tb, x.late(tb), b[1])
                        if tb == 1:
                            end_use(i, d)
                    if tb == 1 and j == 0:
                        head_turn(0, 0, min(head, 3))
                r, f = (SC[:, c + 1024 * tb:c + 1024 * tb + 256 * head] for c in (7040, 9088))
                fd = []
                for k in range(2):
                    if gated and k == 1:
                        fd.append(tt(f, ps[bk[1][0]][:, :], r, ALU.mult, a, d, b0))
                        give(bk[1][0], fd[-1])
                        break
                    w = slice(0, 256 * head) if gated else slice(512 * k, min(512 * k + 512, 256 * head))
                    v = ps[bk[k][0]][:, 0:w.stop - w.start]
                    a = act(r[:, w], v, ACT.Silu if gated else ACT.Relu, d, b0)
                    if not gated:
                        fd.append(stt(f[:, w], v, 0.0, r[:, w], ALU.max, ALU.mult, a, b0))
                    give(bk[k][0], a if gated else fd[-1])
                hd[tb] = (f, fd)

            def head_turn(tb, j0, j1, *w):
                f, fd = hd[tb]
                for c in range(2 * j0, 2 * j1, 4):
                    m = min(4, 2 * j1 - c)
                    b, fr = take()
                    for k in range(m):
                        t = pe(lambda e, k=k, c=c, b=b: e.transpose(ps[b][:, 128 * k:128 * k + 128],
                                                                    f[:, 128 * (c + k):128 * (c + k) + 128], C(C_ID)),
                               fd, fr, inc=(k == m - 1))
                    v = ps[b][:, 0:128 * m].rearrange("p (k n) -> p k n", k=m)
                    o, l = (y[:, c % 6:c % 6 + m, 128 * tb:128 * tb + 128] for y in (f6, l6))
                    a = act(o, v, ACT.Copy, t, w)
                    l = tt(l, v, o.bitcast(F32), ALU.subtract, a, w)
                    give(b, l)
                    for j in range(c // 2, (c + m) // 2):
                        rd.setdefault(j, []).extend([a, l])

            head_up(0)
            head_up(1)
            t_x = both(x)
            acc = None
            if not gated:
                acc = [[take() for _ in range(2)] for _ in range(2)]
                down(0, 0)
                head_turn(1, 0, 3)
                dn[0] = down(0, 1)
                end_use(sl[0][-1], dn[0])
                for tb in range(2):
                    head_turn(tb, 3, 4, dn[0])
            for j in range(head, n):
                banks = []
                for i in ups[j]:
                    b, fr = take()
                    banks.append((b, feat_mm(i, ps[b], t_x, fr)))
                if gated and j == head:
                    head_turn(1, 0, head)
                if j >= 3:
                    if acc is None:
                        acc = [[take() for _ in range(2)] for _ in range(2)]
                    down(j - 3, 0)
                    dn[j - 3] = down(j - 3, 1)
                    end_use(sl[j - 3][-1], dn[j - 3])
                evacuate(j, banks)
                if late and j == n - 4:
                    late()
            for tb in range(2):
                for i in range(n - 3, n):
                    d = down(i, tb)
                    if tb == 1:
                        end_use(sl[i][-1], d)
                        if i == n - 2:
                            nxt.late(0)
                if tb == 1:
                    flush()
                nxt.early(tb, acc[tb], d)

        b0 = bar()
        pT = SC[:, 2048:2560].rearrange("p (k n) -> p k n", k=2)
        e0 = SC[:, 3584:5632].rearrange("p (a b) -> p a b", a=2)
        sgm = SC[:, 5632:7680].rearrange("p (a b) -> p a b", a=2)
        t_pT = dma("pT", pT, D["pT"].rearrange("(k p) n -> p k n", p=128), b0, q=GP)
        t_es, t_ph = {}, []

        def halves():
            t_ph.append(act(phl[0][:, :, :], pT, ACT.Copy, t_pT, b0))
            t_ph.append(tt(phl[1][:, :, :], pT, phl[0][:, :, :].bitcast(F32), ALU.subtract, t_ph[0], b0))

        def projection():
            bk = [[take() for _ in range(2)] for _ in range(2)]
            d = tok_mm(S["proj"], [[(ps[bk[tb][c][0]][:, :], HALF[c]) for c in range(2)] for tb in range(2)], t_ph,
                       [x[1] for y in bk for x in y], a=phl)
            flush()
            for tb in range(2):
                for c in range(2):
                    t_es[tb, c] = act(e0[:, tb, HALF[c]], ps[bk[tb][c][0]][:, :], ACT.Copy, d, b0)
                    give(bk[tb][c][0], t_es[tb, c])

        nxt = Step(normed(rows[:, 1, :], t_r1), P("g_ple_pre", 0, 8))
        ffn(S["ff"], False, stp, nxt, halves)
        projection()
        stp = nxt

        t_r1 = dma("row1", rows[:, 1, :], D["norm_final_2"].partition_broadcast(128), bar(), q=GP)

        def gated(tb, bk, d):
            m = []
            for c in range(2):
                a = act(sgm[:, tb, HALF[c]], ps[bk[c][0]][:, :], ACT.Sigmoid, d, b0)
                give(bk[c][0], a)
                m.append(tt(e0[:, tb, HALF[c]], e0[:, tb, HALF[c]], sgm[:, tb, HALF[c]], ALU.mult, a, t_es[tb, c]))
            return add_norm([e0[:, tb, c] for c in HALF], rows[:, 0, :], t_r0, tb, m)[1]

        nxt = Step(gated, P("nm0", 0, 8))
        proj_out(S["gate"], stp.late(0), lambda: stp.late(1), nxt.early, nxt.late)
        stp = nxt

        b0 = bar()
        sc = Scratch()
        dqm = sc(8, 256)
        dkT = sc(4, 256)
        dvs = sc(2, 512)
        qT = sc(8, 256)
        kT2 = sc(8, 256)
        vm = sc(2, 512)
        Pm = sc(5, 384)
        roped = qT.rearrange("p a b -> p (a b)").rearrange("p (j t n) -> p j t n", j=2, t=2)
        lat = fh_f[:, 0:1344].rearrange("p (t n) -> p t n", t=2)
        qf, kf = (x.rearrange("p (t n) -> p t n", t=2) for x in (fh_f[:, :], fl_f[:, :]))
        cqs, cks, krs = lat[:, :, 0:384], lat[:, :, 384:640], lat[:, :, 640:672]
        PT = hsf[:, 0:1152].rearrange("p (a b) -> p a b", a=3)
        on = hsf[:, 1152:1664].rearrange("p (a b) -> p a b", a=2)
        krr = hsf[:, 1664:1728].rearrange("p (t n) -> p t n", t=2)
        lam = hsf[:, 1728:1792]
        tmp = rows[:, 0, :].rearrange("p (a b) -> p a b", a=4)

        z2 = pool(lambda e: e.memset(dqm, 0.0), b0)

        def wide(names, x0, enter1):
            bk = {n: [take() for _ in range(2)] for n in names}
            out = {n: [None, None] for n in names}
            x = [x0, None]
            todo = [(n, i) for n in names for i in range(2)]
            for tb in range(2):
                for n, i in todo:
                    if tb == 0 and (n, i) == todo[-1]:
                        x[1] = enter1()
                    d = tok_part(S[n][i], [(ps[bk[n][tb][0]][:, :], slice(0, 512))], tb, x[tb], bk[n][tb][1],
                                 k0=4 * i, first=(i == 0), final=(i == 1))
                    if tb == 1:
                        end_use(S[n][i], d)
                    out[n][tb] = (bk[n][tb][0], d)
            flush()
            return out, x

        tmp_gone = [b0]

        def rope(dst, src, tb, nh, half, at, d, *w):
            n = nh * half
            co = cst[:, at + 96 * tb:at + 96 * tb + half].unsqueeze(1).to_broadcast([128, nh, half])
            si = cst[:, at + 96 * tb + half:at + 96 * tb + 2 * half].unsqueeze(1).to_broadcast([128, nh, half])
            x1, x2 = src[:, :, 0:half], src[:, :, half:2 * half]
            u = [tmp[:, i, 0:n].rearrange("p (a b) -> p a b", a=nh) for i in range(4)]
            a = [tt(u[0], x1, co, ALU.mult, d, tmp_gone[0]), tt(u[1], x2, si, ALU.mult, d), tt(u[2], x2, co, ALU.mult, d),
                 tt(u[3], x1, si, ALU.mult, d)]
            tmp_gone[0] = [tt(dst[:, :, 0:half], u[0], u[1], ALU.subtract, a, *w),
                           tt(dst[:, :, half:2 * half], u[2], u[3], ALU.add, a, *w)]
            return [a, tmp_gone[0]]

        t_rp = []
        w_dqk, t_x = wide(["dq", "dk"], stp.late(0), lambda: stp.late(1))
        b0 = [b0, bar()]
        for tb in range(2):
            for j, n in enumerate(("dq", "dk")):
                b, d = w_dqk[n][tb]
                r = rope(roped[:, j, tb, :].rearrange("p (a b) -> p a b", a=8),
                         ps[b][:, :].rearrange("p (a b) -> p a b", a=8), tb, 8, 32, C_ROPE + 32, d, b0)
                give(b, r[0])
                t_rp.append(r)
        b0 = [b0, bar()]
        t_lt = []
        bk = [[take() for _ in range(2)] for _ in range(2)]
        for i in range(4):
            for tb in range(2):
                d = tok_part(S["lat"][i], [(ps[bk[tb][c][0]][:, 0:336], slice(336 * c, 336 * c + 336)) for c in range(2)],
                             tb, t_x, [x[1] for y in bk for x in y], k0=2 * i, first=(i == 0), final=(i == 3))
            end_use(S["lat"][i], d)
        for tb in range(2):
            for c in range(2):
                t_lt.append(act(lat[:, tb, 336 * c:336 * c + 336], ps[bk[tb][c][0]][:, 0:336], ACT.Copy, d, b0))
                give(bk[tb][c][0], t_lt[-1])
        t_lm = {}
        for tb in range(2):
            for i, (src, n) in enumerate(((cqs, 384), (cks, 256))):
                c = 36 + 4 * tb + 2 * i
                q = square(src[:, tb, :], st[:, c:c + 1], 1.0, t_lt, b0)
                r = rstd(st[:, c + 1:c + 2], st[:, c:c + 1], n, q)
                t_lm[tb, i] = ts(src[:, tb, :], src[:, tb, :], st[:, c + 1:c + 2], None, ALU.mult, None, r, q)
        t_kr = [rope(krr[:, tb, :].unsqueeze(1), krs[:, tb, :].unsqueeze(1), tb, 1, 16, C_ROPE, t_lt, b0)
                for tb in range(2)]
        t_dq, t_dk = [], []
        for j in range(2):
            for tb in range(2):
                b, fr = take()
                for k in range(4):
                    d = pe(lambda e, j=j, tb=tb, k=k, b=b: e.transpose(ps[b][:, 128 * k:128 * k + 128],
                                                                       roped[:, j, tb, 128 * k:128 * k + 128], C(C_ID)),
                           t_rp, fr, inc=(k == 3))
                s = slice(128 * tb, 128 * tb + 128)
                v = ps[b][:, :].rearrange("p (k n) -> p k n", k=4)
                if j == 0:
                    for i in range(2):
                        pr = slice(64 * i, 64 * i + 64)
                        t_dq.append(act(dqm.rearrange("p (k i) n -> p k i n", i=2)[pr, :, i, s], v[pr], ACT.Copy, d, z2))
                    give(b, t_dq[-1])
                else:
                    t_dk.append(act(dkT[:, :, s], v, ACT.Copy, d, b0))
                    give(b, t_dk[-1])
        r_gone = PE.last()

        la = []
        for i in range(2):
            a = tt(lam[:, 0:64], srow[:, 8 + 128 * i:72 + 128 * i], srow[:, 72 + 128 * i:136 + 128 * i], ALU.mult, t_sr, b0, la)
            r = vec(lambda e, i=i: e.tensor_reduce(st[:, 48 + i:49 + i], lam[:, 0:64], AX, ALU.add), a)
            la = [r]
        a = act(st[:, 50:52], st[:, 48:50], ACT.Exp, la)
        a = tt(st[:, 52:53], st[:, 50:51], st[:, 51:52], ALU.subtract, a)
        a = ts(st[:, 52:53], st[:, 52:53], LAMBDA0, None, ALU.add, None, a)
        b_ = act(st[:, 53:54], st[:, 52:53], ACT.Abs, a)
        b_ = ts(st[:, 53:54], st[:, 53:54], 1.0, None, ALU.max, None, b_)
        b_ = vec(lambda e: e.reciprocal(st[:, 54:55], st[:, 53:54]), b_)
        b_ = stt(st[:, 55:56], st[:, 52:53], -1.0, st[:, 54:55], ALU.mult, ALU.mult, b_)
        t_lam = stt(st[:, 56:57], st[:, 54:55], EPS, st[:, 54:55], ALU.mult, ALU.mult, b_)

        df_o, df_pt, df_on, D0, ring = [], {}, {}, {}, {}
        turned = [0]

        def df_map(i):
            def scores(o, fr):
                return logits(o, dqm[:, i, :], dkT[:, i // 2, :], fr, [t_dq, t_dk])

            f, g = 54 + i % 2, i // 2
            s, steps = softmax(where[0, i], scores, 0.125, Pm, ring, (st[:, f:f + 1], t_lam), b0)
            if i % 2 == 0:
                D0[g] = s
                return steps
            u, s0, o = {}, D0[g], PT[:, 2, :]
            cc = 58 + 3 * (g % 2)

            def sub():
                u["n"] = tt(s["p"], s["p"], s0["p"], ALU.add, s["n"], s0["n"])
                ring[s0["key"]] = u["n"]

            def c():
                ring[s["key"]], u["t"] = turn(s["p"], o, u["n"], df_pt.get(g - 1), b0, r_gone)

            def d():
                b, fr = take()
                v = slice(128 * g, 128 * g + 128)
                mm(ps[b][:, 0:128], o[:, 0:128], dvs[:, 0, v], True, True, u["t"], t_dv, fr)
                mm(ps[b][:, 128:256], o[:, 128:256], dvs[:, 0, v], True, False)
                df_pt[g] = mm(ps[b][:, 128:256], o[:, 256:384], dvs[:, 1, v], False, True, inc=True)
                q = [square(ps[b][:, 128 * tb:128 * tb + 128], st[:, cc + tb:cc + tb + 1], 1.0, df_pt[g], df_on.get(g - 2))
                     for tb in range(2)]
                y = ts(st[:, cc:cc + 2], st[:, cc:cc + 2], 1.0 / 128, st[:, 56:57], ALU.mult, ALU.add, q, t_lam)
                u["b"], u["y"] = b, rsqrt(st[:, cc:cc + 2], y)

            def e():
                b = u["b"]
                u["m"] = [ts(on[:, g % 2, 128 * tb:128 * tb + 128], ps[b][:, 128 * tb:128 * tb + 128], st[:, cc + tb:cc + tb + 1],
                             1.0 - LAMBDA0, ALU.mult, ALU.mult, u["y"], df_on.get(g - 2), b0) for tb in range(2)]
                give(b, u["m"])

            def f_():
                df_on[g] = []
                for tb in range(2):
                    t = to_xf(on[:, g % 2, 128 * tb:128 * tb + 128], 1, 4 + g, tb, P("subln"), u["m"], lat_gone)
                    df_o.append(t)
                    df_on[g] += t

            return steps + [sub, c, d, e, f_]

        ml_pt, ml_o, lat_gone = {}, [], []
        t_qT, t_vm = [], []

        def ml_head(i):
            def scores(o, fr):
                return logits(o, qT[0:96, i, :], kT2[0:96, i, :], fr, t_qT)

            s, steps = softmax(where[1, i], scores, 96.0 ** -0.5, Pm, ring, None, b0)
            c = slice(128 * (i // 2), 128 * (i // 2) + 128)
            return plain_head(i, s, steps, ring, PT[:, 0:2, :], ml_pt, [vm[:, tb, c] for tb in range(2)], t_vm, xf[:, i // 2, :], ml_o,
                              lat_gone, b0, r_gone)

        order = [(m, i) for m in range(2) for i in range(8)]
        where = {x: n for n, x in enumerate(order)}
        heads = pipeline([(ml_head if m else df_map)(i) for m, i in order])
        bk = [take() for _ in range(2)]
        for i in range(2):
            for tb in range(2):
                d = tok_part(S["dv"][i], [(ps[bk[tb][0]][:, :], slice(0, 512))], tb, t_x, bk[tb][1], k0=4 * i,
                             first=(i == 0), final=(i == 1))
            end_use(S["dv"][i], d)
            next(heads)
            if i == 0:
                t_n = []
                for tb in range(2):
                    for i, (src, n) in enumerate(((cqs, 384), (cks, 256))):
                        t_n.append(to_xf(src[:, tb, :], n // 128, 0 if i == 0 else 3, tb, P("qn", 0, 3) if i == 0 else P("kvn", 0, 2),
                                         t_lm[tb, i]))
        x_gone = d
        t_dv = []
        for tb in range(2):
            t_dv.append(act(dvs[:, tb, :], ps[bk[tb][0]][:, :], ACT.Copy, d, b0))
            give(bk[tb][0], t_dv[-1])
        t_lat = [hilo(0, 5, tb, t_n, x_gone) for tb in range(2)]
        lat_gone += [t_lat, PE.last()]
        next(heads)
        next(heads)
        t_qf = []
        bq = [[take() for _ in range(2)] for _ in range(2)]
        fr = [x[1] for y in bq for x in y]
        for i in range(2):
            d = tok_mm(S["uq"][i], [[(ps[bq[tb][i][0]][:, 0:384], slice(0, 384))] for tb in range(2)], t_lat, fr)
            for tb in range(2):
                v = ps[bq[tb][i][0]][:, 0:384].rearrange("p (a b) -> p a b", a=4)
                o = qf[:, tb, 384 * i:384 * i + 384].rearrange("p (a b) -> p a b", a=4)
                a = act(o[:, :, 0:64], v[:, :, 0:64], ACT.Copy, d, b0, t_kr, lat_gone)
                r = rope(o[:, :, 64:96], v[:, :, 64:96], tb, 4, 16, C_ROPE, [d, a], b0)
                give(bq[tb][i][0], r[0])
                t_qf.append([a, r])
            next(heads)
        wH, wL, tok = use(S["ukv"])
        bkk = [take() for _ in range(2)]
        bvv = [take() for _ in range(2)]
        fr = [x[1] for x in bkk + bvv]
        for tb in range(2):
            s = slice(128 * tb, 128 * tb + 128)
            for o, c in ((ps[bkk[tb][0]], 0), (ps[bvv[tb][0]], 64)):
                for k in range(2):
                    sel = [x[:, k, :].rearrange("p (a b) -> p a b", a=8)[:, :, c:c + 64] for x in (wH, wL)]
                    d = mm3(o[:, :].rearrange("p (a b) -> p a b", a=8), xh[:, 3 + k, s], xl[:, 3 + k, s], sel[0], sel[1],
                            k == 0, k == 1, tok, t_lat, fr, inc=(tb == 1 and c == 64 and k == 1))
        end_use(S["ukv"], d)
        xh_gone = d
        t_kf = []
        for tb in range(2):
            kv = kf[:, tb, :].rearrange("p (a b) -> p a b", a=8)
            a = act(kv[:, :, 0:64], ps[bkk[tb][0]][:, :].rearrange("p (a b) -> p a b", a=8), ACT.Copy, d, b0)
            give(bkk[tb][0], a)
            v = act(vm[:, tb, :], ps[bvv[tb][0]][:, :], ACT.Copy, d, b0)
            give(bvv[tb][0], v)
            t_vm.append(v)
            t_kf.append(a)
        for tb in range(2):
            kv = kf[:, tb, :].rearrange("p (a b) -> p a b", a=8)
            t_kf.append(vcopy(kv[:, :, 64:96], krr[:, tb, :].unsqueeze(1).to_broadcast([128, 8, 32]), t_kr, b0))
        next(heads)
        for src, dst, tk in ((qf, qT, t_qf), (kf, kT2, t_kf)):
            for tb in range(2):
                for c in range(2):
                    b, fr = take()
                    for k in range(4):
                        hd = 4 * c + k
                        d = pe(lambda e, src=src, tb=tb, hd=hd, k=k, b=b: e.transpose(
                            ps[b][0:96, 128 * k:128 * k + 128], src[:, tb, 96 * hd:96 * hd + 96], C(C_ID)),
                            tk, fr, inc=(k == 3))
                    a = act(dst[0:96, 4 * c:4 * c + 4, 128 * tb:128 * tb + 128],
                            ps[b][0:96, :].rearrange("p (k n) -> p k n", k=4), ACT.Copy, d, b0, r_gone)
                    give(b, a)
                    t_qT.append(a)
            if src is qf:
                next(heads)
        for _ in range(8):
            next(heads)
        stp = Step(add_banks, P("nf0", 0, 8))
        so = Split(S["aout"], stp)
        for tb in range(2):
            so.x[2, tb] = so.x[3, tb] = hilo(4, 8, tb, df_o, xh_gone)
        for i in (2, 3):
            for tb in range(2):
                so.part(i, tb)
                next(heads, 0)
        for _ in heads:
            pass
        for tb in range(2):
            so.x[0, tb] = so.x[1, tb] = hilo(0, 4, tb, ml_o, xh_gone)
        so.finish()
        nxt = Step(add_banks, P("nm1", 0, 8))
        ffn(S["f0"], True, stp, nxt)
        stp = nxt

        b0 = bar()
        sc = Scratch()
        hq = sc(4, 256)
        hk = sc(4, 256)
        G = sc(4, 256)
        Dd = sc(2, 1024)
        hiv = sc(2, 512)
        shg = sc(2, 512)
        xb = sc(8, 256)
        sz = sc(2, 512)
        cbs = sc(2, 384)
        QK = hsf.rearrange("p (a b) -> p a b", a=2)
        STt = rows[:, 0, :].rearrange("p (a b) -> p a b", a=8)
        ST2 = fh_f[:, 0:512].rearrange("p (a b) -> p a b", a=4)
        hm = fh_f[:, 512:1536].rearrange("p (a b) -> p a b", a=8)
        xs = fl_f[:, 0:1024].rearrange("p (a b) -> p a b", a=2)
        T2 = fl_f[:, 1024:1280]
        At = fl_f[:, 1280:1360].rearrange("p (a b) -> p a b", a=2)
        wdt = fl_f[:, 1360:1424].rearrange("p (a b) -> p a b", a=8)
        ones = QK[:, 0, 0:256]
        dr = QK[:, 1, :].rearrange("p (a b) -> p a b", a=4)
        xff = xf[:, :, :].rearrange("p a b -> p (a b)")
        Eb = xff[:, 512:1280].rearrange("p (a b) -> p a b", a=2)
        Mb = xff[:, 1280:2048].rearrange("p (a b) -> p a b", a=2)
        ov = Dd[:, 0, :].rearrange("p (a b) -> p a b", a=2)
        z3 = pool(lambda e: e.memset(T2, 0.0), b0)
        t_wd = dma("wdt", wdt, sw[:, 1536:1544].rearrange("(k p) n -> p k n", p=128), b0, q=GP)
        t_hm = dma("hm", hm, D["hmask"], b0, q=GP)
        lb = tt(st[:, 12:16], P("lb1", 0, 4), P("lb0", 0, 4), ALU.subtract, b0)
        lb = act(st[:, 8:12], st[:, 12:16], ACT.Sigmoid, lb, b0)
        lb = [lb, act(st[:, 16:20], st[:, 12:16], ACT.Sigmoid, lb, scale=-1.0)]

        w_zi, t_x = wide(["z", "hi"], stp.late(0), lambda: stp.late(1))
        t_sz, t_hi = [], []
        for n, o, t in (("z", sz, t_sz), ("hi", hiv, t_hi)):
            for tb in range(2):
                b, d = w_zi[n][tb]
                t.append(act(o[:, tb, :], ps[b][:, :], ACT.Copy, d, b0))
                give(b, t[-1])
        b, fr = take()
        for k in range(8):
            d_dt = mm(ps[b][0:8, 0:256], wdt[:, k, :], xf[:, k, :], k == 0, k == 7, t_wd, t_x, fr, inc=(k == 7))
        R = slice(0, 8)
        t_d = ts(dr[R, 0, :], ps[b][R, 0:256], P("dtb")[R], None, ALU.add, None, d_dt, b0)
        give(b, t_d)
        t_hq, t_hf = [], []
        for i in range(2):
            b, d = bank_feat(S["hq"][i], t_x)
            t_hq.append(act(hq[:, 2 * i:2 * i + 2, :], ps[b][:, :].rearrange("p (t n) -> p t n", t=2), ACT.Silu, d, b0))
            give(b, t_hq[-1])
        for i in range(2):
            b, d = bank_feat(S["hf"][i], t_x)
            v = ps[b][:, :].rearrange("p (t n) -> p t n", t=2)
            a = act(G[:, 2 * i:2 * i + 2, :], v, ACT.Sigmoid, d, b0)
            a2 = act(hk[:, 2 * i:2 * i + 2, :], v, ACT.Sigmoid, d, b0, scale=-1.0)
            give(b, a2)
            for t in (2 * i, 2 * i + 1):
                t_hf.append(ts(G[:, t, :], G[:, t, :], st[:, 16 + t:17 + t], st[:, 8 + t:9 + t], ALU.mult, ALU.add, a, lb))
                t_hf.append(ts(hk[:, t, :], hk[:, t, :], st[:, 16 + t:17 + t], None, ALU.mult, None, a2, lb))
        a = ts(G, G, 1e-18, None, ALU.max, None, t_hf)
        lg = Dd[:, 1, :].rearrange("p (a b) -> p a b", a=4)
        a = act(lg, G, ACT.Ln, a, b0)
        o1 = vec(lambda e: e.memset(ones, 1.0), d_dt)
        t_G = [vec(lambda e, t=t: e.tensor_tensor_scan(G[:, t, :], ones, lg[:, t, :], 0.0, ALU.mult, ALU.add), a, o1)
               for t in range(4)]
        t_dt = softplus(dr[R, 0, :], dr[R, 1, :], dr[R, 2, :], dr[R, 3, :], junk[R, 0:256], t_d, b0, sq_last[0], sq_last[1])
        t1 = act(st[R, 61:62], P("alog")[R], ACT.Exp, b0)
        t1 = ts(dr[R, 1, :], dr[R, 0, :], st[R, 61:62], -1.0, ALU.mult, ALU.mult, t1, t_dt)
        t2 = vec(lambda e: e.memset(dr[R, 2, :], 1.0), t_dt)
        t_A = [vec(lambda e: e.tensor_tensor_scan(T2[R, :], dr[R, 2, :], dr[R, 1, :], 0.0, ALU.mult, ALU.add), t1, t2, z3),
               vcopy(T2[32:40, :], dr[R, 0, :], t_dt, z3)]

        Gf, qf_, kf_ = (x.rearrange("p a b -> p (a b)") for x in (G, hq, hk))
        t_s2, t_st = [], []

        def level(n, m):
            u = {}
            nb = 1024 // (2 * m)
            g3, d3, q3, k3, o3 = (x.rearrange("p (b m) -> p b m", m=2 * m)
                                  for x in (Gf, Dd[:, n % 2, :], qf_, kf_, QK[:, n % 2, :]))
            ref = g3[:, :, m - 1:m].to_broadcast([128, nb, m])
            o = QK[:, n % 2, :].rearrange("p (h n) -> p h n", h=4)

            def a():
                w = [t_G, t_A, mult.get(n - 2)]
                u["a"] = [pool(lambda e: e.tensor_tensor(d3[:, :, 0:m], ref, g3[:, :, 0:m], ALU.subtract), w),
                          pool(lambda e: e.tensor_tensor(d3[:, :, m:2 * m], g3[:, :, m:2 * m], ref, ALU.subtract), w)]

            def b():
                u["x"] = act(Dd[:, n % 2, :], Dd[:, n % 2, :], ACT.Exp, u["a"])

            def c():
                w = [u["x"], used_qk.get(n - 2), t_hq, t_hf, t_A, t_G]
                mult[n] = [tt(o3[:, :, 0:m], k3[:, :, 0:m], d3[:, :, 0:m], ALU.mult, w),
                           tt(o3[:, :, m:2 * m], q3[:, :, m:2 * m], d3[:, :, m:2 * m], ALU.mult, w)]

            def d():
                if m == 128:
                    b, fr = take()
                    for hd in range(4):
                        t = mm(ps[b][:, 128 * hd:128 * hd + 128], o[:, hd, 0:128], o[:, hd, 128:256], True, True, mult[n], fr,
                               inc=(hd == 3))
                    t_s2.append(act(ST2, ps[b][:, :].rearrange("p (h n) -> p h n", h=4), ACT.Copy, t, b0))
                    give(b, t_s2[-1])
                    used_qk[n] = t
                else:
                    used_qk[n] = score(o, o, mult[n], LEVELS.index(m))

            return [a, b, c, d]

        mult, used_qk = {}, {}

        def score(s_, l_, tok, i):
            for tb in range(2):
                b, fr = take()
                c = slice(128 * tb, 128 * tb + 128)
                for hd in range(4):
                    d = mm(ps[b][:, 128 * hd:128 * hd + 128], s_[:, hd, c], l_[:, hd, c], True, True, tok, fr, inc=(hd == 3))
                v = ps[b][:, :].rearrange("p (h n) -> p h n", h=4)
                mk = hm[:, i, :].unsqueeze(1).to_broadcast([128, 4, 128])
                z = STt[:, 4 * tb:4 * tb + 4, :]
                if i == 7:
                    t_st.append(tt(z, v, mk, ALU.mult, d, t_hm, b0))
                else:
                    t_st.append(vec(lambda e, z=z, v=v, mk=mk: e.copy_predicated(z, mk.bitcast(I32), v), d, t_st[-2:]))
                give(b, t_st[-1])
            return d

        def hgrn_end():
            bo = [take() for _ in range(2)]
            fro = [x[1] for x in bo]
            for hd in range(4):
                c = slice(128 * hd, 128 * hd + 128)
                mm(ps[bo[0][0]][:, c], STt[:, hd, :], hiv[:, 0, c], True, True, t_st[-2:], t_hi, fro, t_s2)
                mm(ps[bo[1][0]][:, c], ST2[:, hd, :], hiv[:, 0, c], True, False)
                d = mm(ps[bo[1][0]][:, c], STt[:, 4 + hd, :], hiv[:, 1, c], False, True, inc=True)
            yield
            a = {}
            for tb in range(2):
                v = ps[bo[tb][0]][:, :]
                q = act(ov[:, tb, :], v, ACT.Square, d, list(mult.values()))
                r = vec(lambda e, tb=tb: e.tensor_reduce(st[:, 20 + 4 * tb:24 + 4 * tb],
                                                         ov[:, tb, :].rearrange("p (a b) -> p a b", a=4), AX, ALU.add), q, b0)
                a[tb] = rstd(st[:, 28 + 4 * tb:32 + 4 * tb], st[:, 20 + 4 * tb:24 + 4 * tb], 128, r)
            yield
            for tb in range(2):
                v = ps[bo[tb][0]][:, :]
                a[tb] = tt(ov[:, tb, :].rearrange("p (a b) -> p a b", a=4), v.rearrange("p (a b) -> p a b", a=4),
                           st[:, 28 + 4 * tb:32 + 4 * tb].unsqueeze(2).to_broadcast([128, 4, 128]), ALU.mult, a[tb])
                give(bo[tb][0], a[tb])
                a[tb] = tt(ov[:, tb, :], ov[:, tb, :], shg[:, tb, :], ALU.mult, a[tb], silus())
            yield
            for tb in range(2):
                t = to_xf(ov[:, tb, :], 4, 4, tb, P("g_norm"), a[tb], heads_done)
                t_hl[tb, 2] = hilo(4, 8, tb, t, x_last)

        silu_tok = []

        def silus():
            if not silu_tok:
                for x, t in ((sz, t_sz), (shg, t_hg)):
                    v = x.rearrange("p a b -> p (a b)")
                    silu_tok.append(act(v, v, ACT.Silu, t))
            return silu_tok

        t_xb, t_cv, t_hg, x_last = [], [], [], []

        def products():
            for i in range(4):
                b, d = bank_feat(S["xbc"][i], t_x)
                a = act(xf[:, 2 * i:2 * i + 2, :], ps[b][:, :].rearrange("p (t n) -> p t n", t=2), ACT.Copy, d, d_dt, t_x)
                give(b, a)
                for t in (2 * i, 2 * i + 1):
                    c = ts(xb[:, t, :], xf[:, t, :], P("cw", 4 * t + 3), None, ALU.mult, None, a, b0)
                    for k in (2, 1, 0):
                        s = 3 - k
                        c = stt(xb[:, t, s:256], xf[:, t, 0:256 - s], P("cw", 4 * t + k), xb[:, t, s:256], ALU.mult, ALU.add, c)
                    t_cv.append(c)
                yield
            bk = [take() for _ in range(2)]
            for i in range(2):
                for tb in range(2):
                    d = tok_part(S["hg"][i], [(ps[bk[tb][0]][:, :], slice(0, 512))], tb, t_x, bk[tb][1], k0=4 * i,
                                 first=(i == 0), final=(i == 1))
                end_use(S["hg"][i], d)
                if i == 0:
                    yield
            x_last.append(d)
            for tb in range(2):
                t_hg.append(act(shg[:, tb, :], ps[bk[tb][0]][:, :], ACT.Copy, d, b0))
                give(bk[tb][0], t_hg[-1])
            yield

        heads_done = []

        def ssd():
            for t in range(8):
                t_xb.append(act(xb[:, t, :], xb[:, t, :], ACT.Silu, t_cv[t], bias=P("cb", t)))
            yield
            t_at, t_xs, t_cb = [], [], []
            for tb in range(2):
                b, fr = take()
                s = slice(128 * tb, 128 * tb + 128)
                d = pe(lambda e, b=b, s=s: e.transpose(ps[b][:, 0:128], T2[:, s], C(C_ID)), t_A, fr)
                a = ts(At[:, tb, 0:8], ps[b][:, 0:8], -1.0, None, ALU.mult, None, d, b0)
                a = [a, vcopy(At[:, tb, 32:40], ps[b][:, 32:40], d)]
                give(b, a)
                t_at.append(a)
                b, fr = take()
                for k in range(4):
                    d = pe(lambda e, b=b, s=s, k=k: e.transpose(ps[b][:, 128 * k:128 * k + 128], xb[:, k, s], C(C_ID)),
                           t_xb, fr, inc=(k == 3))
                a = act(xs[:, tb, :], ps[b][:, :], ACT.Copy, d, b0)
                give(b, a)
                t_xs.append(a)
            for g in range(2):
                b, fr = take()
                mm(ps[b][:, 0:256], xb[:, 4 + g, 0:128], xb[:, 6 + g, :], True, True, t_xb, fr)
                d = mm(ps[b][:, 256:384], xb[:, 4 + g, 128:256], xb[:, 6 + g, 128:256], True, True, inc=True)
                a = act(cbs[:, g, :], ps[b][:, 0:384], ACT.Copy, d, b0)
                give(b, a)
                t_cb.append(a)
            yield
            by = [take() for _ in range(2)]
            fry = [x[1] for x in by]
            seg, m_gone = {}, {}

            def ssd_seg(i):
                b, fr = take()
                sel = cst[:, C_SEL + 128 * i:C_SEL + 128 * i + 128]
                o = ps[b]
                mm(o[:, 0:256], sel, T2, True, False, t_A, fr)
                mm(o[:, 0:128], idb[:, :], mtb[:, :], False, True, t_m)
                mm(o[:, 256:384], sel, T2[:, 128:256], True, False)
                d = mm(o[:, 256:384], idb[:, :], mtb[:, :], False, True, inc=True)
                a = [act(Eb[:, i % 2, 0:256], o[:, 0:256], ACT.Exp, d, t_at, t_cv, m_gone.get(i - 2), bias=At[:, 0, i:i + 1]),
                     act(Eb[:, i % 2, 256:384], o[:, 256:384], ACT.Exp, bias=At[:, 1, i:i + 1])]
                give(b, a[-1])
                return a

            def ssd_out(i, a):
                e, m, g = Eb[:, i % 2, :], Mb[:, i % 2, :], i // 4
                k = [stt(m[:, 0:256], e[:, 0:256], At[:, 0, 32 + i:33 + i], cbs[:, g, 0:256], ALU.mult, ALU.mult, a, t_cb, t_at,
                         m_gone.get(i - 2)),
                     stt(m[:, 256:384], e[:, 256:384], At[:, 1, 32 + i:33 + i], cbs[:, g, 256:384], ALU.mult, ALU.mult, a)]
                c = slice(64 * i, 64 * i + 64)
                m_gone[i] = [k]
                return [c, m, k]

            def ssd_mm(i, c, m, k):
                mm(ps[by[0][0]][:, c], m[:, 0:128], xs[:, 0, c], True, True, k, t_xs, fry)
                mm(ps[by[1][0]][:, c], m[:, 128:256], xs[:, 0, c], True, False)
                d = mm(ps[by[1][0]][:, c], m[:, 256:384], xs[:, 1, c], False, True, inc=True)
                m_gone[i] += [d]
                return d

            out = {}
            for i in range(10):
                if 2 <= i:
                    d = ssd_mm(i - 2, *out.pop(i - 2))
                if 1 <= i <= 8:
                    out[i - 1] = ssd_out(i - 1, seg.pop(i - 1))
                if i < 8:
                    seg[i] = ssd_seg(i)
                yield
            heads_done.append(d)
            r = {}
            for tb in range(2):
                yt = xs[:, tb, :]
                a = tt(yt.rearrange("p (a b) -> p a b", a=8), yt.rearrange("p (a b) -> p a b", a=8),
                       srow[:, 0:8].unsqueeze(2).to_broadcast([128, 8, 64]), ALU.mult, t_xs, t_sr, d)
                a = tt(yt, yt, ps[by[tb][0]][:, :], ALU.add, a, d)
                give(by[tb][0], a)
                a = tt(yt, yt, sz[:, tb, :], ALU.mult, a, silus())
                q = [square(yt[:, 256 * g:256 * g + 256], st[:, 2 * tb + g:2 * tb + g + 1], 1.0, a, x_last) for g in range(2)]
                r[tb] = rstd(st[:, 4 + 2 * tb:6 + 2 * tb], st[:, 2 * tb:2 * tb + 2], 256, q)
            yield
            for tb in range(2):
                yt = xs[:, tb, :]
                r[tb] = tt(yt.rearrange("p (a b) -> p a b", a=2), yt.rearrange("p (a b) -> p a b", a=2),
                           st[:, 4 + 2 * tb:6 + 2 * tb].unsqueeze(2).to_broadcast([128, 2, 256]), ALU.mult, r[tb])
            yield
            for tb in range(2):
                t = to_xf(xs[:, tb, :], 4, 0, tb, P("s_norm", 0, 4), r[tb], heads_done)
                t_hl[tb, 0] = hilo(0, 4, tb, t, x_last)

        t_hl = {}
        score(hk, hq, [t_hq, t_hf], 7)
        lev = pipeline([level(n, m) for n, m in enumerate([128] + LEVELS)], oldest_first=True)
        prod, sd, end = products(), ssd(), hgrn_end()
        for who in SCHEDULE:
            next({"L": lev, "P": prod, "S": sd, "E": end}[who], 0)
        assert not any(next(g, 1) is None for g in (lev, prod, end))

        stp = Step(add_banks, P("nf1", 0, 8))
        so = Split(S["sout"], stp)
        so.x = {(i, tb): t_hl[tb, i // 2 * 2] for i in (2, 3) for tb in range(2)}
        for i in (2, 3):
            for tb in range(2):
                so.part(i, tb)
            next(sd, 0)
        so.x.update({(i, tb): t_hl[tb, 0] for i in (0, 1) for tb in range(2)})
        so.finish()

        t_out = []

        class Last:
            def late(self, tb):
                pass

            def early(self, tb, bk, d):
                toks = add_banks(tb, bk, d)
                r = rms_of([(h[:, tb, c], t) for c, t in zip(HALF, toks)], 3 * tb)
                for i, c in enumerate(HALF):
                    m = stt(hs[:, tb, c], h[:, tb, c], st[:, 3 * tb + 2:3 * tb + 3], rows[:, 1, c], ALU.mult, ALU.mult,
                            r, t_r1, toks)
                    t_out.append(dma(f"out{tb}{i}", out[128 * tb:128 * tb + 128, c], hs[:, tb, c], m))

        ffn(S["f1"], True, stp, Last())
        assert len(used) == len(slots), (len(used), len(slots))

        block = ctx.enter_context(nc.Block())

        @block.sync
        def _(eng):
            SP.replay(eng)
            for s, c in t_out:
                eng.wait_ge(s, c)

        @block.tensor
        def _(eng):
            PE.replay(eng)

        @block.scalar
        def _(eng):
            AC.replay(eng)

        @block.vector
        def _(eng):
            VE.replay(eng)

        @block.gpsimd
        def _(eng):
            GP.replay(eng)


def constants():
    f = np.float32
    i = np.arange(128)
    c = np.zeros((128, C_N), f)
    c[:, C_ID:C_ID + 128] = np.eye(128, dtype=f)
    c[:, C_MA:C_MA + 128] = np.where(i[None, :] > i[:, None], f(NEG), f(0))
    c[:, C_MT:C_MT + 128] = np.where(i[None, :] < i[:, None], f(NEG), f(0))
    c[:, C_ONE:C_ONE + 128] = f(1.0 / 256)
    for n in range(8):
        c[n, C_SEL + 128 * n:C_SEL + 128 * n + 128] = 1
    pos = np.arange(256, dtype=f)
    for dim, at in ((32, 0), (64, 32)):
        inv = (f(1) / np.power(f(10000.0), np.arange(0, dim, 2, dtype=f) / f(dim))).astype(f)
        ang = (pos[:, None] * inv[None, :]).astype(f)
        for tb in range(2):
            a = ang[128 * tb:128 * tb + 128]
            o = C_ROPE + 96 * tb + at
            c[:, o:o + dim // 2] = np.cos(a)
            c[:, o + dim // 2:o + dim] = np.sin(a)
    t = np.arange(256)
    band = np.zeros((256, 4, 256), f)
    for g, w in enumerate((2, 4, 8, 16)):
        inside = (t[:, None] <= t[None, :]) & (t[:, None] > t[None, :] - w)
        band[:, g, :] = np.where(inside, f(1) / np.minimum(t + 1, w).astype(f)[None, :], f(0)) - np.eye(256, dtype=f)
    band = np.ascontiguousarray(band.reshape(2, 128, 4, 256).transpose(1, 2, 0, 3))
    hm = np.zeros((128, 8, 128), f)
    for n, m in enumerate(LEVELS):
        same = i[:, None] // (2 * m) == i[None, :] // (2 * m)
        hm[:, n, :] = same & ((i[:, None] // m) % 2 == 0) & ((i[None, :] // m) % 2 == 1)
    hm[:, 7, :] = np.eye(128)
    return c, band, hm


def kernel(**inputs):
    import concourse.bacc as bacc
    from concourse.bass_utils import run_bass_kernel_spmd as run

    a = {k: np.asarray(v) for k, v in inputs.items()}
    prm = np.zeros((128, P_N), np.float32)

    def put(name, v, j=0):
        v = np.asarray(v)
        prm[0:v.shape[0], P_AT[name] + j:P_AT[name] + j + v.shape[1]] = v

    def tiles(v):
        return v.reshape(-1, 128).T

    for name, src in (("g_mix_pre", a["g_mix_pre"][0]), ("g_mlp_pre", a["g_mlp_pre"][0]), ("g_ple_pre", a["g_ple_pre"][0]),
                      ("nm0", a["norm_mix_2"][0]), ("nm1", a["norm_mix_2"][1]), ("nf0", a["norm_ffn_2"][0]),
                      ("nf1", a["norm_ffn_2"][1]), ("ln_g", a["conf_ln_g"][0]), ("ln_b", a["conf_ln_b"][0]),
                      ("pool_scale", a["pool_scale"][0]), ("cb", a["s_conv_b_2"][0]), ("qn", a["a_q_norm_2"][0]),
                      ("kvn", a["a_kv_norm_2"][0]), ("subln", a["a_subln_2"][0]), ("s_norm", a["s_norm_2"][0]),
                      ("g_norm", a["h_g_norm_2"][0]), ("lb0", a["h_lower_bound_2"][0]), ("lb1", a["h_lower_bound_2"][1])):
        put(name, tiles(src))
    for name, src in (("dw", a["w_conf_dw"][0]), ("sc", a["w_sc"][0]), ("cw", a["s_conv_w_2"][0])):
        k, n = src.shape
        put(name, src.reshape(k, n // 128, 128).transpose(2, 1, 0).reshape(128, -1))
    prm[0:4, P_AT["bf"]] = a["b_forget"][0]
    prm[32:36, P_AT["bf"]] = a["b_forget"][0]
    prm[0:8, P_AT["dtb"]] = a["s_dt_bias_2"][0]
    prm[0:8, P_AT["alog"]] = a["s_a_log_2"][0]
    for i in range(4):
        prm[i, P_AT["fsel"] + i] = prm[32 + i, P_AT["fsel"] + i] = 1
    prm[:, P_AT["eps"]] = EPS
    prm[:, P_AT["mhalf"]:P_AT["mhalf"] + 4] = -0.5
    srow = np.concatenate([a["s_d_2"][0], a["a_lq1_2"][0], a["a_lk1_2"][0], a["a_lq2_2"][0], a["a_lk2_2"][0]])
    cst, band, hm = constants()
    arrays = {"x": a["x"][0], "pT": np.ascontiguousarray(a["p"][0, 0].T), "prm": prm, "srow": srow, "cst": cst,
              "band": band, "hmask": hm, "w_pool": a["w_pool"][0], "norm_final_2": a["norm_final_2"]}
    for n in ("w_in", "w_conf_pw", "w_out", "w_up", "w_down", "w_ple_gate", "w_ple_proj", "g_mix_post", "g_mlp_post",
              "g_ple_post", "a_w_in_2", "a_w_uq_2", "a_w_ukv_2", "a_w_out_2", "s_w_in_2", "s_w_out_2"):
        arrays[n] = a[n][0]
    for n in ("ffn_gate", "ffn_up", "ffn_down"):
        for l in range(2):
            arrays[f"{n}_{l}"] = a[n + "_2"][l]
    nc = bacc.Bacc("TRN2", target_bir_lowering=False, num_devices=1)
    D, feed = {}, {}
    for n, v in arrays.items():
        v = np.ascontiguousarray(v)
        D[n] = nc.dram_tensor("in_" + n, v.shape, F32, kind="ExternalInput").ap()
        feed["in_" + n] = v
    out = nc.dram_tensor("out_0", (256, 1024), F32, kind="ExternalOutput").ap()
    program(nc, D, out)
    r = run(nc, [feed], core_ids=[0])
    return r.results[0]["out_0"].reshape(1, 256, 1024)
```
